# Optimizing a Trainium2 kernel written in Bass

```python
import jax, jax.numpy as jnp
from jax import lax
import numpy as np

D_MODEL = 1024
BATCH = 1
SEQ = 256
DEPTH = 1
DEC_BATCH = 1
DEC_SEQ = 64
PAST_LEN = 512

CHUNK = 64
D_MIX = D_MODEL
GLA_HEADS = 4
GLA_WIDTH = D_MIX // 2
GLA_DV = GLA_WIDTH // GLA_HEADS
GLA_DK = GLA_DV // 2
GLA_KW = GLA_HEADS * GLA_DK
GATE_RANK = 16
GATE_TAU = 16.0
POOL_WIDTH = D_MIX - GLA_WIDTH
POOL_GROUPS = 4
POOL_GC = POOL_WIDTH // POOL_GROUPS
POOL_WINDOWS = (2, 4, 8, 16)
POOL_BUF = max(POOL_WINDOWS) - 1
SPLITS = (GLA_KW, 2 * GLA_KW, 2 * GLA_KW + GLA_WIDTH, 2 * GLA_KW + 2 * GLA_WIDTH,
          2 * GLA_KW + 2 * GLA_WIDTH + GATE_RANK)
D_IN = 2 * GLA_KW + 2 * GLA_WIDTH + GATE_RANK + POOL_WIDTH
N_MEM = 256
MEM_HEADS = 4
MEM_HD = D_MODEL // MEM_HEADS
N_EXPERTS = 32
TOP_K = 4
D_FF = D_MODEL
SWIGLU_ALPHA = 1.702
SWIGLU_LIMIT = 7.0
MOE_BLOCK = 128
EPS = 1e-6

kernel_name = "hymba_gla_pool_memxattn_moe_stream_step"

def rmsnorm(x, g):
    xf = x.astype(jnp.float32)
    y = xf * lax.rsqrt(jnp.mean(xf * xf, axis=-1, keepdims=True) + EPS)
    return (y * g.astype(jnp.float32)).astype(x.dtype)

def gla_chunked(q, k, v, log_a, s0):
    B, L, H, DK = q.shape
    DV = v.shape[-1]
    C = min(CHUNK, L)
    N = L // C
    f32 = jnp.float32
    q = q.astype(f32).reshape(B, N, C, H, DK)
    k = k.astype(f32).reshape(B, N, C, H, DK)
    v = v.astype(f32).reshape(B, N, C, H, DV)
    b = jnp.cumsum(log_a.astype(f32).reshape(B, N, C, H, DK), axis=2)
    b_last = b[:, :, -1]
    qd = q * jnp.exp(b)
    kd = k * jnp.exp(-b)
    kl = k * jnp.exp(b_last[:, :, None] - b)
    mask = jnp.tril(jnp.ones((C, C), dtype=bool))
    a = jnp.einsum('bnihd,bnjhd->bnhij', qd, kd)
    a = jnp.where(mask, a, 0.0)
    o_intra = jnp.einsum('bnhij,bnjhe->bnihe', a, v)
    ds = jnp.einsum('bnchd,bnche->nbhde', kl, v)
    dec = jnp.exp(b_last).transpose(1, 0, 2, 3)

    def step(s, inp):
        d, dsn = inp
        return d[..., None] * s + dsn, s

    s_fin, s_in = lax.scan(step, s0.astype(f32), (dec, ds))
    o_inter = jnp.einsum('bnchd,nbhde->bnche', qd, s_in)
    o = (o_intra + o_inter).reshape(B, L, H, DV)
    return o, s_fin

def pool_mix(u, prev, hist_len, pool_w, pool_scale):
    B, L, _ = u.shape
    f32 = jnp.float32
    full = jnp.concatenate([prev.astype(u.dtype), u], axis=1)
    valid = jnp.concatenate([(jnp.arange(POOL_BUF) >= POOL_BUF - hist_len).astype(f32),
                             jnp.ones((L,), f32)])
    fullf = full.astype(f32) * valid[None, :, None]
    cs = jnp.concatenate([jnp.zeros((B, 1, POOL_WIDTH), f32), jnp.cumsum(fullf, axis=1)], axis=1)
    cv = jnp.concatenate([jnp.zeros((1,), f32), jnp.cumsum(valid)])
    uf = u.astype(f32)
    e = POOL_BUF + 1
    diffs = []
    for g, w in enumerate(POOL_WINDOWS):
        sl = slice(g * POOL_GC, (g + 1) * POOL_GC)
        s = cs[:, e:e + L, sl] - cs[:, e - w:e - w + L, sl]
        n = cv[e:e + L] - cv[e - w:e - w + L]
        diffs.append(s / n[None, :, None] - uf[..., sl])
    d = jnp.stack(diffs, axis=2)
    y = jnp.einsum('blgc,gcd->blgd', d, pool_w.astype(f32)).reshape(B, L, POOL_WIDTH)
    y = y * pool_scale.astype(f32)
    return y.astype(u.dtype), full[:, -POOL_BUF:]

def token_mix(h, s_gla, pool_prev, hist_len, w_in, w_gate, b_gate, gla_gain, pool_w, pool_scale, w_out):
    B, L, _ = h.shape
    z = h @ w_in
    q, k, v, g, r, u = jnp.split(z, SPLITS, axis=-1)
    q = q.reshape(B, L, GLA_HEADS, GLA_DK) * (GLA_DK ** -0.5)
    k = k.reshape(B, L, GLA_HEADS, GLA_DK)
    v = v.reshape(B, L, GLA_HEADS, GLA_DV)
    log_a = jax.nn.log_sigmoid((r @ w_gate + b_gate).astype(jnp.float32)) / GATE_TAU
    log_a = log_a.reshape(B, L, GLA_HEADS, GLA_DK)
    o, s_new = gla_chunked(q, k, v, log_a, s_gla)
    o = rmsnorm(o, gla_gain.reshape(GLA_HEADS, GLA_DV))
    o = o.reshape(B, L, GLA_WIDTH).astype(h.dtype) * jax.nn.silu(g)
    p, pool_new = pool_mix(u, pool_prev, hist_len, pool_w, pool_scale)
    y = jnp.concatenate([o, p], axis=-1) @ w_out
    return y, s_new.astype(h.dtype), pool_new

def mem_kv(mem, norm_mem_kv, w_mk, w_mv):
    B = mem.shape[0]
    m = rmsnorm(mem, norm_mem_kv)
    k = (m @ w_mk).reshape(B, N_MEM, MEM_HEADS, MEM_HD)
    v = (m @ w_mv).reshape(B, N_MEM, MEM_HEADS, MEM_HD)
    return k, v

def cross_attn(h, k, v, w_mq, w_mo):
    B, L, D = h.shape
    q = (h @ w_mq).reshape(B, L, MEM_HEADS, MEM_HD)
    s = jnp.einsum('blhd,bmhd->bhlm', q, k).astype(jnp.float32) * (MEM_HD ** -0.5)
    p = jax.nn.softmax(s, axis=-1).astype(v.dtype)
    o = jnp.einsum('bhlm,bmhd->blhd', p, v).reshape(B, L, D)
    return o @ w_mo

def moe(h, w_router, b_router, w_up, b_up, w_down, b_down):
    B, L, D = h.shape
    t = h.reshape(-1, D)
    T = t.shape[0]
    logits = (t @ w_router + b_router).astype(jnp.float32)
    top_v, top_i = lax.top_k(logits, TOP_K)
    gates = jax.nn.softmax(top_v, axis=-1)
    S = T * TOP_K
    e = top_i.reshape(-1).astype(jnp.int32)
    tok = jnp.repeat(jnp.arange(T, dtype=jnp.int32), TOP_K)
    wts = gates.reshape(-1)
    order = jnp.argsort(e)
    se, stok, sw = e[order], tok[order], wts[order]
    counts = jnp.bincount(e, length=N_EXPERTS)
    padded = ((counts + MOE_BLOCK - 1) // MOE_BLOCK) * MOE_BLOCK
    start = jnp.cumsum(counts) - counts
    pend = jnp.cumsum(padded)
    pstart = pend - padded
    dest = pstart[se] + jnp.arange(S, dtype=jnp.int32) - start[se]
    nb = (S + N_EXPERTS * (MOE_BLOCK - 1) + MOE_BLOCK - 1) // MOE_BLOCK
    P = nb * MOE_BLOCK
    tok_buf = jnp.zeros((P,), jnp.int32).at[dest].set(stok)
    w_buf = jnp.zeros((P,), jnp.float32).at[dest].set(sw)
    block_e = jnp.minimum(jnp.searchsorted(pend, jnp.arange(nb) * MOE_BLOCK, side='right'),
                          N_EXPERTS - 1).astype(jnp.int32)

    def expert_block(args):
        eid, tk, wt = args
        xb = t[tk]
        uu = xb @ w_up[eid] + b_up[eid]
        glu = jnp.minimum(uu[:, :D_FF], SWIGLU_LIMIT)
        lin = jnp.clip(uu[:, D_FF:], -SWIGLU_LIMIT, SWIGLU_LIMIT)
        act = glu * jax.nn.sigmoid(SWIGLU_ALPHA * glu) * (lin + 1.0)
        yb = act @ w_down[eid] + b_down[eid]
        return yb * wt[:, None].astype(yb.dtype)

    ys = lax.map(expert_block, (block_e, tok_buf.reshape(nb, MOE_BLOCK), w_buf.reshape(nb, MOE_BLOCK)))
    out = jnp.zeros((T, D), ys.dtype).at[tok_buf].add(ys.reshape(P, D))
    return out.reshape(B, L, D).astype(h.dtype)

def block(x, s_gla, pool_prev, hist_len, mk, mv,
          norm_mix, w_in, w_gate, b_gate, gla_gain, pool_w, pool_scale, w_out,
          norm_mem_q, w_mq, w_mo, norm_moe, w_router, b_router, w_up, b_up, w_down, b_down):
    y, s_new, pool_new = token_mix(rmsnorm(x, norm_mix), s_gla, pool_prev, hist_len,
                                   w_in, w_gate, b_gate, gla_gain, pool_w, pool_scale, w_out)
    x = x + y
    x = x + cross_attn(rmsnorm(x, norm_mem_q), mk, mv, w_mq, w_mo)
    x = x + moe(rmsnorm(x, norm_moe), w_router, b_router, w_up, b_up, w_down, b_down)
    return x, s_new, pool_new

def setup_inputs(seed: int = 0) -> dict:
    key = jax.random.key(seed)
    ks = iter(jax.random.split(key, 40))
    f32 = jnp.float32

    def nrm(shape, s):
        return jax.random.normal(next(ks), shape, f32) * s

    def gain(n):
        return 1.0 + 0.05 * jax.random.normal(next(ks), (DEPTH, n), f32)

    return {
        "x_prompt": nrm((BATCH, SEQ, D_MODEL), 1.0),
        "x_sample": nrm((DEC_BATCH, DEC_SEQ, D_MODEL), 1.0),
        "mem_prompt": nrm((BATCH, N_MEM, D_MODEL), 1.0),
        "state_gla": nrm((DEPTH, DEC_BATCH, GLA_HEADS, GLA_DK, GLA_DV), 0.5),
        "state_pool": nrm((DEPTH, DEC_BATCH, POOL_BUF, POOL_WIDTH), 1.0),
        "cache_mem_k": nrm((DEPTH, DEC_BATCH, N_MEM, MEM_HEADS, MEM_HD), 1.0),
        "cache_mem_v": nrm((DEPTH, DEC_BATCH, N_MEM, MEM_HEADS, MEM_HD), 1.0),
        "norm_mix": gain(D_MODEL),
        "w_in": nrm((DEPTH, D_MODEL, D_IN), D_MODEL ** -0.5),
        "w_gate": nrm((DEPTH, GATE_RANK, GLA_KW), GATE_RANK ** -0.5),
        "b_gate": nrm((DEPTH, GLA_KW), 0.1),
        "gla_gain": gain(GLA_WIDTH),
        "pool_w": nrm((DEPTH, POOL_GROUPS, POOL_GC, POOL_GC), POOL_GC ** -0.5),
        "pool_scale": gain(POOL_WIDTH),
        "w_out": nrm((DEPTH, D_MIX, D_MODEL), D_MIX ** -0.5),
        "norm_mem_q": gain(D_MODEL),
        "norm_mem_kv": gain(D_MODEL),
        "w_mq": nrm((DEPTH, D_MODEL, D_MODEL), D_MODEL ** -0.5),
        "w_mk": nrm((DEPTH, D_MODEL, D_MODEL), D_MODEL ** -0.5),
        "w_mv": nrm((DEPTH, D_MODEL, D_MODEL), D_MODEL ** -0.5),
        "w_mo": nrm((DEPTH, D_MODEL, D_MODEL), D_MODEL ** -0.5),
        "norm_moe": gain(D_MODEL),
        "w_router": nrm((DEPTH, D_MODEL, N_EXPERTS), D_MODEL ** -0.5),
        "b_router": nrm((DEPTH, N_EXPERTS), 0.01),
        "w_up": nrm((DEPTH, N_EXPERTS, D_MODEL, 2 * D_FF), D_MODEL ** -0.5),
        "b_up": nrm((DEPTH, N_EXPERTS, 2 * D_FF), 0.01),
        "w_down": nrm((DEPTH, N_EXPERTS, D_FF, D_MODEL), D_FF ** -0.5),
        "b_down": nrm((DEPTH, N_EXPERTS, D_MODEL), 0.01),
        "norm_final": gain(D_MODEL)[0],
    }

def reference(x_prompt, x_sample, mem_prompt, state_gla, state_pool, cache_mem_k, cache_mem_v,
              norm_mix, w_in, w_gate, b_gate, gla_gain, pool_w, pool_scale, w_out,
              norm_mem_q, norm_mem_kv, w_mq, w_mk, w_mv, w_mo,
              norm_moe, w_router, b_router, w_up, b_up, w_down, b_down, norm_final):
    xp, xs = x_prompt, x_sample
    Bp = xp.shape[0]
    gla_p, pool_p, mk_p, mv_p, gla_s, pool_s = [], [], [], [], [], []
    for l in range(DEPTH):
        lw = (norm_mix[l], w_in[l], w_gate[l], b_gate[l], gla_gain[l], pool_w[l], pool_scale[l], w_out[l],
              norm_mem_q[l], w_mq[l], w_mo[l], norm_moe[l], w_router[l], b_router[l],
              w_up[l], b_up[l], w_down[l], b_down[l])
        mk, mv = mem_kv(mem_prompt, norm_mem_kv[l], w_mk[l], w_mv[l])
        s0 = jnp.zeros((Bp, GLA_HEADS, GLA_DK, GLA_DV), xp.dtype)
        p0 = jnp.zeros((Bp, POOL_BUF, POOL_WIDTH), xp.dtype)
        xp, sp, pp = block(xp, s0, p0, 0, mk, mv, *lw)
        gla_p.append(sp)
        pool_p.append(pp)
        mk_p.append(mk)
        mv_p.append(mv)
        xs, ss, ps = block(xs, state_gla[l], state_pool[l], PAST_LEN, cache_mem_k[l], cache_mem_v[l], *lw)
        gla_s.append(ss)
        pool_s.append(ps)
    y_prompt = rmsnorm(xp, norm_final)
    y_sample = rmsnorm(xs, norm_final)
    return (y_prompt, y_sample, jnp.stack(gla_p), jnp.stack(pool_p), jnp.stack(mk_p), jnp.stack(mv_p),
            jnp.stack(gla_s), jnp.stack(pool_s))


_drawn_inputs = setup_inputs


def setup_inputs(seed=0):
    import zlib

    import numpy as np

    out = dict(_drawn_inputs(seed))
    spreads = {}
    factors = {'norm_mem_q': 2.783, 'b_up': 8.0, 'b_down': 8.0}
    for name, (base, spread) in spreads.items():
        noise = np.random.default_rng([zlib.crc32(name.encode()), seed]).standard_normal(out[name].shape)
        drawn = base * np.exp(spread * noise) if base else spread * noise
        out[name] = __import__('jax').numpy.asarray(drawn.astype(out[name].dtype))
    for name, factor in factors.items():
        out[name] = (out[name] * factor).astype(out[name].dtype)
    return out
```

```python
from contextlib import ExitStack, contextmanager

import concourse.bass as bass
from concourse import mybir

F32 = mybir.dt.float32
I32 = mybir.dt.int32
ALU = mybir.AluOpType
ACT = mybir.ActivationFunctionType
AX = mybir.AxisListType

P = 128
D = 1024
KT = D // P
LP, LS = 256, 64
NT = LP + LS
TILES = [(0, 128), (128, 128), (256, 64)]
HEADS, DK, DV = 4, 64, 128
KW, GW = HEADS * DK, HEADS * DV
RANK = 16
CHUNK = 64
NCH = NT // CHUNK
POOL = 512
BUF = 15
UP_P, UP_S = BUF + LP, BUF + LS
UPAD = UP_P + UP_S
NMEM, AH, AHD = 256, 4, 256
E = 32
DFF = 1024
SLOTS = 64
NBLK = NT // SLOTS
EPS = 1e-6
COL = dict(q=0, k=KW, v=2 * KW, g=2 * KW + GW, r=2 * KW + 2 * GW, u=2 * KW + 2 * GW + RANK)


class Jobs:

    def __init__(self, table):
        self.job, self.order, count = {}, [], {"A": 0, "D": 0}
        for n, (name, last) in enumerate(table):
            count[last] += 1
            self.job[name] = (n, last, count[last])
            self.order.append((last, count[last]))

    def bank(self, name):
        return self.job[name][0] % 8

    def filled_at(self, name):
        return self.job[name][0] + 1

    def freed_at(self, name):
        return self.job[name][1:]

    def occupant_before(self, name):
        n = self.job[name][0]
        return self.order[n - 8] if n >= 8 else None


def job_table():
    t = [("vec", "D"), ("bup", "D")]
    t += [(f"memT{i}", "A") for i in range(4)]
    t += [(f"K{i}", "A") for i in range(4)]
    t += [(f"xT{i}", "D") for i in range(KT)]
    t += [("rms0", "D")]
    t += [(f"V{i}", "A") for i in range(4)]
    t += [(f"KTp{i}", "A") for i in range(4)]
    t += [("r", "D"), ("q0", "D"), ("q1", "D"), ("gate0", "A"), ("gate1", "A"), ("k0", "D"), ("k1", "D")]
    t += [(f"v{i}", "A") for i in range(3)]
    t += [("cum0", "D"), ("cum1", "D"), ("prevT", "A")]
    t += [(f"u{i}", "D") for i in range(4)]
    t += [("klT0", "A"), ("klT1", "A")]
    t += [(f"AT{i}", "D") for i in range(3)]
    t += [(f"g{i}", "D") for i in range(4)]
    t += [(f"ds{c}", "D") for c in range(NCH)]
    t += [(f"KTs{i}", "A") for i in range(4)]
    t += [(f"pool{i}", "D") for i in range(4)]
    t += [(f"o{i}", "D") for i in range(3)]
    t += [("hist0", "A"), ("hist1", "A")]
    t += [(f"oT{i}", "D") for i in range(4)]
    t += [(f"out{i}", "D") for i in range(KT)]
    t += [("rms1", "D")] + [(f"mq{i}", "D") for i in range(KT)]
    t += [(f"s{i}", "A") for i in range(6)]
    t += [(f"PT{i}", "D") for i in range(5)]
    t += [(f"PV{i}", "A") for i in range(5)]
    t += [(f"mo{i}", "D") for i in range(KT)]
    t += [("router", "D")]
    t += [(f"x2_{i}", "A") for i in range(6)]
    t += [("rank", "D"), ("GT", "A")]
    return t


def build(nc, a, o):
    J = Jobs(job_table())
    with ExitStack() as ctx:
        sems = {}

        def S(name):
            if name not in sems:
                sems[name] = ctx.enter_context(nc.semaphore(name))
            return sems[name]

        ps = ctx.enter_context(nc.psum_tensor("ps", [P, 8, 512], F32))
        nwords = 40960 + 12248
        arena = ctx.enter_context(nc.sbuf_tensor("arena", [P, nwords], F32))

        def reg(at, n):
            assert at + n <= nwords
            return arena[:, at:at + n]

        RA, RB0, RB1, RD, RP = 0, 16384, 24576, 32768, 40960
        upA = reg(RA, 16384).rearrange("p (k f) -> p k f", k=KT)
        upB = reg(RB0, 16384).rearrange("p (k f) -> p k f", k=KT)
        wdn = reg(RD, 8192).rearrange("p (k f) -> p k f", k=KT)
        c = RP
        def take(n):
            nonlocal c
            r = reg(c, n); c += n
            return r
        ident, iota = take(128), take(128)
        OH_at = c
        tri, ones, below = take(128), take(128), take(128)
        bupT = take(E * 16).rearrange("p (e f) -> p e f", e=E)
        GT_at = c
        wr = take(KT * E).rearrange("p (k e) -> p k e", k=KT)
        gwr = take(KT * E).rearrange("p (k e) -> p k e", k=KT)
        vec = take(40)
        small = take(152)
        brout = take(E)
        g_mix, g_memq, g_memkv, g_moe = (vec[:, 8 * i:8 * i + 8] for i in range(4))
        g_gla, pscale = vec[:, 32:36], vec[:, 36:40]
        XT_at = c; xT = take(2560).rearrange("p (k t) -> p k t", k=KT)
        GX_at = c; gxT = take(2560).rearrange("p (k t) -> p k t", k=KT)
        CAT_at = c; catT = take(2560).rearrange("p (k t) -> p k t", k=KT)
        SP_at = c
        upad = take(4 * UPAD).rearrange("p (g t) -> p g t", g=4)
        rstdb = take(NT)
        rT = take(NT)
        wgate = take(KW)
        wr_col = take(KT * RANK).rearrange("p (k c) -> p k c", k=KT)
        end_at = c
        assert c <= nwords
        ssx, ssm = small[:, 0:3], small[:, 3:5]
        rsx, rsm = small[:, 5:8], small[:, 8:10]
        sso = small[:, 10:22].rearrange("p (i h) -> p i h", i=3)
        rso = small[:, 22:34].rearrange("p (i h) -> p i h", i=3)
        mx = small[:, 34:46]
        nmx = small[:, 46:58]
        rs = small[:, 58:70]
        rinv = small[:, 70:82]
        ss2, rs2 = small[:, 82:88], small[:, 88:91]
        top8 = small[:, 91:115].rearrange("p (i k) -> p i k", i=3)
        nt1 = small[:, 115:118]
        gsum = small[:, 118:121]
        nover = small[:, 121:122]
        over_i = small[:, 122:123].bitcast(I32)
        all_in = small[:, 129:130]
        sst = small[:, 123:129]
        xtok = reg(RB1, 3072).rearrange("p (i d) -> p i d", i=3)
        mem = reg(RB1 + 3072, 2048).rearrange("p (i d) -> p i d", i=2)
        memT = reg(RB1 + 5120, 2048).rearrange("p (k m) -> p k m", k=KT)
        Vp = reg(RB1, 2048).rearrange("p (i d) -> p i d", i=2)
        Kp = reg(CAT_at, 2048).rearrange("p (i d) -> p i d", i=2)
        KTp = reg(RB1 + 3072, 2048).rearrange("p (k m) -> p k m", k=KT)
        Vs = reg(RB1 + 5120, 2048).rearrange("p (i d) -> p i d", i=2)
        Sbuf = [reg(RB1 + 2048 + 256 * i, 256) for i in range(4)] + [reg(RB1 + 7168 + 256 * i, 256) for i in range(3)]
        Sbuf = [s.rearrange("p (r e) -> p r e", r=2) for s in Sbuf]
        wmk = reg(RB0, 8192).rearrange("p (k f) -> p k f", k=KT)
        wmv = reg(RD, 8192).rearrange("p (k f) -> p k f", k=KT)
        Ks = reg(RB0, 2048).rearrange("p (i d) -> p i d", i=2)
        KTs = reg(RB0 + 2048, 2048).rearrange("p (k m) -> p k m", k=KT)
        sgT = reg(RB0 + 4096, 1280).rearrange("p (g t) -> p g t", g=4)
        vtok = reg(RB0 + 5376, 1536).rearrange("p (i d) -> p i d", i=3)
        qT = reg(RB0 + 6912, 640).rearrange("p (r t) -> p r t", r=2)
        kT = reg(RB0 + 7552, 640).rearrange("p (r t) -> p r t", r=2)
        w_qk = reg(RA, 4096).rearrange("p (k f) -> p k f", k=KT)
        w_v = reg(RA + 4096, 4096).rearrange("p (k f) -> p k f", k=KT)
        w_g = reg(RA + 8192, 4096).rearrange("p (k f) -> p k f", k=KT)
        w_u = reg(RA + 12288, 4096).rearrange("p (k f) -> p k f", k=KT)
        la0 = reg(CAT_at, 768).rearrange("p (i f) -> p i f", i=3)
        la1 = reg(CAT_at + 768, 768).rearrange("p (i f) -> p i f", i=3)
        at = RA
        def takeA(n):
            nonlocal at
            r = reg(at, n); at += n
            return r
        bT = takeA(640).rearrange("p (r t) -> p r t", r=2)
        eb = takeA(640).rearrange("p (r t) -> p r t", r=2)
        enb = takeA(640).rearrange("p (r t) -> p r t", r=2)
        ebl = takeA(640).rearrange("p (r t) -> p r t", r=2)
        kdT = takeA(640).rearrange("p (r t) -> p r t", r=2)
        qdz = takeA(1280).rearrange("p (h t) -> p h t", h=4)
        klz = takeA(1280).rearrange("p (c f) -> p c f", c=5)
        AT = takeA(1536).rearrange("p (i h t) -> p i h t", i=3, h=4)
        assert at <= 8192
        otok = reg(RA + 8192, 1536).rearrange("p (i d) -> p i d", i=3)
        osq = reg(RA + 9728, 1536).rearrange("p (i d) -> p i d", i=3)
        hist = reg(RA + 11264, 1024).rearrange("p (i d) -> p i d", i=2)
        s_a = reg(RA + 12288, 4 * UPAD).rearrange("p (g t) -> p g t", g=4)
        s_b = reg(RA + 12288 + 4 * UPAD, 4 * UPAD).rearrange("p (g t) -> p g t", g=4)
        invn = reg(RA + 12288 + 8 * UPAD, 4 * NT).rearrange("p (g t) -> p g t", g=4)
        poolw = reg(GX_at, 512).rearrange("p (g f) -> p g f", g=4)
        smallrows = reg(RB1 + 7168, 128)
        buprow = reg(GX_at, 2048)
        prevrow = reg(RB1 + 7168 + 256, 512)
        rT_diag = reg(CAT_at + 2048, 384).rearrange("p (i t) -> p i t", i=3)
        sgT_f = reg(RB0 + 4096, 1280)
        sgT_e = reg(RA + 9728, 1280)
        sq1 = reg(RB0 + 4096, 2560).rearrange("p (k t) -> p k t", k=KT)
        aqT = reg(RB0 + 4096, 2560).rearrange("p (k t) -> p k t", k=KT)
        probs_p = reg(RB0, 2048).rearrange("p (l h m) -> p l h m", l=2, h=4)
        probs_s = reg(RB0 + 6656, 1024).rearrange("p (h m) -> p h m", h=4)
        PTs = reg(RB0 + 7680, 512).rearrange("p (h i l) -> p h i l", h=4, i=2)
        PTp = reg(GX_at, 2048).rearrange("p (h i l) -> p h i l", h=4, i=2)
        aoT = catT
        wsq = reg(RD, 8192).rearrange("p (c k f) -> p c k f", c=4, k=KT)
        Hm = reg(GX_at, 3072).rearrange("p (i d) -> p i d", i=3)
        acc = reg(GX_at + 3072, 3072).rearrange("p (i d) -> p i d", i=3)
        x_at = GX_at + 6144
        glu = reg(x_at, 512).rearrange("p (k s) -> p k s", k=KT)
        sg = reg(x_at + 512, 512).rearrange("p (k s) -> p k s", k=KT)
        Y = reg(x_at + 1024, 512)
        U = reg(XT_at, 1024)
        lin = reg(XT_at + 1024, 512).rearrange("p (k s) -> p k s", k=KT)
        XG = reg(XT_at + 1536, 512)
        XTe = reg(XT_at + 2048, 512).rearrange("p (q h s) -> p q h s", q=4, h=2)
        OH = reg(OH_at, 384).rearrange("p (i s) -> p i s", i=3)
        GT = reg(GT_at, NT)
        rankx = reg(GT_at + NT, 96).rearrange("p (i e) -> p i e", i=3)
        Gm = reg(GT_at + NT + 96, 96).rearrange("p (i e) -> p i e", i=3)
        gate_col = small[:, 130:131]
        logit = reg(x_at, 96).rearrange("p (i e) -> p i e", i=3)
        sel = reg(x_at + 96, 96).rearrange("p (i e) -> p i e", i=3)
        gpad = reg(x_at + 192, 288).rearrange("p (i e) -> p i e", i=3)
        work = reg(x_at + 512, 96).rearrange("p (i e) -> p i e", i=3)
        topi = reg(x_at + 608, 24).bitcast(mybir.dt.uint32).rearrange("p (i k) -> p i k", i=3)
        topf = reg(x_at + 640, 24).rearrange("p (i k) -> p i k", i=3)
        wide = reg(x_at + 512, 1024)
        bdrow = acc[64:96, 2, :]
        nfinal = reg(RA, D)
        wide2 = reg(RA + D, D)
        GtT = Y[64:96, 0:NT]
        assert x_at + 1536 <= nwords

        filled, freed = S("bank_filled"), {"A": S("bank_read_by_act"), "D": S("bank_read_by_dve")}

        def took(eng, name):
            eng.wait_ge(filled, J.filled_at(name))

        def has(eng, name):
            last, n = J.freed_at(name)
            eng.wait_ge(freed[last], n)

        def bank(name, n=512, rows=P):
            return ps[0:rows, J.bank(name), 0:n]

        PAIRS = E // 2

        def up_src(e):
            src = a["w_up"][0]
            src = src[bass.ds(e, 1)] if not isinstance(e, int) else src[e:e + 1]
            return src.rearrange("a (k p) f -> p (a k) f", p=P)

        def down_src(e):
            src = a["w_down"][0]
            src = src[bass.ds(e, 1)] if not isinstance(e, int) else src[e:e + 1]
            return src.rearrange("a (k p) f -> p (a k) f", p=P)

        def over_experts(eng, one):
            one(0, 0, 0, True, False)
            one(1, 1, 0, False, False)
            with eng.Fori(1, PAIRS - 1) as i:
                for h in range(2):
                    one(i * 2 + h, h, i, False, False)
            one(E - 2, 0, PAIRS - 1, False, False)
            one(E - 1, 1, PAIRS - 1, False, True)

        @contextmanager
        def overflowing(eng):
            eng.wait_ge(S("overflow"), 1)
            with eng.If(eng.value_load(over_i[0:1, 0:1], min_val=0, max_val=1) > 0):
                yield

        def moe_sync(sp):
            def one(e, h, pair, first, last):
                if isinstance(e, int) and e + 2 >= E:
                    return
                sp.wait_ge(S("up_done"), e + 1)
                for c_ in range(4):
                    sp.dma_start((upA, upB)[h][:, 2 * c_:2 * c_ + 2, :], up_src(e + 2)[:, 2 * c_:2 * c_ + 2, :]
                                 ).then_inc(S(f"up{'AB'[h]}_in{c_}"), 16)
            over_experts(sp, one)
            sp.wait_ge(S("up_done"), E - 1)
            sp.wait_ge(S("down_done"), E)
            with overflowing(sp):
                with sp.Fori(0, E) as e:
                    sp.wait_ge(S("up_done"), E + e * (NBLK - 1))
                    for c_ in range(4):
                        sp.dma_start(upA[:, 2 * c_:2 * c_ + 2, :], up_src(e)[:, 2 * c_:2 * c_ + 2, :]
                                     ).then_inc(S(f"upA_in{c_}"), 16)
                    sp.wait_ge(S("down_done"), E + e * (NBLK - 1))
                    for c_ in range(2):
                        sp.dma_start(wdn[:, 4 * c_:4 * c_ + 4, :], down_src(e)[:, 4 * c_:4 * c_ + 4, :]
                                     ).then_inc(S(f"down_in{c_}"), 16)
                sp.wait_ge(S("up_done"), E * NBLK)
            sp.dma_start(nfinal, a["norm_final"].rearrange("(a d) -> a d", a=1).broadcast_to([P, D])).then_inc(S("nf_in"), 16)
            for i, (t0, n) in enumerate(TILES):
                sp.wait_ge(S("y"), i + 1)
                dst = o["y_p"][0, t0:t0 + n, :] if i < 2 else o["y_s"][0]
                sp.dma_start(dst, acc[0:n, i, :]).then_inc(S("y_out"), 16)
            sp.wait_ge(S("y_out"), 48)
            sp.wait_ge(S("k_out"), 16)
            sp.wait_ge(S("v_out"), 16)
            sp.wait_ge(S("states_out"), 32)
            sp.wait_ge(S("hist_out"), 32)

        def gather(pe, at_bank):
            for i in range(3):
                for hd in range(2):
                    ins = pe.matmul(ps[64 * hd:64 * hd + 64, at_bank, :], OH[:, i, 0:SLOTS],
                                    Hm[:, i, 512 * hd:512 * hd + 512], start=(i == 0), stop=(i == 2))
            return ins

        def gather_turn(pe, at_bank):
            for q in range(4):
                ins = pe.transpose(ps[:, at_bank, 128 * q:128 * q + 128], XG[:, 128 * q:128 * q + 128], ident[:, :])
            return ins

        def slots_turn(pe, at_bank, e):
            for i, (t0, n) in enumerate(TILES):
                pe.transpose(ps[:, at_bank, t0:t0 + n], OH[0:n, i, :], ident[0:n, 0:n])
            for i in range(3):
                g = Gm[:, i, e:e + 1] if isinstance(e, int) else Gm[:, i, bass.ds(e, 1)]
                ins = pe.matmul(ps[:, at_bank, NT:NT + 1], OH[:, i, :], g, start=(i == 0), stop=(i == 2))
            return ins

        def up_product(pe, w, k0, nk):
            for k in range(k0, k0 + nk):
                for n_ in range(2):
                    for half in range(2):
                        ins = pe.matmul(ps[64 * half:64 * half + 64, n_, :], XTe[:, k % 4, k // 4, :],
                                        w[:, k, 1024 * half + 512 * n_:1024 * half + 512 * n_ + 512],
                                        start=(k == 0), stop=(k == KT - 1))
            return ins

        def up_turn(pe, f0, nf):
            for f in range(f0, f0 + nf):
                ins = pe.transpose(ps[:, 2 + f // 4, 128 * (f % 4):128 * (f % 4) + 128], U[:, 128 * f:128 * f + 128],
                                   ident[:, :])
            return ins

        def down_product(pe, k0, nk):
            for k in range(k0, k0 + nk):
                for n_ in range(2):
                    ins = pe.matmul(ps[64 * n_:64 * n_ + 64, 6, :], lin[:, k, :],
                                    wdn[:, k, 512 * n_:512 * n_ + 512], start=(k == 0), stop=(k == KT - 1))
            return ins

        def combine(pe, i, at_bank=4):
            t0, n = TILES[i]
            for n_ in range(2):
                ins = pe.matmul(ps[0:n, at_bank + n_, :], GT[64 * n_:64 * n_ + 64, t0:t0 + n], Y[64 * n_:64 * n_ + 64, :],
                                start=True, stop=True)
            return ins

        def down_bias(pe, i):
            t0, n = TILES[i]
            for n_ in range(2):
                ins = pe.matmul(ps[0:n, 4 + n_, :], GtT[:, t0:t0 + n], bdrow[:, 512 * n_:512 * n_ + 512],
                                start=True, stop=True)
            return ins

        def moe_tensor(pe):
            has(pe, "GT"), has(pe, "rank")
            pe.wait_ge(S("slots"), 1)
            pe.wait_ge(S("Hm"), 3)
            pe.wait_ge(S("moe_zero"), 2)
            gather(pe, 6).then_inc(S("gathered"), 1)
            pe.wait_ge(S("gather_read"), 1)
            gather_turn(pe, 7).then_inc(S("gather_turned"), 1)

            def one(e, h, pair, first, last):
                pe.wait_ge(S("tokens_in"), e + 1)
                slots_turn(pe, 7, e).then_inc(S("slots_turned"), 1)
                if not first:
                    pe.wait_ge(S("up_read"), e)
                for c_ in range(4):
                    pe.wait_ge(S(f"up{'AB'[h]}_in{c_}"), (pair + 1) * 16)
                    ins = up_product(pe, (upA, upB)[h], 2 * c_, 2)
                ins.then_inc(S("up_done"), 1)
                if first:
                    pe.wait_ge(S("bdown_in"), 16)
                else:
                    pe.wait_ge(S("y_read"), e)
                    pe.wait_ge(S("combined"), e * 3)
                (down_bias if first else combine)(pe, 0).then_inc(S("combine"), 1)
                if not last:
                    pe.wait_ge(S("slots"), e + 2)
                    gather(pe, 6).then_inc(S("gathered"), 1)
                pe.wait_ge(S("combined"), e * 3 + 1)
                (down_bias if first else combine)(pe, 1).then_inc(S("combine"), 1)
                pe.wait_ge(S("up_read"), e + 1)
                if not first:
                    pe.wait_ge(S("act"), e)
                up_turn(pe, 0, 4)
                pe.wait_ge(S("combined"), e * 3 + 2)
                up_turn(pe, 4, 4).then_inc(S("up_turned"), 1)
                (down_bias if first else combine)(pe, 2).then_inc(S("combine"), 1)
                if not last:
                    pe.wait_ge(S("gather_read"), e + 2)
                    pe.wait_ge(S("slots_read"), e + 1)
                    gather_turn(pe, 7).then_inc(S("gather_turned"), 1)
                pe.wait_ge(S("act"), e + 1)
                for c_ in range(2):
                    pe.wait_ge(S(f"down_in{c_}"), (e + 1) * 16)
                    ins = down_product(pe, 4 * c_, 4)
                ins.then_inc(S("down_done"), 1)
            over_experts(pe, one)
            for i in range(3):
                if i == 0:
                    pe.wait_ge(S("y_read"), E)
                    pe.wait_ge(S("slots_read"), E)
                pe.wait_ge(S("combined"), E * 3 + i)
                combine(pe, i).then_inc(S("combine"), 1)
            pe.wait_ge(S("combined"), E * 3 + 3)
            with overflowing(pe), pe.Fori(0, E) as e:
                for b in range(1, NBLK):
                    n = E + e * (NBLK - 1) + (b - 1)
                    pe.wait_ge(S("slots"), n + 1)
                    slots_turn(pe, 7, e).then_inc(S("slots_turned"), 1)
                    gather(pe, 6).then_inc(S("gathered"), 1)
                    pe.wait_ge(S("slots_read"), n + 1)
                    pe.wait_ge(S("gather_read"), n + 1)
                    gather_turn(pe, 7).then_inc(S("gather_turned"), 1)
                    pe.wait_ge(S("tokens_in"), n + 1)
                    pe.wait_ge(S("combined"), n * 3 + 3)
                    for c_ in range(4):
                        if b == 1:
                            pe.wait_ge(S(f"upA_in{c_}"), (PAIRS + 1 + e) * 16)
                        ins = up_product(pe, upA, 2 * c_, 2)
                    ins.then_inc(S("up_done"), 1)
                    pe.wait_ge(S("up_read"), n + 1)
                    up_turn(pe, 0, KT).then_inc(S("up_turned"), 1)
                    pe.wait_ge(S("act"), n + 1)
                    for c_ in range(2):
                        if b == 1:
                            pe.wait_ge(S(f"down_in{c_}"), (E + 1 + e) * 16)
                        ins = down_product(pe, 4 * c_, 4)
                    ins.then_inc(S("down_done"), 1)
                    pe.wait_ge(S("y_read"), n + 1)
                    for i in range(3):
                        combine(pe, i, 4 - 2 * i).then_inc(S("combine"), 1)

        def moe_act(act):
            act.wait_ge(S("gathered"), 1)
            act.activation(XG[:, :], ps[:, 6, :], ACT.Copy).then_inc(S("gather_read"), 1)

            def one(e, h, pair, first, last):
                act.wait_ge(S("up_done"), e + 1)
                act.activation(U[:, :], ps[:, 0:2, :].rearrange("p b f -> p (b f)"), ACT.Copy).then_inc(S("up_read"), 1)
                if not last:
                    act.wait_ge(S("gathered"), e + 2)
                    act.activation(XG[:, :], ps[:, 6, :], ACT.Copy).then_inc(S("gather_read"), 1)
                act.wait_ge(S("combine"), e * 3 + 3)
                act.wait_ge(S("slots_turned"), e + 1)
                act.activation(gate_col, ps[:, 7, NT:NT + 1], ACT.Copy).then_inc(S("gate_col"), 1)
                act.activation(GT[:, :], ps[:, 7, 0:NT], ACT.Copy).then_inc(S("slots_read"), 1)
                act.wait_ge(S("glu"), e * 2 + 2)
                act.activation(sg, glu, ACT.Sigmoid, scale=1.702).then_inc(S("sigmoid"), 1)
                act.wait_ge(S("gate_col"), e + 1)
                act.wait_ge(S("down_done"), e + 1)
                act.activation(Y[:, :], ps[:, 6, :], ACT.Copy, scale=gate_col).then_inc(S("y_read"), 1)
                if not last:
                    for c_ in range(2):
                        act.dma_start(wdn[:, 4 * c_:4 * c_ + 4, :], down_src(e + 1)[:, 4 * c_:4 * c_ + 4, :]
                                      ).then_inc(S(f"down_in{c_}"), 16)
            over_experts(act, one)
            with overflowing(act), act.Fori(0, E) as e:
                for b in range(1, NBLK):
                    n = E + e * (NBLK - 1) + (b - 1)
                    act.wait_ge(S("slots_turned"), n + 1)
                    act.activation(gate_col, ps[:, 7, NT:NT + 1], ACT.Copy).then_inc(S("gate_col"), 1)
                    act.activation(GT[:, :], ps[:, 7, 0:NT], ACT.Copy).then_inc(S("slots_read"), 1)
                    act.wait_ge(S("gathered"), n + 1)
                    act.activation(XG[:, :], ps[:, 6, :], ACT.Copy).then_inc(S("gather_read"), 1)
                    act.wait_ge(S("up_done"), n + 1)
                    act.activation(U[:, :], ps[:, 0:2, :].rearrange("p b f -> p (b f)"), ACT.Copy).then_inc(S("up_read"), 1)
                    act.wait_ge(S("glu"), n * 2 + 2)
                    act.activation(sg, glu, ACT.Sigmoid, scale=1.702).then_inc(S("sigmoid"), 1)
                    act.wait_ge(S("gate_col"), n + 1)
                    act.wait_ge(S("down_done"), n + 1)
                    act.activation(Y[:, :], ps[:, 6, :], ACT.Copy, scale=gate_col).then_inc(S("y_read"), 1)
            for i, (t0, n) in enumerate(TILES):
                act.wait_ge(S("acc_done"), 1)
                act.activation(wide2[0:n, :], acc[0:n, i, :], ACT.Square, accum_out=ss2[0:n, 3 + i:4 + i]).then_inc(S("ssq3"), 1)
                act.wait_ge(S("meansq3"), i + 1)
                act.activation(rs2[0:n, i:i + 1], rs2[0:n, i:i + 1], ACT.Sqrt).then_inc(S("root3"), 1)

        def moe_dve(dve):
            def slots(e, block=0):
                for i in range(3):
                    r = rankx[:, i, e:e + 1] if isinstance(e, int) else rankx[:, i, bass.ds(e, 1)]
                    ins = dve.tensor_scalar(OH[:, i, :], iota[:, :], float(SLOTS * block), r, ALU.add, ALU.is_equal)
                return ins

            def swiglu(e, n, down_done):
                u = ps[:, 2:4, :].rearrange("p b (k s) -> p (b k) s", s=P)
                be = bupT[:, e, :] if isinstance(e, int) else bupT[:, bass.ds(e, 1), :].rearrange("p e f -> p (e f)")
                dve.tensor_tensor(glu, u[:, :, 0:SLOTS], be[:, 0:8].unsqueeze(2).broadcast_to([P, KT, SLOTS]),
                                  ALU.add).then_inc(S("glu"), 1)
                if down_done is not None:
                    dve.wait_ge(S("down_done"), down_done)
                dve.tensor_tensor(lin, u[:, :, SLOTS:P], be[:, 8:16].unsqueeze(2).broadcast_to([P, KT, SLOTS]),
                                  ALU.add).then_inc(S("lin"), 1)
                dve.wait_ge(S("glu"), n * 2 + 1)
                dve.tensor_scalar(glu, glu, 7.0, None, ALU.min).then_inc(S("glu"), 1)
                dve.wait_ge(S("lin"), n * 3 + 1)
                dve.tensor_scalar(lin, lin, 7.0, -7.0, ALU.min, ALU.max).then_inc(S("lin"), 1)
                dve.wait_ge(S("glu"), n * 2 + 2)
                dve.wait_ge(S("lin"), n * 3 + 2)
                dve.scalar_tensor_tensor(lin, lin, 1.0, glu, ALU.add, ALU.mult).then_inc(S("lin"), 1)
                dve.wait_ge(S("lin"), n * 3 + 3)
                dve.wait_ge(S("sigmoid"), n + 1)
                dve.tensor_tensor(lin, lin, sg, ALU.mult).then_inc(S("act"), 1)

            def tokens():
                g = g_moe.rearrange("p (h q) -> p q h", h=2).unsqueeze(3).broadcast_to([P, 4, 2, SLOTS])
                return dve.tensor_tensor(XTe, ps[:, 7, :].rearrange("p (q h s) -> p q h s", q=4, h=2), g, ALU.mult)

            dve.wait_ge(S("rankx"), 3)
            slots(0).then_inc(S("slots"), 1)
            dve.tensor_reduce(nover, rankx.rearrange("p i e -> p (i e)"), AX.X, ALU.max).then_inc(S("rank_max"), 1)
            dve.wait_ge(S("gather_turned"), 1)
            tokens().then_inc(S("tokens_in"), 1)

            def one(e, h, pair, first, last):
                dve.wait_ge(S("slots_turned"), e + 1)
                if not last:
                    slots(e + 1).then_inc(S("slots"), 1)
                def combined(i):
                    dve.wait_ge(S("combine"), e * 3 + i + 1)
                    n = TILES[i][1]
                    dve.tensor_tensor(acc[0:n, i, :], ps[0:n, 4:6, :].rearrange("p b f -> p (b f)"), acc[0:n, i, :],
                                      ALU.add).then_inc(S("combined"), 1)
                combined(0)
                combined(1)
                dve.wait_ge(S("up_turned"), e + 1)
                swiglu(e, e, None if first else e)
                combined(2)
                if not last:
                    dve.wait_ge(S("gather_turned"), e + 2)
                    dve.wait_ge(S("up_done"), e + 1)
                    tokens().then_inc(S("tokens_in"), 1)
            over_experts(dve, one)
            dve.wait_ge(S("nover"), 1)
            dve.tensor_scalar(over_i, small[:, 131:132], float(SLOTS) - 0.5, None, ALU.is_gt).then_inc(S("overflow"), 1)
            for i, (t0, n) in enumerate(TILES):
                dve.wait_ge(S("combine"), E * 3 + i + 1)
                dve.tensor_tensor(acc[0:n, i, :], ps[0:n, 4:6, :].rearrange("p b f -> p (b f)"), acc[0:n, i, :],
                                  ALU.add).then_inc(S("combined"), 1)
            with overflowing(dve), dve.Fori(0, E) as e:
                for b in range(1, NBLK):
                    n = E + e * (NBLK - 1) + (b - 1)
                    slots(e, b).then_inc(S("slots"), 1)
                    dve.wait_ge(S("gather_turned"), n + 1)
                    tokens().then_inc(S("tokens_in"), 1)
                    dve.wait_ge(S("up_turned"), n + 1)
                    swiglu(e, n, None)
                    for i, (t0, rows) in enumerate(TILES):
                        dve.wait_ge(S("combine"), n * 3 + 3 + i + 1)
                        dve.tensor_tensor(acc[0:rows, i, :], ps[0:rows, 4 - 2 * i:6 - 2 * i, :].rearrange("p b f -> p (b f)"),
                                          acc[0:rows, i, :], ALU.add).then_inc(S("combined"), 1)
                    dve.wait_ge(S("combined"), n * 3 + 6)
            dve.wait_ge(S("combined"), E * 3 + 3)
            dve.tensor_copy(all_in[:, :], nover[:, :]).then_inc(S("acc_done"), 1)
            for i, (t0, n) in enumerate(TILES):
                dve.wait_ge(S("ssq3"), i + 1)
                dve.tensor_scalar(rs2[0:n, i:i + 1], ss2[0:n, 3 + i:4 + i], 1.0 / D, EPS, ALU.mult, ALU.add).then_inc(S("meansq3"), 1)
                dve.wait_ge(S("root3"), i + 1)
                dve.reciprocal(rs2[0:n, i:i + 1], rs2[0:n, i:i + 1]).then_inc(S("rstd3"), 1)
                dve.wait_ge(S("rstd3"), i + 1)
                dve.wait_ge(S("nf_in"), 16)
                dve.scalar_tensor_tensor(acc[0:n, i, :], acc[0:n, i, :], rs2[0:n, i:i + 1], nfinal[0:n, :],
                                         ALU.mult, ALU.mult).then_inc(S("y"), 1)

        block = ctx.enter_context(nc.Block())

        @block.sync
        def _(sp):
            def load(dst, src, name):
                sp.dma_start(dst, src).then_inc(S(name), 16)

            win = a["w_in"][0].rearrange("(k p) f -> p k f", p=P)

            def wcols(w, c0, n):
                return w[0].rearrange("(k p) f -> p k f", p=P)[:, :, c0:c0 + n]

            def wrows(w, k0, n):
                return w[0].rearrange("(k p) f -> p k f", p=P)[:, k0:k0 + n, :]

            load(mem[:, :, :], a["mem_prompt"][0].rearrange("(i p) d -> p i d", p=P), "mem_in")
            for i in range(4):
                load(wmk[:, 2 * i:2 * i + 2, :], wrows(a["w_mk"], 2 * i, 2), f"wmk_in{i}")
            load(xtok[:, 0:2, :], a["x_prompt"][0].rearrange("(i p) d -> p i d", p=P), "x_in")
            load(xtok[0:LS, 2, :], a["x_sample"][0], "xs_in")
            for i in range(4):
                load(wmv[:, 2 * i:2 * i + 2, :], wrows(a["w_mv"], 2 * i, 2), f"wmv_in{i}")
            load(w_qk, win[:, :, 0:2 * KW], "wqk_in")
            load(w_v, win[:, :, COL["v"]:COL["v"] + GW], "wv_in")
            load(w_u, win[:, :, COL["u"]:COL["u"] + POOL], "wu_in")
            load(w_g, win[:, :, COL["g"]:COL["g"] + GW], "wg_in")
            has(sp, "K3")
            load(Ks[:, :, :], a["cache_mem_k"][0, 0].rearrange("(i p) h d -> p i (h d)", p=P), "ks_in")
            has(sp, "V3")
            load(Vs[:, :, :], a["cache_mem_v"][0, 0].rearrange("(i p) h d -> p i (h d)", p=P), "vs_in")
            for i in range(4):
                load(wsq[:, i], wcols(a["w_out"], 256 * i, 256), f"wout_in{i}")
            has(sp, "g3")
            load(poolw, a["pool_w"][0].rearrange("g c d -> c g d"), "poolw_in")
            has(sp, "oT3")
            sp.wait_ge(S("hist_out"), 32)
            for i in range(4):
                load(upA[:, 2 * i:2 * i + 2, :], a["w_up"][0, 0].rearrange("(k p) f -> p k f", p=P)[:, 2 * i:2 * i + 2, :], f"upA_in{i}")
            for i in range(4):
                has(sp, f"out{2 * i + 1}")
                load(wsq[:, i], wcols(a["w_mq"], 256 * i, 256), f"wmq_in{i}")
            for i in range(4):
                has(sp, f"mq{2 * i + 1}")
                load(wsq[:, i], wcols(a["w_mo"], 256 * i, 256), f"wmo_in{i}")
            has(sp, "PV4")
            sp.wait_ge(S("v_out"), 16)
            sp.wait_ge(S("states_out"), 32)
            for i in range(4):
                load(upB[:, 2 * i:2 * i + 2, :], a["w_up"][0, 1].rearrange("(k p) f -> p k f", p=P)[:, 2 * i:2 * i + 2, :], f"upB_in{i}")
            has(sp, "mo7")
            for i in range(2):
                load(wdn[:, 4 * i:4 * i + 4, :], a["w_down"][0, 0].rearrange("(k p) f -> p k f", p=P)[:, 4 * i:4 * i + 4, :], f"down_in{i}")
            moe_sync(sp)

        @block.gpsimd
        def _(pool):
            pool.memset(ident[:, :], 0.0).then_inc(S("const0"), 1)
            pool.memset(tri[:, :], 1.0 / 16.0).then_inc(S("const0"), 1)
            pool.memset(ones[:, :], 1.0).then_inc(S("const0"), 1)
            pool.memset(below[:, :], 1.0).then_inc(S("const0"), 1)
            pool.memset(small[:, :], 0.0).then_inc(S("const0"), 1)
            pool.memset(smallrows[:, :], 0.0).then_inc(S("const0"), 1)
            pool.wait_ge(S("const0"), 6)
            pool.affine_select(out=ident[:, :], in_=ident[:, :], compare_op=ALU.not_equal, fill=1.0, base=0,
                               pattern=[[-1, P]], channel_multiplier=1).then_inc(S("const1"), 1)
            r = 0
            for name, n in (("norm_mix", 8), ("norm_mem_q", 8), ("norm_mem_kv", 8), ("norm_moe", 8),
                            ("gla_gain", 4), ("pool_scale", 4)):
                pool.dma_start(smallrows[r:r + n, :], a[name][0].rearrange("(k p) -> k p", p=P)).then_inc(S("vec_in"), 16)
                r += n
            pool.dma_start(buprow[0:E, :], a["b_up"][0]).then_inc(S("bup_in"), 16)
            pool.dma_start(wr_col, a["w_in"][0].rearrange("(k p) f -> p k f", p=P)[:, :, COL["r"]:COL["r"] + RANK]).then_inc(S("wr_in"), 16)
            pool.dma_start(wgate[0:RANK, :], a["w_gate"][0]).then_inc(S("wgate_in"), 16)
            pool.dma_start(wgate[RANK:RANK + 1, :], a["b_gate"]).then_inc(S("wgate_in"), 16)
            pool.affine_select(out=tri[:, :], in_=tri[:, :], compare_op=ALU.is_ge, fill=0.0, base=0,
                               pattern=[[1, P]], channel_multiplier=-1).then_inc(S("const2"), 1)
            pool.wait_ge(S("const2"), 1)
            pool.memset(tri[0:CHUNK, CHUNK:P], 0.0).then_inc(S("const2"), 1)
            pool.affine_select(out=below[:, :], in_=below[:, :], compare_op=ALU.is_gt, fill=0.0, base=0,
                               pattern=[[1, P]], channel_multiplier=-1).then_inc(S("const2"), 1)
            pool.iota(iota[:, :].bitcast(I32), [[0, 2], [1, SLOTS]], 0, 0).then_inc(S("const2"), 1)
            pool.memset(rT[0:32, :], 1.0).then_inc(S("rT_ones"), 1)
            pool.memset(upad[:, :, 0:BUF], 0.0).then_inc(S("upad_zero"), 1)
            pool.dma_start(wr, a["w_router"][0].rearrange("(k p) e -> p k e", p=P)).then_inc(S("router_in"), 16)
            pool.dma_start(brout, a["b_router"].broadcast_to([P, E])).then_inc(S("router_in"), 16)
            has(pool, "vec")
            pool.dma_start(prevrow[0:BUF, :], a["state_pool"][0, 0]).then_inc(S("prev_in"), 16)
            has(pool, "K3")
            pool.dma_start(o["mem_k"][0, 0].rearrange("(i p) h d -> p i (h d)", p=P), Kp[:, :, :]).then_inc(S("k_out"), 16)
            has(pool, "V3")
            pool.dma_start(o["mem_v"][0, 0].rearrange("(i p) h d -> p i (h d)", p=P), Vp[:, :, :]).then_inc(S("v_out"), 16)
            pool.dma_start(Sbuf[4], a["state_gla"][0, 0].rearrange("(r h) d e -> (h d) r e", r=2)).then_inc(S("s0_in"), 16)
            has(pool, "v2")
            for z in (qdz, klz, AT):
                pool.memset(z, 0.0).then_inc(S("gla_zero"), 1)
            has(pool, "u3")
            for g in range(4):
                w = 2 << g
                pool.memset(invn[:, g, :], 1.0 / w).then_inc(S("invn"), 1)
            pool.wait_ge(S("invn"), 4)
            n = 4
            for g in range(4):
                for t in range((2 << g) - 1):
                    pool.memset(invn[:, g, t:t + 1], 1.0 / (t + 1)).then_inc(S("invn"), 1)
                    n += 1
            has(pool, "prevT")
            src, steps = upad, 0
            for j in range(4):
                dst = (s_a, s_b)[j % 2]
                if j:
                    pool.wait_ge(S("window"), steps)
                off = 1 << j
                pool.tensor_tensor(dst[:, j:4, off:UPAD], src[:, j:4, off:UPAD], src[:, j:4, 0:UPAD - off],
                                   ALU.add).then_inc(S("window"), 1)
                steps += 1
                if j == 0:
                    pool.tensor_copy(dst[:, :, 0:off], src[:, :, 0:off]).then_inc(S("window"), 1)
                    steps += 1
                elif j < 3:
                    pool.tensor_copy(dst[:, j:4, 0:off], src[:, j:4, 0:off]).then_inc(S("window"), 1)
                    steps += 1
                src = dst
            pool.wait_ge(S("invn"), n)
            pool.wait_ge(S("window"), steps)
            k = 0
            for g in range(4):
                sg_ = (s_a, s_b)[g % 2]
                for t0, n0, u0 in ((0, LP, BUF), (LP, LS, UP_P + BUF)):
                    pool.tensor_tensor(sg_[:, g, u0:u0 + n0], sg_[:, g, u0:u0 + n0], invn[:, g, t0:t0 + n0],
                                       ALU.mult).then_inc(S("mean"), 1)
                    k += 1
                    pool.wait_ge(S("mean"), k)
                    pool.tensor_tensor(invn[:, g, t0:t0 + n0], sg_[:, g, u0:u0 + n0], upad[:, g, u0:u0 + n0],
                                       ALU.subtract).then_inc(S("pool_diff"), 1)
            has(pool, "ds4")
            pool.wait_ge(S("state"), 15)
            pool.dma_start(o["gla_p"][0, 0].rearrange("(r h) d e -> (h d) r e", r=2), Sbuf[3]).then_inc(S("states_out"), 16)
            pool.dma_start(o["gla_s"][0, 0].rearrange("(r h) d e -> (h d) r e", r=2), Sbuf[5]).then_inc(S("states_out"), 16)
            has(pool, "hist1")
            for i, name in enumerate(("pool_p", "pool_s")):
                pool.dma_start(o[name][0, 0], hist[0:BUF, i, :]).then_inc(S("hist_out"), 16)
            has(pool, "mo7")
            pool.wait_ge(S("states_out"), 32)
            pool.wait_ge(S("k_out"), 16)
            pool.memset(Hm[64:P, 2, :], 0.0).then_inc(S("moe_zero"), 1)
            pool.wait_ge(S("moe_zero"), 1)
            pool.memset(gpad[:, :, :], 0.0).then_inc(S("moe_zero"), 1)
            pool.dma_start(bdrow, a["b_down"][0]).then_inc(S("bdown_in"), 16)
            pool.wait_ge(S("rank_max"), 1)
            pool.partition_all_reduce(small[:, 131:132], nover, P, bass.bass_isa.ReduceOp.max).then_inc(S("nover"), 1)

        @block.scalar
        def _(act):
            def copy(dst, src, name=None, scale=1.0):
                i = act.activation(dst, src, ACT.Copy, scale=scale)
                return i

            def free(ins, name):
                assert J.freed_at(name) == ("A", free.n + 1), name
                free.n += 1
                ins.then_inc(freed["A"], 1)
            free.n = 0
            act.wait_ge(S("const0"), 6)
            act.wait_ge(S("mem_in"), 16)
            for i in range(2):
                if i:
                    act.wait_ge(S("ssq_mem"), i)
                act.activation(catT.rearrange("p k t -> p (k t)")[:, 0:D], mem[:, i, :], ACT.Square,
                               accum_out=ssm[:, i:i + 1]).then_inc(S("ssq_mem"), 1)
            act.wait_ge(S("x_in"), 16)
            act.wait_ge(S("xs_in"), 16)
            for i, (t0, n) in enumerate(TILES):
                if i:
                    act.wait_ge(S("ssq_x"), i)
                act.activation(catT.rearrange("p k t -> p (k t)")[0:n, 1024:1024 + D], xtok[0:n, i, :], ACT.Square,
                               accum_out=ssx[0:n, i:i + 1]).then_inc(S("ssq_x"), 1)
            act.wait_ge(S("meansq0"), 1)
            act.activation(sst[:, 0:5], sst[:, 0:5], ACT.Sqrt).then_inc(S("root0"), 1)
            has(act, "vec")
            for i in range(4):
                took(act, f"memT{i}")
                b = bank(f"memT{i}")
                act.activation(memT[:, 2 * i, :], b[:, 0:256], ACT.Copy, scale=g_memkv[:, 2 * i:2 * i + 1])
                free(act.activation(memT[:, 2 * i + 1, :], b[:, 256:512], ACT.Copy,
                                    scale=g_memkv[:, 2 * i + 1:2 * i + 2]), f"memT{i}")
            act.wait_ge(S("rstd0"), 1)
            def gained(k):
                has(act, f"xT{k}")
                if k == 0:
                    has(act, "bup")
                act.activation(gxT[:, k, :], xT[:, k, :], ACT.Copy, scale=g_mix[:, k:k + 1]).then_inc(S("gx"), 1)
            for i in range(4):
                took(act, f"K{i}")
                if i == 0:
                    act.wait_ge(S("ssq_x"), 3)
                free(act.activation(Kp[:, i // 2, 512 * (i % 2):512 * (i % 2) + 512], bank(f"K{i}"), ACT.Copy,
                                    scale=rsm[:, i // 2:i // 2 + 1]), f"K{i}")
            for k in range(KT):
                gained(k)
            for i in range(4):
                took(act, f"V{i}")
                free(act.activation(Vp[:, i // 2, 512 * (i % 2):512 * (i % 2) + 512], bank(f"V{i}"), ACT.Copy,
                                    scale=rsm[:, i // 2:i // 2 + 1]), f"V{i}")
            for i in range(4):
                took(act, f"KTp{i}")
                free(act.activation(KTp[:, 2 * i:2 * i + 2, :].rearrange("p k m -> p (k m)"), bank(f"KTp{i}"),
                                    ACT.Copy), f"KTp{i}")
            for j, (i0, ni, n) in enumerate(((0, 2, P), (2, 1, 64))):
                took(act, f"gate{j}")
                act.wait_ge(S("gate_min"), j + 1)
                free(act.activation(la1[0:n, i0:i0 + ni, :].rearrange("p i f -> p (i f)"), bank(f"gate{j}", 256 * ni, n),
                                    ACT.Abs), f"gate{j}")
            for j, (i0, ni, n) in enumerate(((0, 2, P), (2, 1, 64))):
                v_ = la1[0:n, i0:i0 + ni, :].rearrange("p i f -> p (i f)")
                has(act, f"gate{j}")
                act.activation(v_, v_, ACT.Exp, scale=-1.0).then_inc(S("gate_exp"), 1)
                act.wait_ge(S("gate_exp"), j + 1)
                act.activation(v_, v_, ACT.Ln, bias=1.0).then_inc(S("gate_ln"), 1)
            for i, (t0, n) in enumerate(TILES):
                took(act, f"v{i}")
                free(act.activation(vtok[0:n, i, :], bank(f"v{i}", 512, n), ACT.Copy, scale=rsx[0:n, i:i + 1]), f"v{i}")
            has(act, "cum1")
            fl = lambda z: z.rearrange("p r t -> p (r t)")
            act.activation(fl(eb), fl(bT), ACT.Exp).then_inc(S("eb"), 1)
            act.activation(fl(enb), fl(bT), ACT.Exp, scale=-1.0).then_inc(S("enb"), 1)
            act.wait_ge(S("bl_diff"), 1)
            act.activation(fl(ebl), fl(ebl), ACT.Exp).then_inc(S("ebl"), 1)
            took(act, "prevT")
            free(act.activation(upad[:, :, UP_P:UP_P + BUF], bank("prevT", 4 * BUF).rearrange("p (g t) -> p g t", g=4),
                                ACT.Copy), "prevT")
            act.wait_ge(S("gla_zero"), 2)
            for c_ in range(5):
                i, r0 = c_ // 2, 64 * (c_ % 2)
                j = 0 if i < 2 else 1
                if c_ in (0, 4):
                    took(act, f"klT{j}")
                b = ps[r0:r0 + 64, J.bank(f"klT{j}"), 256 * (i % 2):256 * (i % 2) + 256]
                ins = act.activation(klz[r0:r0 + 64, c_, :], b, ACT.Copy)
                if c_ in (3, 4):
                    free(ins, f"klT{j}")
            has(act, "g3")
            act.activation(sgT_e, sgT_f, ACT.Exp, scale=-1.0).then_inc(S("g_exp"), 1)
            for i in range(4):
                took(act, f"KTs{i}")
                free(act.activation(KTs[:, 2 * i:2 * i + 2, :].rearrange("p k m -> p (k m)"), bank(f"KTs{i}"),
                                    ACT.Copy), f"KTs{i}")
            for i, (t0, n) in enumerate(TILES):
                has(act, f"o{i}")
                act.activation(osq[0:n, i, :], otok[0:n, i, :], ACT.Square).then_inc(S("o_sq"), 1)
            act.wait_ge(S("meansq_o"), 1)
            act.activation(small[:, 22:34], small[:, 22:34], ACT.Sqrt).then_inc(S("root_o"), 1)
            for i in range(2):
                took(act, f"hist{i}")
                free(act.activation(hist[0:BUF, i, :], bank(f"hist{i}", 512, BUF), ACT.Copy), f"hist{i}")
            for k in range(KT):
                has(act, f"out{k}")
                if k == 0:
                    has(act, "g3")
                act.activation(gxT[:, k, :], xT[:, k, :], ACT.Copy, scale=g_memq[:, k:k + 1]).then_inc(S("gx1"), 1)
                act.activation(sq1[:, k, :], xT[:, k, :], ACT.Square).then_inc(S("sq1"), 1)
            has(act, "rms1")
            act.activation(rstdb[:, :], rstdb[:, :], ACT.Sqrt).then_inc(S("root1"), 1)
            for j in range(6):
                took(act, f"s{j}")
                act.wait_ge(S("nmax"), j + 1)
                n = P if j < 4 else 64
                for h2 in range(2):
                    h = 2 * (j % 2) + h2
                    dst = probs_p[:, j // 2, h, :] if j < 4 else probs_s[0:64, h, :]
                    cidx = (j // 2) * 4 + h
                    ins = act.activation(dst, bank(f"s{j}", 512, n)[:, 256 * h2:256 * h2 + 256], ACT.Exp,
                                         bias=nmx[0:n, cidx:cidx + 1], scale=1.0 / 16.0,
                                         accum_out=rs[0:n, cidx:cidx + 1])
                free(ins, f"s{j}")
            for h in range(4):
                took(act, f"PV{h}")
                free(act.activation(aoT[:, 2 * h:2 * h + 2, 0:LP], bank(f"PV{h}").rearrange("p (d l) -> p d l", d=2),
                                    ACT.Copy), f"PV{h}")
            took(act, "PV4")
            free(act.activation(aoT[:, :, LP:NT], bank("PV4").rearrange("p (d l) -> p d l", d=KT), ACT.Copy), "PV4")
            has(act, "mo7")
            for j in range(6):
                i, n = j // 2, TILES[j // 2][1]
                took(act, f"x2_{j}")
                free(act.activation(acc[0:n, i, 512 * (j % 2):512 * (j % 2) + 512], bank(f"x2_{j}", 512, n), ACT.Copy),
                     f"x2_{j}")
                if j % 2:
                    has(act, f"x2_{j}")
                    act.activation(wide[0:n, :], acc[0:n, i, :], ACT.Square,
                                   accum_out=ss2[0:n, i:i + 1]).then_inc(S("ssq2"), 1)
            act.wait_ge(S("meansq2"), 1)
            act.activation(rs2[:, :], rs2[:, :], ACT.Sqrt).then_inc(S("root2"), 1)
            act.wait_ge(S("top"), 1)
            for i, (t0, n) in enumerate(TILES):
                act.activation(gpad[0:n, i, 64:96], logit[0:n, i, :], ACT.Exp, bias=nt1[0:n, i:i + 1],
                               scale=1.0).then_inc(S("gate_e"), 1)
            took(act, "GT")
            free(act.activation(GtT, ps[64:96, J.bank("GT"), 0:NT], ACT.Copy), "GT")
            moe_act(act)

        @block.vector
        def _(dve):
            def free(ins, name):
                assert J.freed_at(name) == ("D", free.n + 1), (name, free.n)
                free.n += 1
                ins.then_inc(freed["D"], 1)
            free.n = 0
            dve.wait_ge(S("const2"), 4)
            dve.tensor_copy(iota[:, :], iota[:, :].bitcast(I32)).then_inc(S("iota"), 1)
            took(dve, "vec")
            free(dve.tensor_copy(vec[:, :], bank("vec", 40)), "vec")
            took(dve, "bup")
            free(dve.tensor_copy(bupT.rearrange("p e f -> p f e"), bank("bup").rearrange("p (f e) -> p f e", e=E)), "bup")
            dve.wait_ge(S("ssq_mem"), 2)
            dve.wait_ge(S("ssq_x"), 3)
            dve.tensor_scalar(sst[:, 0:5], small[:, 0:5], 1.0 / D, EPS, ALU.mult, ALU.add).then_inc(S("meansq0"), 1)
            dve.wait_ge(S("root0"), 1)
            dve.reciprocal(small[:, 5:10], sst[:, 0:5]).then_inc(S("rstd0"), 1)
            for k in range(KT):
                took(dve, f"xT{k}")
                free(dve.tensor_copy(xT[:, k, :], bank(f"xT{k}", NT)), f"xT{k}")
                if k == 0:
                    dve.wait_ge(S("rstd0"), 1)
                    for i in range(3):
                        dve.tensor_scalar(rT_diag[:, i, :], ident[:, :], rsx[:, i:i + 1], None,
                                          ALU.mult).then_inc(S("diag"), 1)
            took(dve, "rms0")
            free(dve.tensor_copy(rstdb[:, :], bank("rms0", NT)), "rms0")
            has(dve, "rms0")
            took(dve, "r")
            dve.wait_ge(S("rT_ones"), 1)
            free(dve.tensor_tensor(rT[0:RANK, :], bank("r", NT, RANK), rstdb[0:RANK, :], ALU.mult), "r")
            for j in range(2):
                took(dve, f"q{j}")
                free(dve.tensor_tensor(qT[:, j, :], bank(f"q{j}", NT), rstdb[:, :], ALU.mult), f"q{j}")
            dve.wait_ge(S("k_out"), 16)
            for j, (i0, ni, n) in enumerate(((0, 2, P), (2, 1, 64))):
                took(dve, f"gate{j}")
                dve.tensor_scalar(la0[0:n, i0:i0 + ni, :].rearrange("p i f -> p (i f)"), bank(f"gate{j}", 256 * ni, n),
                                  0.0, None, ALU.min).then_inc(S("gate_min"), 1)
            for j in range(2):
                took(dve, f"k{j}")
                free(dve.tensor_tensor(kT[:, j, :], bank(f"k{j}", NT), rstdb[:, :], ALU.mult), f"k{j}")
            dve.wait_ge(S("gate_ln"), 2)
            for j, (i0, ni, n) in enumerate(((0, 2, P), (2, 1, 64))):
                dve.tensor_tensor(la0[0:n, i0:i0 + ni, :], la0[0:n, i0:i0 + ni, :], la1[0:n, i0:i0 + ni, :],
                                  ALU.subtract).then_inc(S("log_a"), 1)
            for j in range(2):
                took(dve, f"cum{j}")
                free(dve.tensor_copy(bT[:, j, :], bank(f"cum{j}", NT)), f"cum{j}")
            has(dve, "cum1")
            for r_ in range(2):
                bc = bT[:, r_, :].rearrange("p (c t) -> p c t", c=5)
                last = dve.tensor_tensor(ebl[:, r_, :].rearrange("p (c t) -> p c t", c=5),
                                         bc[:, :, CHUNK - 1:CHUNK].broadcast_to([P, 5, CHUNK]), bc, ALU.subtract)
            last.then_inc(S("bl_diff"), 1)
            dve.wait_ge(S("gla_zero"), 3)
            dve.wait_ge(S("eb"), 1)
            for h in range(4):
                r0 = 64 * (h % 2)
                dve.scalar_tensor_tensor(qdz[r0:r0 + 64, h, :], qT[r0:r0 + 64, h // 2, :], DK ** -0.5,
                                         eb[r0:r0 + 64, h // 2, :], ALU.mult, ALU.mult).then_inc(S("qd"), 1)
            dve.wait_ge(S("enb"), 1)
            fl = lambda z: z.rearrange("p r t -> p (r t)")
            dve.tensor_tensor(fl(kdT), fl(kT), fl(enb), ALU.mult).then_inc(S("kd"), 1)
            dve.wait_ge(S("ebl"), 1)
            dve.tensor_tensor(fl(ebl), fl(kT), fl(ebl), ALU.mult).then_inc(S("kl"), 1)
            for g in range(4):
                took(dve, f"u{g}")
                b = bank(f"u{g}", NT)
                dve.tensor_tensor(upad[:, g, BUF:UP_P], b[:, 0:LP], rstdb[:, 0:LP], ALU.mult)
                free(dve.tensor_tensor(upad[:, g, UP_P + BUF:UPAD], b[:, LP:NT], rstdb[:, LP:NT], ALU.mult), f"u{g}")
            for i, (t0, n) in enumerate(TILES):
                took(dve, f"AT{i}")
                m = tri[0:n, 0:n].bitcast(I32).unsqueeze(1).broadcast_to([n, 4, n])
                free(dve.copy_predicated(AT[0:n, i, :, 0:n], m, bank(f"AT{i}", 4 * n, n).rearrange("p (h t) -> p h t", h=4)),
                     f"AT{i}")
            for g in range(4):
                took(dve, f"g{g}")
                free(dve.tensor_tensor(sgT[:, g, :], bank(f"g{g}", NT), rstdb[:, :], ALU.mult), f"g{g}")
            n = 0
            for c_ in range(NCH):
                took(dve, f"ds{c_}")
                b = bank(f"ds{c_}").rearrange("p (r f) -> p r f", r=2)
                src = {0: None, 1: Sbuf[0], 2: Sbuf[1], 3: Sbuf[2], 4: Sbuf[4]}[c_]
                dst = Sbuf[c_] if c_ < 4 else Sbuf[5]
                if c_ in (1, 2, 3):
                    dve.wait_ge(S("state"), n)
                if c_ == 4:
                    dve.wait_ge(S("s0_in"), 16)
                    has(dve, "prevT")
                for hh in range(2):
                    r0 = 64 * hh
                    for r_ in range(2):
                        bb = b[r0:r0 + 64, r_, 128 * hh:128 * hh + 128]
                        if src is None:
                            ins = dve.tensor_copy(dst[r0:r0 + 64, r_, :], bb)
                        else:
                            ins = dve.scalar_tensor_tensor(dst[r0:r0 + 64, r_, :], src[r0:r0 + 64, r_, :],
                                                           eb[r0:r0 + 64, r_, CHUNK * c_ + 63:CHUNK * c_ + 64], bb,
                                                           ALU.mult, ALU.add)
                        if (hh, r_) == (1, 1):
                            free(ins, f"ds{c_}")
                        else:
                            ins.then_inc(S("state"), 1)
                            n += 1
                has(dve, f"ds{c_}")
            dve.wait_ge(S("g_exp"), 1)
            dve.tensor_scalar(sgT_e, sgT_e, 1.0, None, ALU.add).then_inc(S("silu"), 1)
            dve.wait_ge(S("silu"), 1)
            dve.reciprocal(sgT_e, sgT_e).then_inc(S("silu"), 1)
            dve.wait_ge(S("silu"), 2)
            dve.tensor_tensor(sgT_f, sgT_f, sgT_e, ALU.mult).then_inc(S("silu"), 1)
            for g in range(4):
                took(dve, f"pool{g}")
                free(dve.tensor_scalar(catT[:, 4 + g, :], bank(f"pool{g}", NT), pscale[:, g:g + 1], None, ALU.mult),
                     f"pool{g}")
            for i, (t0, n) in enumerate(TILES):
                took(dve, f"o{i}")
                free(dve.tensor_copy(otok[0:n, i, :], bank(f"o{i}", 512, n)), f"o{i}")
            for i, (t0, n) in enumerate(TILES):
                dve.wait_ge(S("o_sq"), i + 1)
                dve.tensor_reduce(sso[0:n, i, :], osq[0:n, i, :].rearrange("p (h e) -> p h e", h=4), AX.X,
                                  ALU.add).then_inc(S("o_sum"), 1)
            dve.wait_ge(S("o_sum"), 3)
            dve.tensor_scalar(small[:, 22:34], small[:, 10:22], 1.0 / DV, EPS, ALU.mult, ALU.add).then_inc(S("meansq_o"), 1)
            dve.wait_ge(S("root_o"), 1)
            dve.reciprocal(small[:, 22:34], small[:, 22:34]).then_inc(S("rstd_o"), 1)
            dve.wait_ge(S("rstd_o"), 1)
            for i, (t0, n) in enumerate(TILES):
                v_ = otok[0:n, i, :].rearrange("p (h e) -> p h e", h=4)
                dve.tensor_tensor(v_, v_, rso[0:n, i, :].unsqueeze(2).broadcast_to([n, 4, DV]),
                                  ALU.mult).then_inc(S("o_norm"), 1)
            dve.wait_ge(S("silu"), 3)
            for h in range(4):
                took(dve, f"oT{h}")
                free(dve.scalar_tensor_tensor(catT[:, h, :], bank(f"oT{h}", NT), g_gla[:, h:h + 1], sgT[:, h, :],
                                              ALU.mult, ALU.mult), f"oT{h}")
            for k in range(KT):
                took(dve, f"out{k}")
                free(dve.tensor_tensor(xT[:, k, :], bank(f"out{k}", NT), xT[:, k, :], ALU.add), f"out{k}")
            def queries(k):
                took(dve, f"mq{k}")
                free(dve.tensor_tensor(aqT[:, k, :], bank(f"mq{k}", NT), rstdb[:, :], ALU.mult), f"mq{k}")
            took(dve, "rms1")
            free(dve.tensor_scalar(rstdb[:, :], bank("rms1", NT), 1.0 / D, EPS, ALU.mult, ALU.add), "rms1")
            dve.wait_ge(S("root1"), 1)
            dve.reciprocal(rstdb[:, :], rstdb[:, :]).then_inc(S("rstd1"), 1)
            dve.wait_ge(S("rstd1"), 1)
            for k in range(KT):
                queries(k)
            for j in range(6):
                took(dve, f"s{j}")
                n = P if j < 4 else 64
                c0 = (j // 2) * 4 + 2 * (j % 2)
                dve.tensor_reduce(mx[0:n, c0:c0 + 2], bank(f"s{j}", 512, n).rearrange("p (h m) -> p h m", h=2), AX.X,
                                  ALU.max).then_inc(S("smax"), 1)
                dve.wait_ge(S("smax"), j + 1)
                dve.tensor_scalar(nmx[0:n, c0:c0 + 2], mx[0:n, c0:c0 + 2], -1.0 / 16.0, None,
                                  ALU.mult).then_inc(S("nmax"), 1)
            m = 0
            for j in range(6):
                has(dve, f"s{j}")
                n = P if j < 4 else 64
                c0 = (j // 2) * 4 + 2 * (j % 2)
                dve.reciprocal(rinv[0:n, c0:c0 + 2], rs[0:n, c0:c0 + 2]).then_inc(S("rinv"), 1)
                dve.wait_ge(S("rinv"), j + 1)
                for h2 in range(2):
                    h = 2 * (j % 2) + h2
                    v_ = probs_p[:, j // 2, h, :] if j < 4 else probs_s[0:64, h, :]
                    dve.tensor_scalar(v_, v_, rinv[0:n, c0 + h2:c0 + h2 + 1], None, ALU.mult).then_inc(S("probs"), 1)
            for h in range(4):
                took(dve, f"PT{h}")
                free(dve.tensor_copy(PTp[:, h, :, :].rearrange("p i l -> p (i l)"), bank(f"PT{h}")), f"PT{h}")
            took(dve, "PT4")
            free(dve.tensor_copy(PTs.rearrange("p h i l -> p (h i l)"), bank("PT4")), "PT4")
            dve.wait_ge(S("router_in"), 32)
            dve.tensor_tensor(gwr, wr, g_moe.unsqueeze(2).broadcast_to([P, KT, E]), ALU.mult).then_inc(S("gwr"), 1)
            for k in range(KT):
                took(dve, f"mo{k}")
                free(dve.tensor_tensor(xT[:, k, :], bank(f"mo{k}", NT), xT[:, k, :], ALU.add), f"mo{k}")
            dve.wait_ge(S("ssq2"), 3)
            dve.tensor_scalar(rs2[:, :], ss2[:, 0:3], 1.0 / D, EPS, ALU.mult, ALU.add).then_inc(S("meansq2"), 1)
            dve.wait_ge(S("root2"), 1)
            dve.reciprocal(rs2[:, :], rs2[:, :]).then_inc(S("rstd2"), 1)
            dve.wait_ge(S("rstd2"), 1)
            took(dve, "router")
            for i, (t0, n) in enumerate(TILES):
                ins = dve.scalar_tensor_tensor(logit[0:n, i, :], ps[0:n, J.bank("router"), 32 * i:32 * i + 32],
                                               rs2[0:n, i:i + 1], brout[0:n, :], ALU.mult, ALU.add)
            free(ins, "router")
            has(dve, "router")
            dve.wait_ge(S("moe_zero"), 2)
            for i, (t0, n) in enumerate(TILES):
                dve.max(top8[0:n, i, :], logit[0:n, i, :]).then_inc(S("max8"), 1)
            dve.memset(rankx[64:P, 2, :], -1.0)
            dve.memset(Gm[64:P, 2, :], 0.0)
            dve.memset(sel[64:P, 2, :], 0.0).then_inc(S("max8"), 1)
            dve.wait_ge(S("max8"), 4)
            dve.tensor_scalar(nt1[:, :], top8[:, :, 0], -1.0, None, ALU.mult).then_inc(S("top"), 1)
            for i, (t0, n) in enumerate(TILES):
                dve.max_index(topi[0:n, i, :], top8[0:n, i, :], logit[0:n, i, :]).then_inc(S("top_at"), 1)
            dve.wait_ge(S("top_at"), 3)
            for i, (t0, n) in enumerate(TILES):
                dve.tensor_copy(topf[0:n, i, :], topi[0:n, i, :]).then_inc(S("top_at"), 1)
            dve.wait_ge(S("top_at"), 6)
            for k in range(4):
                for i, (t0, n) in enumerate(TILES):
                    if k == 0:
                        ins = dve.tensor_scalar(sel[0:n, i, :], iota[0:n, 0:E], topf[0:n, i, 0:1], None, ALU.is_equal)
                    else:
                        ins = dve.scalar_tensor_tensor(sel[0:n, i, :], iota[0:n, 0:E], topf[0:n, i, k:k + 1],
                                                       sel[0:n, i, :], ALU.is_equal, ALU.add)
                    ins.then_inc(S("sel"), 1)
                dve.wait_ge(S("sel"), 3 * k + 3)
            dve.wait_ge(S("sel"), 12)
            dve.wait_ge(S("gate_e"), 3)
            for i, (t0, n) in enumerate(TILES):
                dve.tensor_tensor(gpad[0:n, i, 64:96], gpad[0:n, i, 64:96], sel[0:n, i, :], ALU.mult).then_inc(S("gsel"), 1)
            dve.wait_ge(S("gsel"), 3)
            dve.tensor_reduce(gsum[:, :], gpad[:, :, 64:96], AX.X, ALU.add).then_inc(S("gsel"), 1)
            dve.wait_ge(S("gsel"), 4)
            dve.reciprocal(gsum[:, 0:2], gsum[:, 0:2]).then_inc(S("gsel"), 1)
            dve.reciprocal(gsum[0:64, 2:3], gsum[0:64, 2:3]).then_inc(S("gsel"), 1)
            dve.wait_ge(S("gsel"), 6)
            for i, (t0, n) in enumerate(TILES):
                dve.tensor_scalar(gpad[0:n, i, 64:96], gpad[0:n, i, 64:96], gsum[0:n, i:i + 1], None,
                                  ALU.mult).then_inc(S("gates"), 1)
            dve.wait_ge(S("gates"), 3)
            for i, (t0, n) in enumerate(TILES):
                dve.tensor_copy(Gm[0:n, i, :], gpad[0:n, i, 64:96]).then_inc(S("Gm"), 1)
            took(dve, "rank")
            for i, (t0, n) in enumerate(TILES):
                ins = dve.scalar_tensor_tensor(rankx[0:n, i, :], ps[0:n, J.bank("rank"), 32 * i:32 * i + 32], 1.0,
                                               sel[0:n, i, :], ALU.add, ALU.mult)
            free(ins, "rank")
            has(dve, "rank")
            for i, (t0, n) in enumerate(TILES):
                dve.tensor_scalar(rankx[0:n, i, :], rankx[0:n, i, :], -1.0, None, ALU.add).then_inc(S("rankx"), 1)
            for i, (t0, n) in enumerate(TILES):
                dve.tensor_scalar(Hm[0:n, i, :], acc[0:n, i, :], rs2[0:n, i:i + 1], None, ALU.mult).then_inc(S("Hm"), 1)
            moe_dve(dve)

        @block.tensor
        def _(pe):
            def begin(name):
                before = J.occupant_before(name)
                if before:
                    pe.wait_ge(freed[before[0]], before[1])

            def end(ins):
                ins.then_inc(filled, 1)

            def turn(name, pieces):
                begin(name)
                for c0, src, rows, cols in pieces:
                    ins = pe.transpose(ps[0:cols, J.bank(name), c0:c0 + rows], src, ident[0:rows, 0:rows])
                end(ins)

            def project(name, w, x, rows=P):
                begin(name)
                for k in range(KT):
                    ins = pe.matmul(bank(name, NT, rows), w[:, k, :], x[:, k, :], start=(k == 0), stop=(k == KT - 1))
                end(ins)

            pe.wait_ge(S("const1"), 1)
            pe.wait_ge(S("vec_in"), 96)
            turn("vec", [(0, smallrows[0:40, :], 40, P)])
            pe.wait_ge(S("bup_in"), 16)
            turn("bup", [(E * f, buprow[0:E, 128 * f:128 * f + 128], E, P) for f in range(16)])
            pe.wait_ge(S("mem_in"), 16)
            for j in range(4):
                turn(f"memT{j}", [(256 * kk + 128 * i, mem[:, i, 128 * (2 * j + kk):128 * (2 * j + kk) + 128], P, P)
                                  for kk in range(2) for i in range(2)])

            def memory_product(what, w, sem):
                for j in range(4):
                    begin(f"{what}{j}")
                for k in range(KT):
                    if k % 2 == 0:
                        pe.wait_ge(S(f"{sem}{k // 2}"), 16)
                        if what == "K":
                            has(pe, f"memT{k // 2}")
                    for j in range(4):
                        ins = pe.matmul(bank(f"{what}{j}"), memT[:, k, 128 * (j // 2):128 * (j // 2) + 128],
                                        w[:, k, 512 * (j % 2):512 * (j % 2) + 512], start=(k == 0), stop=(k == KT - 1))
                        if k == KT - 1:
                            end(ins)
            memory_product("K", wmk, "wmk_in")
            pe.wait_ge(S("x_in"), 16)
            pe.wait_ge(S("xs_in"), 16)
            for k in range(KT):
                turn(f"xT{k}", [(t0, xtok[0:n, i, 128 * k:128 * k + 128], n, P) for i, (t0, n) in enumerate(TILES)])
            pe.wait_ge(S("diag"), 3)
            begin("rms0")
            for i, (t0, n) in enumerate(TILES):
                ins = pe.matmul(bank("rms0", NT)[:, t0:t0 + n], ones[0:n, :], rT_diag[0:n, i, 0:n], start=True, stop=True)
            end(ins)
            memory_product("V", wmv, "wmv_in")
            has(pe, "K3")
            for j in range(4):
                turn(f"KTp{j}", [(256 * kk + 128 * i, Kp[:, i, 128 * (2 * j + kk):128 * (2 * j + kk) + 128], P, P)
                                 for kk in range(2) for i in range(2)])
            pe.wait_ge(S("gx"), 8)
            pe.wait_ge(S("wr_in"), 16)
            project("r", wr_col, gxT, RANK)
            pe.wait_ge(S("wqk_in"), 16)
            project("q0", w_qk[:, :, 0:128], gxT)
            project("q1", w_qk[:, :, 128:256], gxT)
            pe.wait_ge(S("wgate_in"), 32)
            has(pe, "r")
            for j, tiles in enumerate(((0, 1), (2,))):
                begin(f"gate{j}")
                for m, i in enumerate(tiles):
                    t0, n = TILES[i]
                    ins = pe.matmul(ps[0:n, J.bank(f"gate{j}"), 256 * m:256 * m + 256], rT[0:RANK + 1, t0:t0 + n],
                                    wgate[0:RANK + 1, :], start=True, stop=True)
                end(ins)
            project("k0", w_qk[:, :, 256:384], gxT)
            project("k1", w_qk[:, :, 384:512], gxT)
            pe.wait_ge(S("wv_in"), 16)
            for i, (t0, n) in enumerate(TILES):
                begin(f"v{i}")
                for k in range(KT):
                    ins = pe.matmul(bank(f"v{i}", 512, n), gxT[:, k, t0:t0 + n], w_v[:, k, :], start=(k == 0),
                                    stop=(k == KT - 1))
                end(ins)
            pe.wait_ge(S("log_a"), 2)
            pe.wait_ge(S("const2"), 4)
            for j in range(2):
                begin(f"cum{j}")
                for i, (t0, n) in enumerate(TILES):
                    ins = pe.matmul(bank(f"cum{j}", NT)[:, t0:t0 + n], la0[0:n, i, 128 * j:128 * j + 128], tri[0:n, 0:n],
                                    start=True, stop=True)
                end(ins)
            pe.wait_ge(S("prev_in"), 16)
            turn("prevT", [(BUF * g, prevrow[0:BUF, 128 * g:128 * g + 128], BUF, P) for g in range(4)])
            pe.wait_ge(S("wu_in"), 16)
            for g in range(4):
                project(f"u{g}", w_u[:, :, 128 * g:128 * g + 128], gxT)
            pe.wait_ge(S("kl"), 1)
            for j, tiles in enumerate(((0, 1), (2,))):
                begin(f"klT{j}")
                for m, i in enumerate(tiles):
                    t0, n = TILES[i]
                    for r_ in range(2):
                        ins = pe.transpose(ps[0:n, J.bank(f"klT{j}"), 256 * m + 128 * r_:256 * m + 128 * r_ + 128],
                                           ebl[:, r_, t0:t0 + n], ident[:, :])
                end(ins)
            pe.wait_ge(S("qd"), 4)
            pe.wait_ge(S("kd"), 1)
            for i, (t0, n) in enumerate(TILES):
                begin(f"AT{i}")
                for h in range(4):
                    ins = pe.matmul(ps[0:n, J.bank(f"AT{i}"), n * h:n * h + n], kdT[:, h // 2, t0:t0 + n],
                                    qdz[:, h, t0:t0 + n], start=True, stop=True)
                end(ins)
            pe.wait_ge(S("wg_in"), 16)
            for g in range(4):
                project(f"g{g}", w_g[:, :, 128 * g:128 * g + 128], gxT)
            has(pe, "klT1")
            has(pe, "v2")
            for c_ in range(NCH):
                i, n = c_ // 2, TILES[c_ // 2][1]
                begin(f"ds{c_}")
                for r_ in range(2):
                    ins = pe.matmul(ps[:, J.bank(f"ds{c_}"), 256 * r_:256 * r_ + 256], klz[0:n, c_, 128 * r_:128 * r_ + 128],
                                    vtok[0:n, i, 256 * r_:256 * r_ + 256], start=True, stop=True)
                end(ins)
            pe.wait_ge(S("ks_in"), 16)
            for j in range(4):
                turn(f"KTs{j}", [(256 * kk + 128 * i, Ks[:, i, 128 * (2 * j + kk):128 * (2 * j + kk) + 128], P, P)
                                 for kk in range(2) for i in range(2)])
            pe.wait_ge(S("pool_diff"), 8)
            pe.wait_ge(S("poolw_in"), 16)
            for g in range(4):
                begin(f"pool{g}")
                end(pe.matmul(bank(f"pool{g}", NT), poolw[:, g, :], invn[:, g, :], start=True, stop=True))
            has(pe, "AT2")
            has(pe, "ds4")
            pe.wait_ge(S("state"), 15)
            for i, (t0, n) in enumerate(TILES):
                begin(f"o{i}")
                for h in range(4):
                    c0 = 128 * h
                    ins = pe.matmul(ps[0:n, J.bank(f"o{i}"), c0:c0 + 128], AT[0:n, i, h, 0:n], vtok[0:n, i, c0:c0 + 128],
                                    start=True, stop=False, skip_group_check=True)
                    for c_ in ((0, 1), (2, 3), (4,))[i]:
                        if c_ == 0:
                            continue
                        st = Sbuf[c_ - 1] if c_ < 4 else Sbuf[4]
                        r0 = 64 * (c_ % 2)
                        ins = pe.matmul(ps[r0:r0 + 64, J.bank(f"o{i}"), c0:c0 + 128], qdz[:, h, 64 * c_:64 * c_ + 64],
                                        st[:, h // 2, :], start=False, stop=True, skip_group_check=True)
                end(ins)
            for j, t_end in enumerate((UP_P, UPAD)):
                begin(f"hist{j}")
                for g in range(4):
                    ins = pe.transpose(ps[0:BUF, J.bank(f"hist{j}"), 128 * g:128 * g + 128],
                                       upad[:, g, t_end - BUF:t_end], ident[:, :])
                end(ins)
            pe.wait_ge(S("o_norm"), 3)
            for h in range(4):
                turn(f"oT{h}", [(t0, otok[0:n, i, 128 * h:128 * h + 128], n, P) for i, (t0, n) in enumerate(TILES)])
            has(pe, "oT3")
            for k in range(KT):
                if k % 2 == 0:
                    pe.wait_ge(S(f"wout_in{k // 2}"), 16)
                project(f"out{k}", wsq[:, k // 2, :, 128 * (k % 2):128 * (k % 2) + 128], catT)
            begin("rms1")
            for k in range(KT):
                pe.wait_ge(S("sq1"), k + 1)
                ins = pe.matmul(bank("rms1", NT), ones[:, :], sq1[:, k, :], start=(k == 0), stop=(k == KT - 1))
            end(ins)
            for k in range(KT):
                if k % 2 == 0:
                    pe.wait_ge(S(f"wmq_in{k // 2}"), 16)
                project(f"mq{k}", wsq[:, k // 2, :, 128 * (k % 2):128 * (k % 2) + 128], gxT)
            has(pe, "mq7")
            for j in range(6):
                begin(f"s{j}")
                t0, n = TILES[j // 2]
                KTx = KTp if j < 4 else KTs
                for h2 in range(2):
                    h = 2 * (j % 2) + h2
                    for d_ in range(2):
                        ins = pe.matmul(ps[0:n, J.bank(f"s{j}"), 256 * h2:256 * h2 + 256], aqT[:, 2 * h + d_, t0:t0 + n],
                                        KTx[:, 2 * h + d_, :], start=(d_ == 0), stop=(d_ == 1))
                end(ins)
            pe.wait_ge(S("probs"), 8)
            for h in range(4):
                turn(f"PT{h}", [(256 * i + 128 * l, probs_p[:, l, h, 128 * i:128 * i + 128], P, P)
                                for i in range(2) for l in range(2)])
            pe.wait_ge(S("probs"), 12)
            turn("PT4", [(128 * h + 64 * i, probs_s[0:64, h, 128 * i:128 * i + 128], 64, P)
                         for h in range(4) for i in range(2)])
            for h in range(4):
                begin(f"PV{h}")
                has(pe, f"PT{h}")
                for d_ in range(2):
                    for i in range(2):
                        c0 = 256 * h + 128 * d_
                        ins = pe.matmul(bank(f"PV{h}")[:, 256 * d_:256 * d_ + 256], Vp[:, i, c0:c0 + 128], PTp[:, h, i, :],
                                        start=(i == 0), stop=(i == 1))
                end(ins)
            begin("PV4")
            has(pe, "PT4")
            pe.wait_ge(S("vs_in"), 16)
            for d_ in range(KT):
                for i in range(2):
                    ins = pe.matmul(bank("PV4")[:, 64 * d_:64 * d_ + 64], Vs[:, i, 128 * d_:128 * d_ + 128],
                                    PTs[:, d_ // 2, i, :], start=(i == 0), stop=(i == 1))
            end(ins)
            has(pe, "PV4")
            for k in range(KT):
                if k % 2 == 0:
                    pe.wait_ge(S(f"wmo_in{k // 2}"), 16)
                project(f"mo{k}", wsq[:, k // 2, :, 128 * (k % 2):128 * (k % 2) + 128], aoT)
            has(pe, "mo7")
            pe.wait_ge(S("gwr"), 1)
            begin("router")
            for i, (t0, n) in enumerate(TILES):
                for k in range(KT):
                    ins = pe.matmul(ps[0:n, J.bank("router"), E * i:E * i + E], xT[:, k, t0:t0 + n], gwr[:, k, :],
                                    start=(k == 0), stop=(k == KT - 1))
            end(ins)
            for j in range(6):
                i, n = j // 2, TILES[j // 2][1]
                t0 = TILES[i][0]
                begin(f"x2_{j}")
                for kk in range(4):
                    ins = pe.transpose(ps[0:n, J.bank(f"x2_{j}"), 128 * kk:128 * kk + 128],
                                       xT[:, 4 * (j % 2) + kk, t0:t0 + n], ident[:, :])
                end(ins)
            pe.wait_ge(S("sel"), 12)
            begin("rank")
            for i, (t0, n) in enumerate(TILES):
                for j in range(i + 1):
                    m = TILES[j][1]
                    lhs = below[0:m, 0:n] if j == i else ones[0:m, 0:n]
                    ins = pe.matmul(ps[0:n, J.bank("rank"), E * i:E * i + E], lhs, sel[0:m, j, :], start=(j == 0),
                                    stop=(j == i))
            end(ins)
            pe.wait_ge(S("gates"), 3)
            begin("GT")
            for i, (t0, n) in enumerate(TILES):
                ins = pe.transpose(ps[0:96, J.bank("GT"), t0:t0 + n], gpad[0:n, i, :], ident[0:n, 0:n])
            end(ins)
            moe_tensor(pe)


IN = ["x_prompt", "x_sample", "mem_prompt", "state_gla", "state_pool", "cache_mem_k", "cache_mem_v", "norm_mix",
      "w_in", "w_gate", "b_gate", "gla_gain", "pool_w", "pool_scale", "w_out", "norm_mem_q", "norm_mem_kv", "w_mq",
      "w_mk", "w_mv", "w_mo", "norm_moe", "w_router", "b_router", "w_up", "b_up", "w_down", "b_down", "norm_final"]
OUT = [("y_p", (1, LP, D)), ("y_s", (1, LS, D)), ("gla_p", (1, 1, HEADS, DK, DV)), ("pool_p", (1, 1, BUF, POOL)),
       ("mem_k", (1, 1, NMEM, AH, AHD)), ("mem_v", (1, 1, NMEM, AH, AHD)), ("gla_s", (1, 1, HEADS, DK, DV)),
       ("pool_s", (1, 1, BUF, POOL))]


def kernel(**inputs):
    import numpy as np
    import concourse.bacc as bacc
    from concourse.bass_utils import run_bass_kernel_spmd

    nc = bacc.Bacc("TRN2", target_bir_lowering=False, num_devices=1)
    arrays, a, o = {}, {}, {}
    for name in IN:
        x = np.ascontiguousarray(inputs[name])
        arrays[f"in_{name}"] = x
        a[name] = nc.dram_tensor(f"in_{name}", x.shape, mybir.dt.from_np(x.dtype), kind="ExternalInput").ap()
    for name, shape in OUT:
        o[name] = nc.dram_tensor(f"out_{name}", shape, F32, kind="ExternalOutput").ap()
    build(nc, a, o)
    r = run_bass_kernel_spmd(nc, [arrays], core_ids=[0])
    return tuple(r.results[0][f"out_{name}"] for name, _ in OUT)
```

```python
from contextlib import ExitStack, contextmanager

import concourse.bass as bass
from concourse import mybir

F32 = mybir.dt.float32
I32 = mybir.dt.int32
ALU = mybir.AluOpType
ACT = mybir.ActivationFunctionType
AX = mybir.AxisListType

P = 128
D = 1024
KT = D // P
LP, LS = 256, 64
NT = LP + LS
TILES = [(0, 128), (128, 128), (256, 64)]
HEADS, DK, DV = 4, 64, 128
KW, GW = HEADS * DK, HEADS * DV
RANK = 16
CHUNK = 64
NCH = NT // CHUNK
POOL = 512
BUF = 15
UP_P, UP_S = BUF + LP, BUF + LS
UPAD = UP_P + UP_S
NMEM, AH, AHD = 256, 4, 256
E = 32
DFF = 1024
SLOTS = 64
NBLK = NT // SLOTS
EPS = 1e-6
COL = dict(q=0, k=KW, v=2 * KW, g=2 * KW + GW, r=2 * KW + 2 * GW, u=2 * KW + 2 * GW + RANK)


class Jobs:

    def __init__(self, table):
        self.job, self.order, count = {}, [], {"A": 0, "D": 0}
        for n, (name, last) in enumerate(table):
            count[last] += 1
            self.job[name] = (n, last, count[last])
            self.order.append((last, count[last]))

    def bank(self, name):
        return self.job[name][0] % 8

    def filled_at(self, name):
        return self.job[name][0] + 1

    def freed_at(self, name):
        return self.job[name][1:]

    def occupant_before(self, name):
        n = self.job[name][0]
        return self.order[n - 8] if n >= 8 else None


def job_table():
    t = [("vec", "D")]
    t += [(f"memT{i}", "A") for i in range(4)]
    t += [(f"K{i}", "A") for i in range(4)]
    t += [("bup", "D")]
    t += [(f"xT{i}", "D") for i in range(KT)]
    t += [("rms0", "D")]
    t += [(f"V{i}", "A") for i in range(4)]
    t += [(f"KTp{i}", "A") for i in range(4)]
    t += [("r", "D"), ("q0", "D"), ("q1", "D"), ("gate0", "A"), ("gate1", "A"), ("k0", "D"), ("k1", "D")]
    t += [(f"v{i}", "A") for i in range(3)]
    t += [(f"u{i}", "D") for i in range(4)]
    t += [("cum0", "D"), ("cum1", "D"), ("prevT", "A")]
    t += [(f"g{i}", "D") for i in range(4)]
    t += [("klT0", "A"), ("klT1", "A")]
    t += [(f"AT{i}", "D") for i in range(3)]
    t += [(f"ds{c}", "D") for c in range(NCH)]
    t += [(f"KTs{i}", "A") for i in range(4)]
    t += [(f"o{i}", "D") for i in range(3)]
    t += [(f"pool{i}", "D") for i in range(4)]
    t += [("hist0", "A"), ("hist1", "A")]
    t += [(f"oT{i}", "D") for i in range(4)]
    t += [(f"out{i}", "D") for i in range(KT)]
    t += [(f"mq{i}", "D") for i in range(KT)] + [("rms1", "D")]
    t += [(f"s{i}", "A") for i in range(6)]
    t += [(f"PT{i}", "D") for i in range(5)]
    t += [(f"PV{i}", "A") for i in range(5)]
    t += [(f"mo{i}", "D") for i in range(KT)]
    t += [("router", "D")]
    t += [(f"x2_{i}", "A") for i in range(6)]
    t += [("rank", "D")]
    return t


def build(nc, a, o):
    J = Jobs(job_table())
    with ExitStack() as ctx:
        sems = {}

        def S(name):
            if name not in sems:
                sems[name] = ctx.enter_context(nc.semaphore(name))
            return sems[name]

        ps = ctx.enter_context(nc.psum_tensor("ps", [P, 8, 512], F32))
        nwords = 40960 + 12248
        arena = ctx.enter_context(nc.sbuf_tensor("arena", [P, nwords], F32))

        def reg(at, n):
            assert at + n <= nwords
            return arena[:, at:at + n]

        RA, RB0, RB1, RD, RP = 0, 16384, 24576, 32768, 40960
        upA = reg(RA, 16384).rearrange("p (k f) -> p k f", k=KT)
        upB = reg(RB0, 16384).rearrange("p (k f) -> p k f", k=KT)
        wdn = reg(RD, 8192).rearrange("p (k f) -> p k f", k=KT)
        wlast = reg(RA + 8192, 8192).rearrange("p (k f) -> p k f", k=KT)
        c = RP
        def take(n):
            nonlocal c
            r = reg(c, n); c += n
            return r
        ident, iota = take(128), take(128)
        OH_at = c
        tri, ones, below = take(128), take(128), take(128)
        bupT = take(E * 16).rearrange("p (e f) -> p e f", e=E)
        GT_at = c
        wr = take(KT * E).rearrange("p (k e) -> p k e", k=KT)
        gwr = take(KT * E).rearrange("p (k e) -> p k e", k=KT)
        vec = take(40)
        small = take(152)
        brout = take(E)
        g_mix, g_memq, g_memkv, g_moe = (vec[:, 8 * i:8 * i + 8] for i in range(4))
        g_gla, pscale = vec[:, 32:36], vec[:, 36:40]
        XT_at = c; xT = take(2560).rearrange("p (k t) -> p k t", k=KT)
        GX_at = c; gxT = take(2560).rearrange("p (k t) -> p k t", k=KT)
        CAT_at = c; catT = take(2560).rearrange("p (k t) -> p k t", k=KT)
        SP_at = c
        upad = take(4 * UPAD).rearrange("p (g t) -> p g t", g=4)
        rstdb = take(NT)
        rT = take(NT)
        wgate = take(KW)
        wr_col = take(KT * RANK).rearrange("p (k c) -> p k c", k=KT)
        end_at = c
        assert c <= nwords
        ssx, ssm = small[:, 0:3], small[:, 3:5]
        rsx, rsm = small[:, 5:8], small[:, 8:10]
        sso = small[:, 10:22].rearrange("p (i h) -> p i h", i=3)
        rso = small[:, 22:34].rearrange("p (i h) -> p i h", i=3)
        mx = small[:, 34:46]
        nmx = small[:, 46:58]
        rs = small[:, 58:70]
        rinv = small[:, 70:82]
        ss2, rs2 = small[:, 82:88], small[:, 88:91]
        top8 = small[:, 91:115].rearrange("p (i k) -> p i k", i=3)
        nt1 = small[:, 115:118]
        gsum = small[:, 118:121]
        nover = small[:, 121:122]
        over_i = small[:, 122:123].bitcast(I32)
        sst = small[:, 123:129]
        ms1, rs1, rs1p, rs1n = (small[:, 132 + 3 * i:135 + 3 * i] for i in range(4))
        xtok = reg(RB1, 3072).rearrange("p (i d) -> p i d", i=3)
        mem = reg(RB1 + 3072, 2048).rearrange("p (i d) -> p i d", i=2)
        memT = reg(RB1 + 5120, 2048).rearrange("p (k m) -> p k m", k=KT)
        Vp = reg(RB1, 2048).rearrange("p (i d) -> p i d", i=2)
        Kp = reg(CAT_at, 2048).rearrange("p (i d) -> p i d", i=2)
        KTp = reg(RB1 + 3072, 2048).rearrange("p (k m) -> p k m", k=KT)
        Vs = reg(RB1 + 5120, 2048).rearrange("p (i d) -> p i d", i=2)
        Sbuf = [reg(RB1 + 2048 + 256 * i, 256) for i in range(4)] + [reg(RB1 + 7168 + 256 * i, 256) for i in range(3)]
        Sbuf = [s.rearrange("p (r e) -> p r e", r=2) for s in Sbuf]
        wmk = reg(RB0, 8192).rearrange("p (k f) -> p k f", k=KT)
        wmv = reg(RD, 8192).rearrange("p (k f) -> p k f", k=KT)
        Ks = reg(RB0, 2048).rearrange("p (i d) -> p i d", i=2)
        KTs = reg(RB0 + 2048, 2048).rearrange("p (k m) -> p k m", k=KT)
        sgT = reg(RB0 + 4096, 1280).rearrange("p (g t) -> p g t", g=4)
        vtok = reg(RB0 + 5376, 1536).rearrange("p (i d) -> p i d", i=3)
        qT = reg(RB0 + 6912, 640).rearrange("p (r t) -> p r t", r=2)
        kT = reg(RB0 + 7552, 640).rearrange("p (r t) -> p r t", r=2)
        w_qk = reg(RA, 4096).rearrange("p (k f) -> p k f", k=KT)
        w_v = reg(RA + 4096, 4096).rearrange("p (k f) -> p k f", k=KT)
        w_g = reg(RA + 8192, 4096).rearrange("p (k f) -> p k f", k=KT)
        w_u = reg(RA + 12288, 4096).rearrange("p (k f) -> p k f", k=KT)
        la0 = reg(CAT_at, 768).rearrange("p (i f) -> p i f", i=3)
        la1 = reg(CAT_at + 768, 768).rearrange("p (i f) -> p i f", i=3)
        at = RA
        def takeA(n):
            nonlocal at
            r = reg(at, n); at += n
            return r
        bT = takeA(640).rearrange("p (r t) -> p r t", r=2)
        eb = takeA(640).rearrange("p (r t) -> p r t", r=2)
        enb = takeA(640).rearrange("p (r t) -> p r t", r=2)
        ebl = takeA(640).rearrange("p (r t) -> p r t", r=2)
        kdT = takeA(640).rearrange("p (r t) -> p r t", r=2)
        qdz = takeA(1280).rearrange("p (h t) -> p h t", h=4)
        klz = takeA(1280).rearrange("p (c f) -> p c f", c=5)
        AT = takeA(1536).rearrange("p (i h t) -> p i h t", i=3, h=4)
        assert at <= 8192
        otok = reg(RA + 8192, 1536).rearrange("p (i d) -> p i d", i=3)
        osq = reg(RA + 9728, 1536).rearrange("p (i d) -> p i d", i=3)
        hist = reg(RA + 11264, 1024).rearrange("p (i d) -> p i d", i=2)
        s_a = reg(RA + 12288, 4 * UPAD).rearrange("p (g t) -> p g t", g=4)
        s_b = reg(RA + 12288 + 4 * UPAD, 4 * UPAD).rearrange("p (g t) -> p g t", g=4)
        invn = reg(RA + 12288 + 8 * UPAD, 4 * NT).rearrange("p (g t) -> p g t", g=4)
        poolw = reg(GX_at, 512).rearrange("p (g f) -> p g f", g=4)
        smallrows = reg(RB1 + 7168, 128)
        buprow = reg(GX_at, 2048)
        prevrow = reg(RB1 + 7168 + 256, 512)
        rT_diag = reg(CAT_at + 2048, 384).rearrange("p (i t) -> p i t", i=3)
        sgT_f = reg(RB0 + 4096, 1280)
        sgT_e = reg(RA + 9728, 1280)
        sq1 = reg(SP_at, 2560).rearrange("p (k t) -> p k t", k=KT)
        sq2 = reg(GX_at, 2560).rearrange("p (k t) -> p k t", k=KT)
        aqT = reg(RB0 + 4096, 2560).rearrange("p (k t) -> p k t", k=KT)
        probs_p = reg(RB0, 2048).rearrange("p (l h m) -> p l h m", l=2, h=4)
        probs_s = reg(RB0 + 6656, 1024).rearrange("p (h m) -> p h m", h=4)
        PTs = reg(RB0 + 7680, 512).rearrange("p (h i l) -> p h i l", h=4, i=2)
        PTp = reg(GX_at, 2048).rearrange("p (h i l) -> p h i l", h=4, i=2)
        aoT = catT
        wsq = reg(RD, 8192).rearrange("p (c k f) -> p c k f", c=4, k=KT)
        Hm = reg(GX_at, 3072).rearrange("p (i d) -> p i d", i=3)
        acc = reg(GX_at + 3072, 3072).rearrange("p (i d) -> p i d", i=3)
        x_at = GX_at + 6144
        glu = reg(x_at, 512).rearrange("p (k s) -> p k s", k=KT)
        Y = reg(x_at + 512, 1024)
        U = reg(XT_at, 1024)
        sg = U[:, 0:512].rearrange("p (k s) -> p k s", k=KT)
        lin = reg(XT_at + 1024, 512).rearrange("p (k s) -> p k s", k=KT)
        XG = reg(XT_at + 1536, 512)
        XTe = reg(XT_at + 2048, 512).rearrange("p (q h s) -> p q h s", q=4, h=2)
        OH = reg(OH_at, 384).rearrange("p (i s) -> p i s", i=3)
        GT = reg(GT_at, NT)
        rankx = reg(GT_at + NT, 96).rearrange("p (i e) -> p i e", i=3)
        Gm = reg(GT_at + NT + 96, 96).rearrange("p (i e) -> p i e", i=3)
        gate_col = small[:, 130:131]
        logit = reg(x_at, 96).rearrange("p (i e) -> p i e", i=3)
        sel = reg(x_at + 96, 96).rearrange("p (i e) -> p i e", i=3)
        gpad = reg(x_at + 192, 288).rearrange("p (i e) -> p i e", i=3)
        work = reg(x_at + 512, 96).rearrange("p (i e) -> p i e", i=3)
        topi = reg(x_at + 608, 24).bitcast(mybir.dt.uint32).rearrange("p (i k) -> p i k", i=3)
        topf = reg(x_at + 640, 24).rearrange("p (i k) -> p i k", i=3)
        wide = reg(x_at + 512, 1024)
        bdrow = acc[64:96, 2, :]
        nfinal = reg(RA, D)
        wide2 = reg(RA + D, D)
        GtT = Y[64:96, 0:NT]
        assert x_at + 1536 <= nwords

        filled, freed = S("bank_filled"), {"A": S("bank_read_by_act"), "D": S("bank_read_by_dve")}

        def took(eng, name):
            eng.wait_ge(filled, J.filled_at(name))

        def has(eng, name):
            last, n = J.freed_at(name)
            eng.wait_ge(freed[last], n)

        def bank(name, n=512, rows=P):
            return ps[0:rows, J.bank(name), 0:n]

        PAIRS = E // 2

        def up_src(e):
            src = a["w_up"][0]
            src = src[bass.ds(e, 1)] if not isinstance(e, int) else src[e:e + 1]
            return src.rearrange("a (k p) f -> p (a k) f", p=P)

        def down_src(e):
            src = a["w_down"][0]
            src = src[bass.ds(e, 1)] if not isinstance(e, int) else src[e:e + 1]
            return src.rearrange("a (k p) f -> p (a k) f", p=P)

        def over_experts(eng, one):
            one(0, 0, 0, True, False)
            one(1, 1, 0, False, False)
            with eng.Fori(1, PAIRS - 1) as i:
                for h in range(2):
                    one(i * 2 + h, h, i, False, False)
            one(E - 2, 0, PAIRS - 1, False, False)
            one(E - 1, 1, PAIRS - 1, False, True)

        @contextmanager
        def overflowing(eng):
            eng.wait_ge(S("overflow"), 1)
            with eng.If(eng.value_load(over_i[0:1, 0:1], min_val=0, max_val=1) > 0):
                yield

        def block_counts(e, b):
            n = b - 1
            return E + e * (NBLK - 1) + n, n % 2, PAIRS + e * ((NBLK - 1) // 2) + n // 2

        def moe_sync(sp):
            def one(e, h, pair, first, last):
                if isinstance(e, int) and e + 2 >= E:
                    return
                for c_ in range(4):
                    sp.wait_ge(S("up_done"), e * 4 + c_ + 1)
                    sp.dma_start((upA, upB)[h][:, 2 * c_:2 * c_ + 2, :], up_src(e + 2)[:, 2 * c_:2 * c_ + 2, :]
                                 ).then_inc(S(f"up{'AB'[h]}_in{c_}"), 16)
            over_experts(sp, one)
            sp.wait_ge(S("up_done"), (E - 1) * 4)
            for c_ in range(2):
                sp.dma_start(wlast[:, 4 * c_:4 * c_ + 4, :], down_src(E - 1)[:, 4 * c_:4 * c_ + 4, :]
                             ).then_inc(S(f"last_down_in{c_}"), 16)
            with overflowing(sp):
                sp.wait_ge(S("down_done"), E * 2)
                with sp.Fori(0, E) as e:
                    for c_ in range(4):
                        sp.wait_ge(S("up_done"), (E + e * (NBLK - 1)) * 4)
                        sp.dma_start(upA[:, 2 * c_:2 * c_ + 2, :], up_src(e)[:, 2 * c_:2 * c_ + 2, :]
                                     ).then_inc(S(f"upA_in{c_}"), 16)
                    sp.wait_ge(S("down_done"), (E + e * (NBLK - 1)) * 2)
                    for c_ in range(2):
                        sp.dma_start(wdn[:, 4 * c_:4 * c_ + 4, :], down_src(e)[:, 4 * c_:4 * c_ + 4, :]
                                     ).then_inc(S(f"down_in{c_}"), 16)
                sp.wait_ge(S("up_done"), E * NBLK * 4)
            sp.dma_start(nfinal, a["norm_final"].rearrange("(a d) -> a d", a=1).broadcast_to([P, D])).then_inc(S("nf_in"), 16)
            for i, (t0, n) in enumerate(TILES):
                sp.wait_ge(S("y"), i + 1)
                dst = o["y_p"][0, t0:t0 + n, :] if i < 2 else o["y_s"][0]
                sp.dma_start(dst, acc[0:n, i, :]).then_inc(S("y_out"), 16)
            sp.wait_ge(S("y_out"), 48)
            sp.wait_ge(S("k_out"), 16)
            sp.wait_ge(S("v_out"), 16)
            sp.wait_ge(S("states_out"), 32)
            sp.wait_ge(S("hist_out"), 32)

        def gather(pe, at_bank, h):
            for i in range(3):
                for hd in range(2):
                    ins = pe.matmul(ps[64 * hd:64 * hd + 64, at_bank, :], OH[:, i, SLOTS * h:SLOTS * h + SLOTS],
                                    Hm[:, i, 512 * hd:512 * hd + 512], start=(i == 0), stop=(i == 2))
            return ins

        def gather_turn(pe, at_bank):
            for q in range(4):
                ins = pe.transpose(ps[:, at_bank, 128 * q:128 * q + 128], XG[:, 128 * q:128 * q + 128], ident[:, :])
            return ins

        def slots_turn(pe, at_bank, e, ne):
            for i, (t0, n) in enumerate(TILES):
                pe.transpose(ps[:, at_bank, t0:t0 + n], OH[0:n, i, :], ident[0:n, 0:n])
            for i in range(3):
                g = Gm[:, i, e:e + ne] if isinstance(e, int) else Gm[:, i, bass.ds(e, ne)]
                ins = pe.matmul(ps[:, at_bank, NT:NT + ne], OH[:, i, :], g, start=(i == 0), stop=(i == 2))
            return ins

        def up_product(pe, w, k0, nk):
            for k in range(k0, k0 + nk):
                for n_ in range(2):
                    for half in range(2):
                        ins = pe.matmul(ps[64 * half:64 * half + 64, n_, :], XTe[:, k % 4, k // 4, :],
                                        w[:, k, 1024 * half + 512 * n_:1024 * half + 512 * n_ + 512],
                                        start=(k == 0), stop=(k == KT - 1))
            return ins

        def up_turn(pe, f0, nf):
            for f in range(f0, f0 + nf):
                ins = pe.transpose(ps[:, 2 + f // 4, 128 * (f % 4):128 * (f % 4) + 128], U[:, 128 * f:128 * f + 128],
                                   ident[:, :])
            return ins

        def down_product(pe, w, k0, nk):
            for k in range(k0, k0 + nk):
                for n_ in range(2):
                    ins = pe.matmul(ps[64 * n_:64 * n_ + 64, 6, :], lin[:, k, :],
                                    w[:, k, 512 * n_:512 * n_ + 512], start=(k == 0), stop=(k == KT - 1))
            return ins

        def combine(pe, i, at_bank=4):
            t0, n = TILES[i]
            for n_ in range(2):
                ins = pe.matmul(ps[0:n, at_bank + n_, :], GT[:, t0:t0 + n], Y[:, 512 * n_:512 * n_ + 512],
                                start=True, stop=True)
            return ins

        def down_bias(pe, i):
            t0, n = TILES[i]
            for n_ in range(2):
                ins = pe.matmul(ps[0:n, 4 + n_, :], GtT[:, t0:t0 + n], bdrow[:, 512 * n_:512 * n_ + 512],
                                start=True, stop=True)
            return ins

        def moe_tensor(pe):
            has(pe, "x2_5"), has(pe, "rank")
            pe.wait_ge(S("slots"), 1)
            pe.wait_ge(S("Hm"), 3)
            pe.wait_ge(S("moe_zero"), 2)
            gather(pe, 6, 0).then_inc(S("gathered"), 1)
            pe.wait_ge(S("gather_read"), 1)
            gather_turn(pe, 7).then_inc(S("gather_turned"), 1)

            def down(e, last):
                pe.wait_ge(S("act"), e + 1)
                for c_ in range(2):
                    if last:
                        pe.wait_ge(S(f"last_down_in{c_}"), 16)
                    else:
                        pe.wait_ge(S(f"down_in{c_}"), (e + 1) * 16)
                    down_product(pe, wlast if last else wdn, 4 * c_, 4).then_inc(S("down_done"), 1)

            def one(e, h, pair, first, last):
                second = isinstance(e, int) and e == 1
                rows = down_bias if second else combine if h == 0 and not first else None
                pe.wait_ge(S("tokens_in"), e + 1)
                if h == 1:
                    if second:
                        pe.wait_ge(S("Gm"), 3)
                    slots_turn(pe, 7, e - 1, 2).then_inc(S("slots_turned"), 1)
                if not first:
                    pe.wait_ge(S("up_read"), e)
                for c_ in range(4):
                    pe.wait_ge(S(f"up{'AB'[h]}_in{c_}"), (pair + 1) * 16)
                    up_product(pe, (upA, upB)[h], 2 * c_, 2).then_inc(S("up_done"), 1)
                if first:
                    pe.wait_ge(S("gates"), 3)
                    for i, (t0, n) in enumerate(TILES):
                        ins = pe.transpose(ps[0:96, 4, t0:t0 + n], gpad[0:n, i, :], ident[0:n, 0:n])
                    ins.then_inc(S("gates_turned"), 1)
                else:
                    down(e - 1, False)
                    pe.wait_ge(S("act"), e)
                pe.wait_ge(S("up_read"), e + 1)
                up_turn(pe, 0, KT).then_inc(S("up_turned"), 1)
                if second:
                    pe.wait_ge(S("GtT"), 1)
                    pe.wait_ge(S("bdown_in"), 16)
                if not first:
                    pe.wait_ge(S("y_read"), e)
                if rows:
                    if not second:
                        pe.wait_ge(S("combined"), pair * 3)
                    rows(pe, 0).then_inc(S("combine"), 1)
                count = 0 if second else pair * 3
                if not last:
                    if h == 1:
                        pe.wait_ge(S("slots"), pair + 2)
                    gather(pe, 6, 1 - h).then_inc(S("gathered"), 1)
                if rows:
                    pe.wait_ge(S("combined"), count + 1)
                    rows(pe, 1).then_inc(S("combine"), 1)
                if not last:
                    pe.wait_ge(S("gather_read"), e + 2)
                    if h == 1:
                        pe.wait_ge(S("slots_read"), pair + 1)
                    gather_turn(pe, 7).then_inc(S("gather_turned"), 1)
                if rows:
                    pe.wait_ge(S("combined"), count + 2)
                    rows(pe, 2).then_inc(S("combine"), 1)
            over_experts(pe, one)
            down(E - 1, True)
            pe.wait_ge(S("y_read"), E)
            pe.wait_ge(S("combined"), PAIRS * 3)
            for i in range(3):
                combine(pe, i, 4 - 2 * i).then_inc(S("combine"), 1)
            with overflowing(pe), pe.Fori(0, E) as e:
                for b in range(1, NBLK):
                    n, h, pair = block_counts(e, b)
                    if h == 0:
                        pe.wait_ge(S("slots"), pair + 1)
                        slots_turn(pe, 7, e, 1).then_inc(S("slots_turned"), 1)
                        pe.wait_ge(S("slots_read"), pair + 1)
                    gather(pe, 6, h).then_inc(S("gathered"), 1)
                    pe.wait_ge(S("gather_read"), n + 1)
                    gather_turn(pe, 7).then_inc(S("gather_turned"), 1)
                    pe.wait_ge(S("tokens_in"), n + 1)
                    pe.wait_ge(S("combined"), pair * 3 + 3)
                    for c_ in range(4):
                        if b == 1:
                            pe.wait_ge(S(f"upA_in{c_}"), (PAIRS + 1 + e) * 16)
                        up_product(pe, upA, 2 * c_, 2).then_inc(S("up_done"), 1)
                    pe.wait_ge(S("up_read"), n + 1)
                    up_turn(pe, 0, KT).then_inc(S("up_turned"), 1)
                    pe.wait_ge(S("act"), n + 1)
                    for c_ in range(2):
                        if b == 1:
                            pe.wait_ge(S(f"down_in{c_}"), (E + e) * 16)
                        down_product(pe, wdn, 4 * c_, 4).then_inc(S("down_done"), 1)
                    pe.wait_ge(S("y_read"), n + 1)
                    if h == 1:
                        for i in range(3):
                            combine(pe, i, 4 - 2 * i).then_inc(S("combine"), 1)

        def moe_act(act):
            def slots_read(pair, upper):
                for half in range(2):
                    col = NT + (upper if half else 0)
                    act.activation(gate_col[64 * half:64 * half + 64, :], ps[64 * half:64 * half + 64, 7, col:col + 1],
                                   ACT.Copy).then_inc(S("gate_col"), 1)
                act.wait_ge(S("gate_col"), pair * 2 + 2)
                act.activation(GT[:, :], ps[:, 7, 0:NT], ACT.Copy, scale=gate_col).then_inc(S("slots_read"), 1)

            def rows_read(h):
                for n_ in range(2):
                    ins = act.activation(Y[64 * h:64 * h + 64, 512 * n_:512 * n_ + 512], ps[64 * n_:64 * n_ + 64, 6, :],
                                         ACT.Copy)
                ins.then_inc(S("y_read"), 1)

            act.wait_ge(S("gathered"), 1)
            act.activation(XG[:, :], ps[:, 6, :], ACT.Copy).then_inc(S("gather_read"), 1)

            def one(e, h, pair, first, last):
                if h == 1:
                    act.wait_ge(S("slots_turned"), pair + 1)
                    if not isinstance(e, int) or e > 1:
                        act.wait_ge(S("combine"), pair * 3 + 3)
                    slots_read(pair, 1)
                if not first:
                    act.wait_ge(S("act"), e)
                act.wait_ge(S("up_done"), (e + 1) * 4)
                act.activation(U[:, :], ps[:, 0:2, :].rearrange("p b f -> p (b f)"), ACT.Copy).then_inc(S("up_read"), 1)
                if first:
                    act.wait_ge(S("gates_turned"), 1)
                    act.activation(GtT, ps[64:96, 4, 0:NT], ACT.Copy).then_inc(S("GtT"), 1)
                else:
                    def load_down(c_):
                        act.dma_start(wdn[:, 4 * c_:4 * c_ + 4, :], down_src(e)[:, 4 * c_:4 * c_ + 4, :]
                                      ).then_inc(S(f"down_in{c_}"), 16)
                    if not last:
                        act.wait_ge(S("down_done"), e * 2 - 1)
                        load_down(0)
                    act.wait_ge(S("down_done"), e * 2)
                    if isinstance(e, int) and e == 2:
                        act.wait_ge(S("combine"), 3)
                    rows_read(1 - h)
                    if not last:
                        load_down(1)
                if not last:
                    act.wait_ge(S("gathered"), e + 2)
                    act.activation(XG[:, :], ps[:, 6, :], ACT.Copy).then_inc(S("gather_read"), 1)
                act.wait_ge(S("glu"), e * 2 + 2)
                act.activation(sg, glu, ACT.Sigmoid, scale=1.702).then_inc(S("sigmoid"), 1)
            over_experts(act, one)
            act.wait_ge(S("down_done"), E * 2)
            rows_read(1)
            with overflowing(act), act.Fori(0, E) as e:
                for b in range(1, NBLK):
                    n, h, pair = block_counts(e, b)
                    if h == 0:
                        act.wait_ge(S("slots_turned"), pair + 1)
                        slots_read(pair, 0)
                    act.wait_ge(S("gathered"), n + 1)
                    act.activation(XG[:, :], ps[:, 6, :], ACT.Copy).then_inc(S("gather_read"), 1)
                    act.wait_ge(S("up_done"), (n + 1) * 4)
                    act.activation(U[:, :], ps[:, 0:2, :].rearrange("p b f -> p (b f)"), ACT.Copy).then_inc(S("up_read"), 1)
                    act.wait_ge(S("glu"), n * 2 + 2)
                    act.activation(sg, glu, ACT.Sigmoid, scale=1.702).then_inc(S("sigmoid"), 1)
                    act.wait_ge(S("down_done"), (n + 1) * 2)
                    rows_read(h)
                    if h == 1:
                        act.wait_ge(S("combined"), pair * 3 + 6)
            for i, (t0, n) in enumerate(TILES):
                act.wait_ge(S("combined"), PAIRS * 3 + i + 1)
                act.activation(wide2[0:n, :], acc[0:n, i, :], ACT.Square, accum_out=ss2[0:n, 3 + i:4 + i]).then_inc(S("ssq3"), 1)
                act.wait_ge(S("meansq3"), i + 1)
                act.activation(rs2[0:n, i:i + 1], rs2[0:n, i:i + 1], ACT.Sqrt).then_inc(S("root3"), 1)

        def moe_dve(dve):
            def slots(halves):
                for h, (e, block) in enumerate(halves):
                    for i in range(3):
                        r = rankx[:, i, e:e + 1] if isinstance(e, int) else rankx[:, i, bass.ds(e, 1)]
                        ins = dve.tensor_scalar(OH[:, i, SLOTS * h:SLOTS * h + SLOTS], iota[:, 0:SLOTS],
                                                float(SLOTS * block), r, ALU.add, ALU.is_equal)
                ins.then_inc(S("slots"), 1)

            def swiglu(e, n, down_done):
                u = ps[:, 2:4, :].rearrange("p b (k s) -> p (b k) s", s=P)
                be = bupT[:, e, :] if isinstance(e, int) else bupT[:, bass.ds(e, 1), :].rearrange("p e f -> p (e f)")
                dve.tensor_tensor(glu, u[:, :, 0:SLOTS], be[:, 0:8].unsqueeze(2).broadcast_to([P, KT, SLOTS]),
                                  ALU.add).then_inc(S("glu"), 1)
                if down_done is not None:
                    dve.wait_ge(S("down_done"), down_done * 2)
                dve.tensor_tensor(lin, u[:, :, SLOTS:P], be[:, 8:16].unsqueeze(2).broadcast_to([P, KT, SLOTS]),
                                  ALU.add).then_inc(S("lin"), 1)
                dve.wait_ge(S("glu"), n * 2 + 1)
                dve.tensor_scalar(glu, glu, 7.0, None, ALU.min).then_inc(S("glu"), 1)
                dve.wait_ge(S("lin"), n * 3 + 1)
                dve.tensor_scalar(lin, lin, 7.0, -7.0, ALU.min, ALU.max).then_inc(S("lin"), 1)
                dve.wait_ge(S("glu"), n * 2 + 2)
                dve.wait_ge(S("lin"), n * 3 + 2)
                dve.scalar_tensor_tensor(lin, lin, 1.0, glu, ALU.add, ALU.mult).then_inc(S("lin"), 1)

            def swiglu_end(n):
                dve.wait_ge(S("lin"), n * 3 + 3)
                dve.wait_ge(S("sigmoid"), n + 1)
                dve.tensor_tensor(lin, lin, sg, ALU.mult).then_inc(S("act"), 1)

            def tokens():
                g = g_moe.rearrange("p (h q) -> p q h", h=2).unsqueeze(3).broadcast_to([P, 4, 2, SLOTS])
                return dve.tensor_tensor(XTe, ps[:, 7, :].rearrange("p (q h s) -> p q h s", q=4, h=2), g, ALU.mult)

            dve.wait_ge(S("rankx"), 3)
            slots([(0, 0), (1, 0)])
            dve.tensor_reduce(nover, rankx.rearrange("p i e -> p (i e)"), AX.X, ALU.max).then_inc(S("rank_max"), 1)
            dve.wait_ge(S("gather_turned"), 1)
            tokens().then_inc(S("tokens_in"), 1)
            dve.wait_ge(S("gate_e"), 3)
            for i, (t0, n) in enumerate(TILES):
                dve.tensor_tensor(gpad[0:n, i, 64:96], gpad[0:n, i, 64:96], sel[0:n, i, :], ALU.mult).then_inc(S("gsel"), 1)
            dve.wait_ge(S("gsel"), 3)
            dve.tensor_reduce(gsum[:, :], gpad[:, :, 64:96], AX.X, ALU.add).then_inc(S("gsel"), 1)
            dve.wait_ge(S("gsel"), 4)
            dve.reciprocal(gsum[:, 0:2], gsum[:, 0:2]).then_inc(S("gsel"), 1)
            dve.reciprocal(gsum[0:64, 2:3], gsum[0:64, 2:3]).then_inc(S("gsel"), 1)
            dve.wait_ge(S("gsel"), 6)
            for i, (t0, n) in enumerate(TILES):
                dve.tensor_scalar(gpad[0:n, i, 64:96], gpad[0:n, i, 64:96], gsum[0:n, i:i + 1], None,
                                  ALU.mult).then_inc(S("gates"), 1)
            dve.wait_ge(S("gates"), 3)
            for i, (t0, n) in enumerate(TILES):
                dve.tensor_copy(Gm[0:n, i, :], gpad[0:n, i, 64:96]).then_inc(S("Gm"), 1)
            dve.wait_ge(S("nover"), 1)
            dve.tensor_scalar(over_i, small[:, 131:132], float(SLOTS) - 0.5, None, ALU.is_gt).then_inc(S("overflow"), 1)

            def one(e, h, pair, first, last):
                second = isinstance(e, int) and e == 1
                rows = second or (h == 0 and not first)
                if h == 1 and not last:
                    dve.wait_ge(S("slots_turned"), pair + 1)
                    dve.wait_ge(S("gathered"), e + 1)
                    slots([(e + 1, 0), (e + 2, 0)])
                def combined(i):
                    dve.wait_ge(S("combine"), (0 if second else pair * 3) + i + 1)
                    n = TILES[i][1]
                    dve.tensor_tensor(acc[0:n, i, :], ps[0:n, 4:6, :].rearrange("p b f -> p (b f)"), acc[0:n, i, :],
                                      ALU.add).then_inc(S("combined"), 1)
                if first:
                    dve.wait_ge(S("Gm"), 3)
                    dve.wait_ge(S("gates_turned"), 1)
                dve.wait_ge(S("up_turned"), e + 1)
                swiglu(e, e, None if first else e)
                if rows:
                    combined(0)
                    combined(1)
                if not last:
                    dve.wait_ge(S("gather_turned"), e + 2)
                    dve.wait_ge(S("up_done"), (e + 1) * 4)
                    tokens().then_inc(S("tokens_in"), 1)
                swiglu_end(e)
                if rows:
                    combined(2)
            over_experts(dve, one)
            for i, (t0, n) in enumerate(TILES):
                dve.wait_ge(S("combine"), PAIRS * 3 + i + 1)
                dve.tensor_tensor(acc[0:n, i, :], ps[0:n, 4 - 2 * i:6 - 2 * i, :].rearrange("p b f -> p (b f)"), acc[0:n, i, :],
                                  ALU.add).then_inc(S("combined"), 1)
            with overflowing(dve), dve.Fori(0, E) as e:
                for b in range(1, NBLK):
                    n, h, pair = block_counts(e, b)
                    if h == 0:
                        slots([(e, b), (e, b + 1)])
                    dve.wait_ge(S("gather_turned"), n + 1)
                    tokens().then_inc(S("tokens_in"), 1)
                    dve.wait_ge(S("up_turned"), n + 1)
                    swiglu(e, n, None)
                    swiglu_end(n)
                    if h == 1:
                        for i, (t0, rows) in enumerate(TILES):
                            dve.wait_ge(S("combine"), pair * 3 + 3 + i + 1)
                            dve.tensor_tensor(acc[0:rows, i, :], ps[0:rows, 4 - 2 * i:6 - 2 * i, :].rearrange("p b f -> p (b f)"),
                                              acc[0:rows, i, :], ALU.add).then_inc(S("combined"), 1)
                        dve.wait_ge(S("combined"), pair * 3 + 6)
            for i, (t0, n) in enumerate(TILES):
                dve.wait_ge(S("ssq3"), i + 1)
                dve.tensor_scalar(rs2[0:n, i:i + 1], ss2[0:n, 3 + i:4 + i], 1.0 / D, EPS, ALU.mult, ALU.add).then_inc(S("meansq3"), 1)
                dve.wait_ge(S("root3"), i + 1)
                dve.reciprocal(rs2[0:n, i:i + 1], rs2[0:n, i:i + 1]).then_inc(S("rstd3"), 1)
                dve.wait_ge(S("rstd3"), i + 1)
                dve.wait_ge(S("nf_in"), 16)
                dve.scalar_tensor_tensor(acc[0:n, i, :], acc[0:n, i, :], rs2[0:n, i:i + 1], nfinal[0:n, :],
                                         ALU.mult, ALU.mult).then_inc(S("y"), 1)

        block = ctx.enter_context(nc.Block())

        @block.sync
        def _(sp):
            def load(dst, src, name):
                sp.dma_start(dst, src).then_inc(S(name), 16)

            win = a["w_in"][0].rearrange("(k p) f -> p k f", p=P)

            def wcols(w, c0, n):
                return w[0].rearrange("(k p) f -> p k f", p=P)[:, :, c0:c0 + n]

            def wrows(w, k0, n):
                return w[0].rearrange("(k p) f -> p k f", p=P)[:, k0:k0 + n, :]

            load(mem[:, :, :], a["mem_prompt"][0].rearrange("(i p) d -> p i d", p=P), "mem_in")
            sp.wait_ge(S("vec_in"), 96)
            for i in range(4):
                load(wmk[:, 2 * i:2 * i + 2, :], wrows(a["w_mk"], 2 * i, 2), f"wmk_in{i}")
            load(xtok[:, 0:2, :], a["x_prompt"][0].rearrange("(i p) d -> p i d", p=P), "x_in")
            load(xtok[0:LS, 2, :], a["x_sample"][0], "xs_in")
            for i in range(4):
                load(wmv[:, 2 * i:2 * i + 2, :], wrows(a["w_mv"], 2 * i, 2), f"wmv_in{i}")
            load(w_qk, win[:, :, 0:2 * KW], "wqk_in")
            load(w_v, win[:, :, COL["v"]:COL["v"] + GW], "wv_in")
            load(w_u, win[:, :, COL["u"]:COL["u"] + POOL], "wu_in")
            load(w_g, win[:, :, COL["g"]:COL["g"] + GW], "wg_in")
            has(sp, "K3")
            load(Ks[:, :, :], a["cache_mem_k"][0, 0].rearrange("(i p) h d -> p i (h d)", p=P), "ks_in")
            has(sp, "V3")
            load(Vs[:, :, :], a["cache_mem_v"][0, 0].rearrange("(i p) h d -> p i (h d)", p=P), "vs_in")
            for i in range(4):
                load(wsq[:, i], wcols(a["w_out"], 256 * i, 256), f"wout_in{i}")
            has(sp, "g3")
            load(poolw, a["pool_w"][0].rearrange("g c d -> c g d"), "poolw_in")
            has(sp, "oT3")
            sp.wait_ge(S("hist_out"), 32)
            for i in range(4):
                load(upA[:, 2 * i:2 * i + 2, :], a["w_up"][0, 0].rearrange("(k p) f -> p k f", p=P)[:, 2 * i:2 * i + 2, :], f"upA_in{i}")
            for i in range(4):
                has(sp, f"out{2 * i + 1}")
                load(wsq[:, i], wcols(a["w_mq"], 256 * i, 256), f"wmq_in{i}")
            for i in range(4):
                has(sp, f"mq{2 * i + 1}")
                load(wsq[:, i], wcols(a["w_mo"], 256 * i, 256), f"wmo_in{i}")
            has(sp, "PV4")
            sp.wait_ge(S("v_out"), 16)
            sp.wait_ge(S("states_out"), 32)
            for i in range(4):
                load(upB[:, 2 * i:2 * i + 2, :], a["w_up"][0, 1].rearrange("(k p) f -> p k f", p=P)[:, 2 * i:2 * i + 2, :], f"upB_in{i}")
            has(sp, "mo7")
            for i in range(2):
                load(wdn[:, 4 * i:4 * i + 4, :], a["w_down"][0, 0].rearrange("(k p) f -> p k f", p=P)[:, 4 * i:4 * i + 4, :], f"down_in{i}")
            moe_sync(sp)

        @block.gpsimd
        def _(pool):
            pool.memset(ident[:, :], 0.0).then_inc(S("const0"), 1)
            pool.memset(tri[:, :], 1.0 / 16.0).then_inc(S("const0"), 1)
            pool.memset(ones[:, :], 1.0).then_inc(S("const0"), 1)
            pool.memset(below[:, :], 1.0).then_inc(S("const0"), 1)
            pool.memset(small[:, :], 1.0).then_inc(S("const0"), 1)
            pool.wait_ge(S("const0"), 1)
            pool.affine_select(out=ident[:, :], in_=ident[:, :], compare_op=ALU.not_equal, fill=1.0, base=0,
                               pattern=[[-1, P]], channel_multiplier=1).then_inc(S("const1"), 1)
            pool.wait_ge(S("const0"), 5)
            pool.dma_start(buprow[0:E, :], a["b_up"][0]).then_inc(S("bup_in"), 16)
            pool.dma_start(wr_col, a["w_in"][0].rearrange("(k p) f -> p k f", p=P)[:, :, COL["r"]:COL["r"] + RANK]).then_inc(S("wr_in"), 16)
            pool.dma_start(wgate[0:RANK, :], a["w_gate"][0]).then_inc(S("wgate_in"), 16)
            pool.dma_start(wgate[RANK:RANK + 1, :], a["b_gate"]).then_inc(S("wgate_in"), 16)
            pool.affine_select(out=tri[:, :], in_=tri[:, :], compare_op=ALU.is_ge, fill=0.0, base=0,
                               pattern=[[1, P]], channel_multiplier=-1).then_inc(S("const2"), 1)
            pool.wait_ge(S("const2"), 1)
            pool.memset(tri[0:CHUNK, CHUNK:P], 0.0).then_inc(S("const2"), 1)
            pool.affine_select(out=below[:, :], in_=below[:, :], compare_op=ALU.is_gt, fill=0.0, base=0,
                               pattern=[[1, P]], channel_multiplier=-1).then_inc(S("const2"), 1)
            pool.iota(iota[:, :].bitcast(I32), [[0, 2], [1, SLOTS]], 0, 0).then_inc(S("const2"), 1)
            pool.memset(rT[0:32, :], 1.0).then_inc(S("rT_ones"), 1)
            pool.memset(upad[:, :, 0:BUF], 0.0).then_inc(S("upad_zero"), 1)
            pool.dma_start(wr, a["w_router"][0].rearrange("(k p) e -> p k e", p=P)).then_inc(S("router_in"), 16)
            pool.dma_start(brout, a["b_router"].broadcast_to([P, E])).then_inc(S("router_in"), 16)
            has(pool, "vec")
            pool.dma_start(prevrow[0:BUF, :], a["state_pool"][0, 0]).then_inc(S("prev_in"), 16)
            has(pool, "K3")
            pool.dma_start(o["mem_k"][0, 0].rearrange("(i p) h d -> p i (h d)", p=P), Kp[:, :, :]).then_inc(S("k_out"), 16)
            has(pool, "V3")
            pool.dma_start(o["mem_v"][0, 0].rearrange("(i p) h d -> p i (h d)", p=P), Vp[:, :, :]).then_inc(S("v_out"), 16)
            pool.dma_start(Sbuf[4], a["state_gla"][0, 0].rearrange("(r h) d e -> (h d) r e", r=2)).then_inc(S("s0_in"), 16)
            has(pool, "v2")
            for z in (qdz, klz, AT):
                pool.memset(z, 0.0).then_inc(S("gla_zero"), 1)
            has(pool, "u3")
            for g in range(4):
                w = 2 << g
                pool.memset(invn[:, g, :], 1.0 / w).then_inc(S("invn"), 1)
            pool.wait_ge(S("invn"), 4)
            n = 4
            for g in range(4):
                for t in range((2 << g) - 1):
                    pool.memset(invn[:, g, t:t + 1], 1.0 / (t + 1)).then_inc(S("invn"), 1)
                    n += 1
            has(pool, "prevT")
            src, steps = upad, 0
            for j in range(4):
                dst = (s_a, s_b)[j % 2]
                if j:
                    pool.wait_ge(S("window"), steps)
                off = 1 << j
                pool.tensor_tensor(dst[:, j:4, off:UPAD], src[:, j:4, off:UPAD], src[:, j:4, 0:UPAD - off],
                                   ALU.add).then_inc(S("window"), 1)
                steps += 1
                if j == 0:
                    pool.tensor_copy(dst[:, :, 0:off], src[:, :, 0:off]).then_inc(S("window"), 1)
                    steps += 1
                elif j < 3:
                    pool.tensor_copy(dst[:, j:4, 0:off], src[:, j:4, 0:off]).then_inc(S("window"), 1)
                    steps += 1
                src = dst
            pool.wait_ge(S("invn"), n)
            pool.wait_ge(S("window"), steps)
            k = 0
            for g in range(4):
                sg_ = (s_a, s_b)[g % 2]
                for t0, n0, u0 in ((0, LP, BUF), (LP, LS, UP_P + BUF)):
                    pool.tensor_tensor(sg_[:, g, u0:u0 + n0], sg_[:, g, u0:u0 + n0], invn[:, g, t0:t0 + n0],
                                       ALU.mult).then_inc(S("mean"), 1)
                    k += 1
                    pool.wait_ge(S("mean"), k)
                    pool.tensor_tensor(invn[:, g, t0:t0 + n0], sg_[:, g, u0:u0 + n0], upad[:, g, u0:u0 + n0],
                                       ALU.subtract).then_inc(S("pool_diff"), 1)
            has(pool, "ds4")
            pool.wait_ge(S("state"), 15)
            pool.dma_start(o["gla_p"][0, 0].rearrange("(r h) d e -> (h d) r e", r=2), Sbuf[3]).then_inc(S("states_out"), 16)
            pool.dma_start(o["gla_s"][0, 0].rearrange("(r h) d e -> (h d) r e", r=2), Sbuf[5]).then_inc(S("states_out"), 16)
            has(pool, "hist1")
            for i, name in enumerate(("pool_p", "pool_s")):
                pool.dma_start(o[name][0, 0], hist[0:BUF, i, :]).then_inc(S("hist_out"), 16)
            has(pool, "router")
            pool.wait_ge(S("states_out"), 32)
            pool.wait_ge(S("k_out"), 16)
            pool.memset(Hm[64:P, 2, :], 0.0).then_inc(S("moe_zero"), 1)
            pool.wait_ge(S("moe_zero"), 1)
            pool.memset(gpad[:, :, :], 0.0).then_inc(S("moe_zero"), 1)
            pool.dma_start(bdrow, a["b_down"][0]).then_inc(S("bdown_in"), 16)
            pool.wait_ge(S("rank_max"), 1)
            pool.partition_all_reduce(small[:, 131:132], nover, P, bass.bass_isa.ReduceOp.max).then_inc(S("nover"), 1)

        @block.scalar
        def _(act):
            def copy(dst, src, name=None, scale=1.0):
                i = act.activation(dst, src, ACT.Copy, scale=scale)
                return i

            def free(ins, name):
                assert J.freed_at(name) == ("A", free.n + 1), name
                free.n += 1
                ins.then_inc(freed["A"], 1)
            free.n = 0
            r = 0
            for name, n in (("norm_mix", 8), ("norm_mem_q", 8), ("norm_mem_kv", 8), ("norm_moe", 8),
                            ("gla_gain", 4), ("pool_scale", 4)):
                act.dma_start(smallrows[r:r + n, :], a[name][0].rearrange("(k p) -> k p", p=P)).then_inc(S("vec_in"), 16)
                r += n
            act.wait_ge(S("const0"), 5)
            act.wait_ge(S("mem_in"), 16)
            for i in range(2):
                if i:
                    act.wait_ge(S("ssq_mem"), i)
                act.activation(catT.rearrange("p k t -> p (k t)")[:, 0:D], mem[:, i, :], ACT.Square,
                               accum_out=ssm[:, i:i + 1]).then_inc(S("ssq_mem"), 1)
            has(act, "vec")
            for i in range(4):
                took(act, f"memT{i}")
                b = bank(f"memT{i}")
                act.activation(memT[:, 2 * i, :], b[:, 0:256], ACT.Copy, scale=g_memkv[:, 2 * i:2 * i + 1])
                free(act.activation(memT[:, 2 * i + 1, :], b[:, 256:512], ACT.Copy,
                                    scale=g_memkv[:, 2 * i + 1:2 * i + 2]), f"memT{i}")
            act.wait_ge(S("x_in"), 16)
            act.wait_ge(S("xs_in"), 16)
            for i, (t0, n) in enumerate(TILES):
                if i:
                    act.wait_ge(S("ssq_x"), i)
                act.activation(catT.rearrange("p k t -> p (k t)")[0:n, 1024:1024 + D], xtok[0:n, i, :], ACT.Square,
                               accum_out=ssx[0:n, i:i + 1]).then_inc(S("ssq_x"), 1)
            act.wait_ge(S("meansq0"), 1)
            act.activation(sst[:, 0:5], sst[:, 0:5], ACT.Sqrt).then_inc(S("root0"), 1)
            act.wait_ge(S("rstd0"), 1)
            def gained(k):
                has(act, f"xT{k}")
                if k == 0:
                    has(act, "bup")
                act.activation(gxT[:, k, :], xT[:, k, :], ACT.Copy, scale=g_mix[:, k:k + 1]).then_inc(S("gx"), 1)
            for i in range(4):
                took(act, f"K{i}")
                if i == 0:
                    act.wait_ge(S("ssq_x"), 3)
                free(act.activation(Kp[:, i // 2, 512 * (i % 2):512 * (i % 2) + 512], bank(f"K{i}"), ACT.Copy,
                                    scale=rsm[:, i // 2:i // 2 + 1]), f"K{i}")
            for k in range(KT):
                gained(k)
            for i in range(4):
                took(act, f"V{i}")
                free(act.activation(Vp[:, i // 2, 512 * (i % 2):512 * (i % 2) + 512], bank(f"V{i}"), ACT.Copy,
                                    scale=rsm[:, i // 2:i // 2 + 1]), f"V{i}")
            for i in range(4):
                took(act, f"KTp{i}")
                free(act.activation(KTp[:, 2 * i:2 * i + 2, :].rearrange("p k m -> p (k m)"), bank(f"KTp{i}"),
                                    ACT.Copy), f"KTp{i}")
            for j, (i0, ni, n) in enumerate(((0, 2, P), (2, 1, 64))):
                took(act, f"gate{j}")
                act.wait_ge(S("gate_min"), j + 1)
                free(act.activation(la1[0:n, i0:i0 + ni, :].rearrange("p i f -> p (i f)"), bank(f"gate{j}", 256 * ni, n),
                                    ACT.Abs), f"gate{j}")
            for j, (i0, ni, n) in enumerate(((0, 2, P), (2, 1, 64))):
                v_ = la1[0:n, i0:i0 + ni, :].rearrange("p i f -> p (i f)")
                has(act, f"gate{j}")
                act.activation(v_, v_, ACT.Exp, scale=-1.0).then_inc(S("gate_exp"), 1)
                act.wait_ge(S("gate_exp"), j + 1)
                act.activation(v_, v_, ACT.Ln, bias=1.0).then_inc(S("gate_ln"), 1)
            for i, (t0, n) in enumerate(TILES):
                took(act, f"v{i}")
                free(act.activation(vtok[0:n, i, :], bank(f"v{i}", 512, n), ACT.Copy, scale=rsx[0:n, i:i + 1]), f"v{i}")
            has(act, "cum1")
            fl = lambda z: z.rearrange("p r t -> p (r t)")
            act.activation(fl(eb), fl(bT), ACT.Exp).then_inc(S("eb"), 1)
            act.activation(fl(enb), fl(bT), ACT.Exp, scale=-1.0).then_inc(S("enb"), 1)
            act.wait_ge(S("bl_diff"), 1)
            act.activation(fl(ebl), fl(ebl), ACT.Exp).then_inc(S("ebl"), 1)
            took(act, "prevT")
            free(act.activation(upad[:, :, UP_P:UP_P + BUF], bank("prevT", 4 * BUF).rearrange("p (g t) -> p g t", g=4),
                                ACT.Copy), "prevT")
            act.wait_ge(S("gla_zero"), 2)
            for c_ in range(5):
                i, r0 = c_ // 2, 64 * (c_ % 2)
                j = 0 if i < 2 else 1
                if c_ in (0, 4):
                    took(act, f"klT{j}")
                b = ps[r0:r0 + 64, J.bank(f"klT{j}"), 256 * (i % 2):256 * (i % 2) + 256]
                ins = act.activation(klz[r0:r0 + 64, c_, :], b, ACT.Copy)
                if c_ in (3, 4):
                    free(ins, f"klT{j}")
            has(act, "g3")
            act.activation(sgT_e, sgT_f, ACT.Sigmoid).then_inc(S("g_sigmoid"), 1)
            for i in range(4):
                took(act, f"KTs{i}")
                free(act.activation(KTs[:, 2 * i:2 * i + 2, :].rearrange("p k m -> p (k m)"), bank(f"KTs{i}"),
                                    ACT.Copy), f"KTs{i}")
            for i, (t0, n) in enumerate(TILES):
                has(act, f"o{i}")
                act.activation(osq[0:n, i, :], otok[0:n, i, :], ACT.Square).then_inc(S("o_sq"), 1)
            act.wait_ge(S("meansq_o"), 1)
            act.activation(small[:, 22:34], small[:, 22:34], ACT.Sqrt).then_inc(S("root_o"), 1)
            for i in range(2):
                took(act, f"hist{i}")
                free(act.activation(hist[0:BUF, i, :], bank(f"hist{i}", 512, BUF), ACT.Copy), f"hist{i}")
            for k in range(KT):
                has(act, f"out{k}")
                if k == 0:
                    has(act, "g3")
                act.activation(gxT[:, k, :], xT[:, k, :], ACT.Copy, scale=g_memq[:, k:k + 1]).then_inc(S("gx1"), 1)
                act.activation(sq1[:, k, :], xT[:, k, :], ACT.Square).then_inc(S("sq1"), 1)
            has(act, "rms1")
            act.activation(ms1[:, :], ms1[:, :], ACT.Sqrt).then_inc(S("root1"), 1)
            for j in range(6):
                took(act, f"s{j}")
                act.wait_ge(S("nmax"), j + 1)
                n = P if j < 4 else 64
                for h2 in range(2):
                    h = 2 * (j % 2) + h2
                    dst = probs_p[:, j // 2, h, :] if j < 4 else probs_s[0:64, h, :]
                    cidx = (j // 2) * 4 + h
                    ins = act.activation(dst, bank(f"s{j}", 512, n)[:, 256 * h2:256 * h2 + 256], ACT.Exp,
                                         bias=nmx[0:n, cidx:cidx + 1], scale=rs1p[0:n, j // 2:j // 2 + 1],
                                         accum_out=rs[0:n, cidx:cidx + 1])
                free(ins, f"s{j}")
            for h in range(4):
                took(act, f"PV{h}")
                free(act.activation(aoT[:, 2 * h:2 * h + 2, 0:LP], bank(f"PV{h}").rearrange("p (d l) -> p d l", d=2),
                                    ACT.Copy), f"PV{h}")
            took(act, "PV4")
            free(act.activation(aoT[:, :, LP:NT], bank("PV4").rearrange("p (d l) -> p d l", d=KT), ACT.Copy), "PV4")
            for k in range(KT):
                has(act, f"mo{k}")
                act.activation(sq2[:, k, :], xT[:, k, :], ACT.Square).then_inc(S("sq2"), 1)
            act.wait_ge(S("meansq2"), 1)
            act.activation(rs2[:, :], rs2[:, :], ACT.Sqrt).then_inc(S("root2"), 1)
            for j in range(6):
                i, n = j // 2, TILES[j // 2][1]
                took(act, f"x2_{j}")
                free(act.activation(acc[0:n, i, 512 * (j % 2):512 * (j % 2) + 512], bank(f"x2_{j}", 512, n), ACT.Copy),
                     f"x2_{j}")
            act.wait_ge(S("rstd2"), 1)
            for i, (t0, n) in enumerate(TILES):
                has(act, f"x2_{2 * i + 1}")
                act.activation(Hm[0:n, i, :], acc[0:n, i, :], ACT.Copy, scale=rs2[0:n, i:i + 1]).then_inc(S("Hm"), 1)
            act.wait_ge(S("top"), 1)
            act.wait_ge(S("moe_zero"), 2)
            for i, (t0, n) in enumerate(TILES):
                act.activation(gpad[0:n, i, 64:96], logit[0:n, i, :], ACT.Exp, bias=nt1[0:n, i:i + 1],
                               scale=1.0).then_inc(S("gate_e"), 1)
            moe_act(act)

        @block.vector
        def _(dve):
            def free(ins, name):
                assert J.freed_at(name) == ("D", free.n + 1), (name, free.n)
                free.n += 1
                ins.then_inc(freed["D"], 1)
            free.n = 0
            dve.wait_ge(S("const2"), 4)
            dve.tensor_copy(iota[:, :], iota[:, :].bitcast(I32)).then_inc(S("iota"), 1)
            took(dve, "vec")
            free(dve.tensor_copy(vec[:, :], bank("vec", 40)), "vec")
            dve.wait_ge(S("ssq_mem"), 2)
            dve.wait_ge(S("ssq_x"), 3)
            dve.tensor_scalar(sst[:, 0:5], small[:, 0:5], 1.0 / D, EPS, ALU.mult, ALU.add).then_inc(S("meansq0"), 1)
            dve.wait_ge(S("root0"), 1)
            dve.reciprocal(small[:, 5:10], sst[:, 0:5]).then_inc(S("rstd0"), 1)
            took(dve, "bup")
            free(dve.tensor_copy(bupT.rearrange("p e f -> p f e"), bank("bup").rearrange("p (f e) -> p f e", e=E)), "bup")
            for k in range(KT):
                took(dve, f"xT{k}")
                free(dve.tensor_copy(xT[:, k, :], bank(f"xT{k}", NT)), f"xT{k}")
                if k == 0:
                    dve.wait_ge(S("rstd0"), 1)
                    for i in range(3):
                        dve.tensor_scalar(rT_diag[:, i, :], ident[:, :], rsx[:, i:i + 1], None,
                                          ALU.mult).then_inc(S("diag"), 1)
            took(dve, "rms0")
            free(dve.tensor_copy(rstdb[:, :], bank("rms0", NT)), "rms0")
            has(dve, "rms0")
            took(dve, "r")
            dve.wait_ge(S("rT_ones"), 1)
            free(dve.tensor_tensor(rT[0:RANK, :], bank("r", NT, RANK), rstdb[0:RANK, :], ALU.mult), "r")
            for j in range(2):
                took(dve, f"q{j}")
                free(dve.tensor_tensor(qT[:, j, :], bank(f"q{j}", NT), rstdb[:, :], ALU.mult), f"q{j}")
            dve.wait_ge(S("k_out"), 16)
            for j, (i0, ni, n) in enumerate(((0, 2, P), (2, 1, 64))):
                took(dve, f"gate{j}")
                dve.tensor_scalar(la0[0:n, i0:i0 + ni, :].rearrange("p i f -> p (i f)"), bank(f"gate{j}", 256 * ni, n),
                                  0.0, None, ALU.min).then_inc(S("gate_min"), 1)
            for j in range(2):
                took(dve, f"k{j}")
                free(dve.tensor_tensor(kT[:, j, :], bank(f"k{j}", NT), rstdb[:, :], ALU.mult), f"k{j}")
            dve.wait_ge(S("gate_ln"), 2)
            for j, (i0, ni, n) in enumerate(((0, 2, P), (2, 1, 64))):
                dve.tensor_tensor(la0[0:n, i0:i0 + ni, :], la0[0:n, i0:i0 + ni, :], la1[0:n, i0:i0 + ni, :],
                                  ALU.subtract).then_inc(S("log_a"), 1)
            for g in range(4):
                took(dve, f"u{g}")
                b = bank(f"u{g}", NT)
                dve.tensor_tensor(upad[:, g, BUF:UP_P], b[:, 0:LP], rstdb[:, 0:LP], ALU.mult)
                free(dve.tensor_tensor(upad[:, g, UP_P + BUF:UPAD], b[:, LP:NT], rstdb[:, LP:NT], ALU.mult), f"u{g}")
            for j in range(2):
                took(dve, f"cum{j}")
                free(dve.tensor_copy(bT[:, j, :], bank(f"cum{j}", NT)), f"cum{j}")
            has(dve, "cum1")
            for r_ in range(2):
                bc = bT[:, r_, :].rearrange("p (c t) -> p c t", c=5)
                last = dve.tensor_tensor(ebl[:, r_, :].rearrange("p (c t) -> p c t", c=5),
                                         bc[:, :, CHUNK - 1:CHUNK].broadcast_to([P, 5, CHUNK]), bc, ALU.subtract)
            last.then_inc(S("bl_diff"), 1)
            dve.wait_ge(S("gla_zero"), 3)
            dve.wait_ge(S("eb"), 1)
            for h in range(4):
                r0 = 64 * (h % 2)
                dve.scalar_tensor_tensor(qdz[r0:r0 + 64, h, :], qT[r0:r0 + 64, h // 2, :], DK ** -0.5,
                                         eb[r0:r0 + 64, h // 2, :], ALU.mult, ALU.mult).then_inc(S("qd"), 1)
            dve.wait_ge(S("enb"), 1)
            fl = lambda z: z.rearrange("p r t -> p (r t)")
            dve.tensor_tensor(fl(kdT), fl(kT), fl(enb), ALU.mult).then_inc(S("kd"), 1)
            dve.wait_ge(S("ebl"), 1)
            dve.tensor_tensor(fl(ebl), fl(kT), fl(ebl), ALU.mult).then_inc(S("kl"), 1)
            for g in range(4):
                took(dve, f"g{g}")
                free(dve.tensor_tensor(sgT[:, g, :], bank(f"g{g}", NT), rstdb[:, :], ALU.mult), f"g{g}")
            for i, (t0, n) in enumerate(TILES):
                took(dve, f"AT{i}")
                m = tri[0:n, 0:n].bitcast(I32).unsqueeze(1).broadcast_to([n, 4, n])
                free(dve.copy_predicated(AT[0:n, i, :, 0:n], m, bank(f"AT{i}", 4 * n, n).rearrange("p (h t) -> p h t", h=4)),
                     f"AT{i}")
            n = 0
            for c_ in range(NCH):
                took(dve, f"ds{c_}")
                b = bank(f"ds{c_}").rearrange("p (r f) -> p r f", r=2)
                src = {0: None, 1: Sbuf[0], 2: Sbuf[1], 3: Sbuf[2], 4: Sbuf[4]}[c_]
                dst = Sbuf[c_] if c_ < 4 else Sbuf[5]
                if c_ in (1, 2, 3):
                    dve.wait_ge(S("state"), n)
                if c_ == 4:
                    dve.wait_ge(S("s0_in"), 16)
                    has(dve, "prevT")
                for hh in range(2):
                    r0 = 64 * hh
                    for r_ in range(2):
                        bb = b[r0:r0 + 64, r_, 128 * hh:128 * hh + 128]
                        if src is None:
                            ins = dve.tensor_copy(dst[r0:r0 + 64, r_, :], bb)
                        else:
                            ins = dve.scalar_tensor_tensor(dst[r0:r0 + 64, r_, :], src[r0:r0 + 64, r_, :],
                                                           eb[r0:r0 + 64, r_, CHUNK * c_ + 63:CHUNK * c_ + 64], bb,
                                                           ALU.mult, ALU.add)
                        if (hh, r_) == (1, 1):
                            free(ins, f"ds{c_}")
                        else:
                            ins.then_inc(S("state"), 1)
                            n += 1
                has(dve, f"ds{c_}")
            dve.wait_ge(S("g_sigmoid"), 1)
            dve.tensor_tensor(sgT_f, sgT_f, sgT_e, ALU.mult).then_inc(S("silu"), 1)
            for i, (t0, n) in enumerate(TILES):
                took(dve, f"o{i}")
                free(dve.tensor_copy(otok[0:n, i, :], bank(f"o{i}", 512, n)), f"o{i}")
            for g in range(4):
                took(dve, f"pool{g}")
                free(dve.tensor_scalar(catT[:, 4 + g, :], bank(f"pool{g}", NT), pscale[:, g:g + 1], None, ALU.mult),
                     f"pool{g}")
            for i, (t0, n) in enumerate(TILES):
                dve.wait_ge(S("o_sq"), i + 1)
                dve.tensor_reduce(sso[0:n, i, :], osq[0:n, i, :].rearrange("p (h e) -> p h e", h=4), AX.X,
                                  ALU.add).then_inc(S("o_sum"), 1)
            dve.wait_ge(S("o_sum"), 3)
            dve.tensor_scalar(small[:, 22:34], small[:, 10:22], 1.0 / DV, EPS, ALU.mult, ALU.add).then_inc(S("meansq_o"), 1)
            dve.wait_ge(S("root_o"), 1)
            dve.reciprocal(small[:, 22:34], small[:, 22:34]).then_inc(S("rstd_o"), 1)
            dve.wait_ge(S("rstd_o"), 1)
            for i, (t0, n) in enumerate(TILES):
                v_ = otok[0:n, i, :].rearrange("p (h e) -> p h e", h=4)
                dve.tensor_tensor(v_, v_, rso[0:n, i, :].unsqueeze(2).broadcast_to([n, 4, DV]),
                                  ALU.mult).then_inc(S("o_norm"), 1)
            dve.wait_ge(S("silu"), 1)
            for h in range(4):
                took(dve, f"oT{h}")
                free(dve.scalar_tensor_tensor(catT[:, h, :], bank(f"oT{h}", NT), g_gla[:, h:h + 1], sgT[:, h, :],
                                              ALU.mult, ALU.mult), f"oT{h}")
            for k in range(KT):
                took(dve, f"out{k}")
                free(dve.tensor_tensor(xT[:, k, :], bank(f"out{k}", NT), xT[:, k, :], ALU.add), f"out{k}")
            for k in range(KT):
                took(dve, f"mq{k}")
                free(dve.tensor_copy(aqT[:, k, :], bank(f"mq{k}", NT)), f"mq{k}")
            took(dve, "rms1")
            dve.tensor_scalar(ms1[:, 0:2], bank("rms1", 2), 1.0 / D, EPS, ALU.mult, ALU.add)
            free(dve.tensor_scalar(ms1[0:LS, 2:3], ps[0:LS, J.bank("rms1"), 2:3], 1.0 / D, EPS, ALU.mult, ALU.add), "rms1")
            dve.wait_ge(S("root1"), 1)
            dve.reciprocal(rs1[:, :], ms1[:, :]).then_inc(S("rstd1"), 1)
            dve.wait_ge(S("rstd1"), 1)
            dve.tensor_scalar(rs1p[:, :], rs1[:, :], 1.0 / 16.0, None, ALU.mult).then_inc(S("rstd1"), 1)
            dve.tensor_scalar(rs1n[:, :], rs1[:, :], -1.0 / 16.0, None, ALU.mult).then_inc(S("rstd1"), 1)
            dve.wait_ge(S("rstd1"), 3)
            for j in range(6):
                took(dve, f"s{j}")
                n = P if j < 4 else 64
                c0 = (j // 2) * 4 + 2 * (j % 2)
                dve.tensor_reduce(mx[0:n, c0:c0 + 2], bank(f"s{j}", 512, n).rearrange("p (h m) -> p h m", h=2), AX.X,
                                  ALU.max).then_inc(S("smax"), 1)
                dve.wait_ge(S("smax"), j + 1)
                dve.tensor_scalar(nmx[0:n, c0:c0 + 2], mx[0:n, c0:c0 + 2], rs1n[0:n, j // 2:j // 2 + 1], None,
                                  ALU.mult).then_inc(S("nmax"), 1)
            m = 0
            for j in range(6):
                has(dve, f"s{j}")
                n = P if j < 4 else 64
                c0 = (j // 2) * 4 + 2 * (j % 2)
                dve.reciprocal(rinv[0:n, c0:c0 + 2], rs[0:n, c0:c0 + 2]).then_inc(S("rinv"), 1)
                dve.wait_ge(S("rinv"), j + 1)
                for h2 in range(2):
                    h = 2 * (j % 2) + h2
                    v_ = probs_p[:, j // 2, h, :] if j < 4 else probs_s[0:64, h, :]
                    dve.tensor_scalar(v_, v_, rinv[0:n, c0 + h2:c0 + h2 + 1], None, ALU.mult).then_inc(S("probs"), 1)
            for h in range(4):
                took(dve, f"PT{h}")
                free(dve.tensor_copy(PTp[:, h, :, :].rearrange("p i l -> p (i l)"), bank(f"PT{h}")), f"PT{h}")
            took(dve, "PT4")
            free(dve.tensor_copy(PTs.rearrange("p h i l -> p (h i l)"), bank("PT4")), "PT4")
            dve.wait_ge(S("router_in"), 32)
            dve.tensor_tensor(gwr, wr, g_moe.unsqueeze(2).broadcast_to([P, KT, E]), ALU.mult).then_inc(S("gwr"), 1)
            for k in range(KT):
                took(dve, f"mo{k}")
                free(dve.tensor_tensor(xT[:, k, :], bank(f"mo{k}", NT), xT[:, k, :], ALU.add), f"mo{k}")
            took(dve, "router")
            dve.tensor_scalar(rs2[:, 0:2], ps[:, J.bank("router"), 96:98], 1.0 / D, EPS, ALU.mult, ALU.add)
            dve.tensor_scalar(rs2[0:LS, 2:3], ps[0:LS, J.bank("router"), 98:99], 1.0 / D, EPS, ALU.mult,
                              ALU.add).then_inc(S("meansq2"), 1)
            dve.wait_ge(S("root2"), 1)
            dve.reciprocal(rs2[:, :], rs2[:, :]).then_inc(S("rstd2"), 1)
            dve.wait_ge(S("rstd2"), 1)
            for i, (t0, n) in enumerate(TILES):
                ins = dve.scalar_tensor_tensor(logit[0:n, i, :], ps[0:n, J.bank("router"), 32 * i:32 * i + 32],
                                               rs2[0:n, i:i + 1], brout[0:n, :], ALU.mult, ALU.add)
            free(ins, "router")
            has(dve, "router")
            for i, (t0, n) in enumerate(TILES):
                dve.max(top8[0:n, i, :], logit[0:n, i, :]).then_inc(S("max8"), 1)
            dve.memset(rankx[64:P, 2, :], -1.0)
            dve.memset(Gm[64:P, 2, :], 0.0)
            dve.memset(sel[64:P, 2, :], 0.0).then_inc(S("max8"), 1)
            dve.wait_ge(S("max8"), 4)
            dve.tensor_scalar(nt1[:, :], top8[:, :, 0], -1.0, None, ALU.mult).then_inc(S("top"), 1)
            for i, (t0, n) in enumerate(TILES):
                dve.max_index(topi[0:n, i, :], top8[0:n, i, :], logit[0:n, i, :]).then_inc(S("top_at"), 1)
            dve.wait_ge(S("top_at"), 3)
            for i, (t0, n) in enumerate(TILES):
                dve.tensor_copy(topf[0:n, i, :], topi[0:n, i, :]).then_inc(S("top_at"), 1)
            dve.wait_ge(S("top_at"), 6)
            for k in range(4):
                for i, (t0, n) in enumerate(TILES):
                    if k == 0:
                        ins = dve.tensor_scalar(sel[0:n, i, :], iota[0:n, 0:E], topf[0:n, i, 0:1], None, ALU.is_equal)
                    else:
                        ins = dve.scalar_tensor_tensor(sel[0:n, i, :], iota[0:n, 0:E], topf[0:n, i, k:k + 1],
                                                       sel[0:n, i, :], ALU.is_equal, ALU.add)
                    ins.then_inc(S("sel"), 1)
                dve.wait_ge(S("sel"), 3 * k + 3)
            dve.wait_ge(S("sel"), 12)
            took(dve, "rank")
            for i, (t0, n) in enumerate(TILES):
                ins = dve.scalar_tensor_tensor(rankx[0:n, i, :], ps[0:n, J.bank("rank"), 32 * i:32 * i + 32], 1.0,
                                               sel[0:n, i, :], ALU.add, ALU.mult)
            free(ins, "rank")
            has(dve, "rank")
            for i, (t0, n) in enumerate(TILES):
                dve.tensor_scalar(rankx[0:n, i, :], rankx[0:n, i, :], -1.0, None, ALU.add).then_inc(S("rankx"), 1)
            moe_dve(dve)

        @block.tensor
        def _(pe):
            def begin(name):
                before = J.occupant_before(name)
                if before:
                    pe.wait_ge(freed[before[0]], before[1])

            def end(ins):
                ins.then_inc(filled, 1)

            def turn(name, pieces):
                begin(name)
                for c0, src, rows, cols in pieces:
                    ins = pe.transpose(ps[0:cols, J.bank(name), c0:c0 + rows], src, ident[0:rows, 0:rows])
                end(ins)

            def project(name, w, x, rows=P):
                begin(name)
                for k in range(KT):
                    ins = pe.matmul(bank(name, NT, rows), w[:, k, :], x[:, k, :], start=(k == 0), stop=(k == KT - 1))
                end(ins)

            pe.wait_ge(S("const1"), 1)
            pe.wait_ge(S("vec_in"), 96)
            turn("vec", [(0, smallrows[0:40, :], 40, P)])
            pe.wait_ge(S("mem_in"), 16)
            for j in range(4):
                turn(f"memT{j}", [(256 * kk + 128 * i, mem[:, i, 128 * (2 * j + kk):128 * (2 * j + kk) + 128], P, P)
                                  for kk in range(2) for i in range(2)])

            def memory_product(what, w, sem):
                for j in range(4):
                    begin(f"{what}{j}")
                for k in range(KT):
                    if k % 2 == 0:
                        pe.wait_ge(S(f"{sem}{k // 2}"), 16)
                        if what == "K":
                            has(pe, f"memT{k // 2}")
                    for j in range(4):
                        ins = pe.matmul(bank(f"{what}{j}"), memT[:, k, 128 * (j // 2):128 * (j // 2) + 128],
                                        w[:, k, 512 * (j % 2):512 * (j % 2) + 512], start=(k == 0), stop=(k == KT - 1))
                        if k == KT - 1:
                            end(ins)
            memory_product("K", wmk, "wmk_in")
            pe.wait_ge(S("bup_in"), 16)
            turn("bup", [(E * f, buprow[0:E, 128 * f:128 * f + 128], E, P) for f in range(16)])
            pe.wait_ge(S("x_in"), 16)
            pe.wait_ge(S("xs_in"), 16)
            for k in range(KT):
                turn(f"xT{k}", [(t0, xtok[0:n, i, 128 * k:128 * k + 128], n, P) for i, (t0, n) in enumerate(TILES)])
            pe.wait_ge(S("diag"), 3)
            begin("rms0")
            for i, (t0, n) in enumerate(TILES):
                ins = pe.matmul(bank("rms0", NT)[:, t0:t0 + n], ones[0:n, :], rT_diag[0:n, i, 0:n], start=True, stop=True)
            end(ins)
            memory_product("V", wmv, "wmv_in")
            has(pe, "K3")
            for j in range(4):
                turn(f"KTp{j}", [(256 * kk + 128 * i, Kp[:, i, 128 * (2 * j + kk):128 * (2 * j + kk) + 128], P, P)
                                 for kk in range(2) for i in range(2)])
            pe.wait_ge(S("gx"), 8)
            pe.wait_ge(S("wr_in"), 16)
            project("r", wr_col, gxT, RANK)
            pe.wait_ge(S("wqk_in"), 16)
            project("q0", w_qk[:, :, 0:128], gxT)
            project("q1", w_qk[:, :, 128:256], gxT)
            pe.wait_ge(S("wgate_in"), 32)
            has(pe, "r")
            for j, tiles in enumerate(((0, 1), (2,))):
                begin(f"gate{j}")
                for m, i in enumerate(tiles):
                    t0, n = TILES[i]
                    ins = pe.matmul(ps[0:n, J.bank(f"gate{j}"), 256 * m:256 * m + 256], rT[0:RANK + 1, t0:t0 + n],
                                    wgate[0:RANK + 1, :], start=True, stop=True)
                end(ins)
            project("k0", w_qk[:, :, 256:384], gxT)
            project("k1", w_qk[:, :, 384:512], gxT)
            pe.wait_ge(S("wv_in"), 16)
            for i, (t0, n) in enumerate(TILES):
                begin(f"v{i}")
                for k in range(KT):
                    ins = pe.matmul(bank(f"v{i}", 512, n), gxT[:, k, t0:t0 + n], w_v[:, k, :], start=(k == 0),
                                    stop=(k == KT - 1))
                end(ins)
            pe.wait_ge(S("wu_in"), 16)
            for g in range(4):
                project(f"u{g}", w_u[:, :, 128 * g:128 * g + 128], gxT)
            pe.wait_ge(S("log_a"), 2)
            pe.wait_ge(S("const2"), 4)
            for j in range(2):
                begin(f"cum{j}")
                for i, (t0, n) in enumerate(TILES):
                    ins = pe.matmul(bank(f"cum{j}", NT)[:, t0:t0 + n], la0[0:n, i, 128 * j:128 * j + 128], tri[0:n, 0:n],
                                    start=True, stop=True)
                end(ins)
            pe.wait_ge(S("prev_in"), 16)
            turn("prevT", [(BUF * g, prevrow[0:BUF, 128 * g:128 * g + 128], BUF, P) for g in range(4)])
            pe.wait_ge(S("wg_in"), 16)
            for g in range(4):
                project(f"g{g}", w_g[:, :, 128 * g:128 * g + 128], gxT)
            pe.wait_ge(S("kl"), 1)
            for j, tiles in enumerate(((0, 1), (2,))):
                begin(f"klT{j}")
                for m, i in enumerate(tiles):
                    t0, n = TILES[i]
                    for r_ in range(2):
                        ins = pe.transpose(ps[0:n, J.bank(f"klT{j}"), 256 * m + 128 * r_:256 * m + 128 * r_ + 128],
                                           ebl[:, r_, t0:t0 + n], ident[:, :])
                end(ins)
            pe.wait_ge(S("qd"), 4)
            pe.wait_ge(S("kd"), 1)
            for i, (t0, n) in enumerate(TILES):
                begin(f"AT{i}")
                for h in range(4):
                    ins = pe.matmul(ps[0:n, J.bank(f"AT{i}"), n * h:n * h + n], kdT[:, h // 2, t0:t0 + n],
                                    qdz[:, h, t0:t0 + n], start=True, stop=True)
                end(ins)
            has(pe, "klT1")
            has(pe, "v2")
            for c_ in range(NCH):
                i, n = c_ // 2, TILES[c_ // 2][1]
                begin(f"ds{c_}")
                for r_ in range(2):
                    ins = pe.matmul(ps[:, J.bank(f"ds{c_}"), 256 * r_:256 * r_ + 256], klz[0:n, c_, 128 * r_:128 * r_ + 128],
                                    vtok[0:n, i, 256 * r_:256 * r_ + 256], start=True, stop=True)
                end(ins)
            pe.wait_ge(S("ks_in"), 16)
            for j in range(4):
                turn(f"KTs{j}", [(256 * kk + 128 * i, Ks[:, i, 128 * (2 * j + kk):128 * (2 * j + kk) + 128], P, P)
                                 for kk in range(2) for i in range(2)])
            has(pe, "AT2")
            has(pe, "ds4")
            pe.wait_ge(S("state"), 15)
            for i, (t0, n) in enumerate(TILES):
                begin(f"o{i}")
                for h in range(4):
                    c0 = 128 * h
                    ins = pe.matmul(ps[0:n, J.bank(f"o{i}"), c0:c0 + 128], AT[0:n, i, h, 0:n], vtok[0:n, i, c0:c0 + 128],
                                    start=True, stop=False, skip_group_check=True)
                    for c_ in ((0, 1), (2, 3), (4,))[i]:
                        if c_ == 0:
                            continue
                        st = Sbuf[c_ - 1] if c_ < 4 else Sbuf[4]
                        r0 = 64 * (c_ % 2)
                        ins = pe.matmul(ps[r0:r0 + 64, J.bank(f"o{i}"), c0:c0 + 128], qdz[:, h, 64 * c_:64 * c_ + 64],
                                        st[:, h // 2, :], start=False, stop=True, skip_group_check=True)
                end(ins)
            pe.wait_ge(S("pool_diff"), 8)
            pe.wait_ge(S("poolw_in"), 16)
            for g in range(4):
                begin(f"pool{g}")
                end(pe.matmul(bank(f"pool{g}", NT), poolw[:, g, :], invn[:, g, :], start=True, stop=True))
            for j, t_end in enumerate((UP_P, UPAD)):
                begin(f"hist{j}")
                for g in range(4):
                    ins = pe.transpose(ps[0:BUF, J.bank(f"hist{j}"), 128 * g:128 * g + 128],
                                       upad[:, g, t_end - BUF:t_end], ident[:, :])
                end(ins)
            def out_half(k, j0):
                for j in range(j0, j0 + 4):
                    ins = pe.matmul(bank(f"out{k}", NT), wsq[:, k // 2, j, 128 * (k % 2):128 * (k % 2) + 128],
                                    catT[:, j, :], start=(j == 4), stop=(j == 3))
                return ins
            has(pe, "pool3")
            for k in range(4):
                if k % 2 == 0:
                    pe.wait_ge(S(f"wout_in{k // 2}"), 16)
                begin(f"out{k}")
                out_half(k, 4)
            pe.wait_ge(S("o_norm"), 3)
            for h in range(4):
                turn(f"oT{h}", [(t0, otok[0:n, i, 128 * h:128 * h + 128], n, P) for i, (t0, n) in enumerate(TILES)])
            has(pe, "oT3")
            for k in range(KT):
                if k >= 4:
                    if k % 2 == 0:
                        pe.wait_ge(S(f"wout_in{k // 2}"), 16)
                    begin(f"out{k}")
                    out_half(k, 4)
                end(out_half(k, 0))
            pe.wait_ge(S("gx1"), KT)
            pe.wait_ge(S("sq1"), KT)
            for k in range(KT):
                if k % 2 == 0:
                    pe.wait_ge(S(f"wmq_in{k // 2}"), 16)
                project(f"mq{k}", wsq[:, k // 2, :, 128 * (k % 2):128 * (k % 2) + 128], gxT)
            begin("rms1")
            for i, (t0, n) in enumerate(TILES):
                for k in range(KT):
                    ins = pe.matmul(ps[0:n, J.bank("rms1"), i:i + 1], sq1[:, k, t0:t0 + n], ones[:, 0:1],
                                    start=(k == 0), stop=(k == KT - 1))
            end(ins)
            has(pe, "mq7")
            for j in range(6):
                begin(f"s{j}")
                t0, n = TILES[j // 2]
                KTx = KTp if j < 4 else KTs
                for h2 in range(2):
                    h = 2 * (j % 2) + h2
                    for d_ in range(2):
                        ins = pe.matmul(ps[0:n, J.bank(f"s{j}"), 256 * h2:256 * h2 + 256], aqT[:, 2 * h + d_, t0:t0 + n],
                                        KTx[:, 2 * h + d_, :], start=(d_ == 0), stop=(d_ == 1))
                end(ins)
            pe.wait_ge(S("probs"), 8)
            for h in range(4):
                turn(f"PT{h}", [(256 * i + 128 * l, probs_p[:, l, h, 128 * i:128 * i + 128], P, P)
                                for i in range(2) for l in range(2)])
            pe.wait_ge(S("probs"), 12)
            turn("PT4", [(128 * h + 64 * i, probs_s[0:64, h, 128 * i:128 * i + 128], 64, P)
                         for h in range(4) for i in range(2)])
            for h in range(4):
                begin(f"PV{h}")
                has(pe, f"PT{h}")
                for d_ in range(2):
                    for i in range(2):
                        c0 = 256 * h + 128 * d_
                        ins = pe.matmul(bank(f"PV{h}")[:, 256 * d_:256 * d_ + 256], Vp[:, i, c0:c0 + 128], PTp[:, h, i, :],
                                        start=(i == 0), stop=(i == 1))
                end(ins)
            begin("PV4")
            has(pe, "PT4")
            pe.wait_ge(S("vs_in"), 16)
            for d_ in range(KT):
                for i in range(2):
                    ins = pe.matmul(bank("PV4")[:, 64 * d_:64 * d_ + 64], Vs[:, i, 128 * d_:128 * d_ + 128],
                                    PTs[:, d_ // 2, i, :], start=(i == 0), stop=(i == 1))
            end(ins)
            has(pe, "PV4")
            for k in range(KT):
                if k % 2 == 0:
                    pe.wait_ge(S(f"wmo_in{k // 2}"), 16)
                project(f"mo{k}", wsq[:, k // 2, :, 128 * (k % 2):128 * (k % 2) + 128], aoT)
            has(pe, "mo7")
            pe.wait_ge(S("gwr"), 1)
            begin("router")
            for i, (t0, n) in enumerate(TILES):
                for k in range(KT):
                    pe.matmul(ps[0:n, J.bank("router"), E * i:E * i + E], xT[:, k, t0:t0 + n], gwr[:, k, :],
                              start=(k == 0), stop=(k == KT - 1))
            pe.wait_ge(S("sq2"), KT)
            for i, (t0, n) in enumerate(TILES):
                for k in range(KT):
                    ins = pe.matmul(ps[0:n, J.bank("router"), 96 + i:97 + i], sq2[:, k, t0:t0 + n], ones[:, 0:1],
                                    start=(k == 0), stop=(k == KT - 1))
            end(ins)
            for j in range(6):
                i, n = j // 2, TILES[j // 2][1]
                t0 = TILES[i][0]
                begin(f"x2_{j}")
                for kk in range(4):
                    ins = pe.transpose(ps[0:n, J.bank(f"x2_{j}"), 128 * kk:128 * kk + 128],
                                       xT[:, 4 * (j % 2) + kk, t0:t0 + n], ident[:, :])
                end(ins)
            pe.wait_ge(S("sel"), 12)
            begin("rank")
            for i, (t0, n) in enumerate(TILES):
                for j in range(i + 1):
                    m = TILES[j][1]
                    lhs = below[0:m, 0:n] if j == i else ones[0:m, 0:n]
                    ins = pe.matmul(ps[0:n, J.bank("rank"), E * i:E * i + E], lhs, sel[0:m, j, :], start=(j == 0),
                                    stop=(j == i))
            end(ins)
            moe_tensor(pe)


IN = ["x_prompt", "x_sample", "mem_prompt", "state_gla", "state_pool", "cache_mem_k", "cache_mem_v", "norm_mix",
      "w_in", "w_gate", "b_gate", "gla_gain", "pool_w", "pool_scale", "w_out", "norm_mem_q", "norm_mem_kv", "w_mq",
      "w_mk", "w_mv", "w_mo", "norm_moe", "w_router", "b_router", "w_up", "b_up", "w_down", "b_down", "norm_final"]
OUT = [("y_p", (1, LP, D)), ("y_s", (1, LS, D)), ("gla_p", (1, 1, HEADS, DK, DV)), ("pool_p", (1, 1, BUF, POOL)),
       ("mem_k", (1, 1, NMEM, AH, AHD)), ("mem_v", (1, 1, NMEM, AH, AHD)), ("gla_s", (1, 1, HEADS, DK, DV)),
       ("pool_s", (1, 1, BUF, POOL))]


def kernel(**inputs):
    import numpy as np
    import concourse.bacc as bacc
    from concourse.bass_utils import run_bass_kernel_spmd

    nc = bacc.Bacc("TRN2", target_bir_lowering=False, num_devices=1)
    arrays, a, o = {}, {}, {}
    for name in IN:
        x = np.ascontiguousarray(inputs[name])
        arrays[f"in_{name}"] = x
        a[name] = nc.dram_tensor(f"in_{name}", x.shape, mybir.dt.from_np(x.dtype), kind="ExternalInput").ap()
    for name, shape in OUT:
        o[name] = nc.dram_tensor(f"out_{name}", shape, F32, kind="ExternalOutput").ap()
    build(nc, a, o)
    r = run_bass_kernel_spmd(nc, [arrays], core_ids=[0])
    return tuple(r.results[0][f"out_{name}"] for name, _ in OUT)
```

```python
from contextlib import ExitStack, contextmanager

import concourse.bass as bass
from concourse import mybir

F32 = mybir.dt.float32
F32R = mybir.dt.float32r
I32 = mybir.dt.int32
ALU = mybir.AluOpType
ACT = mybir.ActivationFunctionType
AX = mybir.AxisListType

P = 128
D = 1024
KT = D // P
LP, LS = 256, 64
NT = LP + LS
TILES = [(0, 128), (128, 128), (256, 64)]
HEADS, DK, DV = 4, 64, 128
KW, GW = HEADS * DK, HEADS * DV
RANK = 16
CHUNK = 64
NCH = NT // CHUNK
POOL = 512
BUF = 15
UP_P, UP_S = BUF + LP, BUF + LS
UPAD = UP_P + UP_S
NMEM, AH, AHD = 256, 4, 256
E = 32
SLOTS = 64
NBLK = NT // SLOTS
EPS = 1e-6
SCORES = (0, 2, 1, 3, 4, 5)
COL = dict(q=0, k=KW, v=2 * KW, g=2 * KW + GW, r=2 * KW + 2 * GW, u=2 * KW + 2 * GW + RANK)


class Jobs:

    def __init__(self, table):
        self.job, self.order, count = {}, [], {"A": 0, "D": 0}
        for n, (name, last) in enumerate(table):
            count[last] += 1
            self.job[name] = (n, last, count[last])
            self.order.append((last, count[last]))

    def bank(self, name):
        return self.job[name][0] % 8

    def filled_at(self, name):
        return self.job[name][0] + 1

    def freed_at(self, name):
        return self.job[name][1:]

    def occupant_before(self, name):
        n = self.job[name][0]
        return self.order[n - 8] if n >= 8 else None


def job_table():
    t = [("vec", "D")]
    t += [(f"memT{i}", "A") for i in range(4)]
    t += [(f"K{i}", "A") for i in range(4)]
    t += [("bup", "D")]
    t += [(f"xT{i}", "D") for i in range(KT)]
    t += [("rms0", "D")]
    t += [(f"V{i}", "A") for i in range(4)]
    t += [(f"KTp{i}", "A") for i in range(4)]
    t += [("r", "D"), ("q0", "D"), ("q1", "D"), ("gate0", "A"), ("gate1", "A"), ("k0", "D"), ("k1", "D")]
    t += [(f"v{i}", "A") for i in range(3)]
    t += [(f"u{i}", "D") for i in range(4)]
    t += [("cum0", "D"), ("cum1", "D"), ("prevT", "A")]
    t += [(f"g{i}", "D") for i in range(4)]
    t += [("klT0", "A"), ("klT1", "A")]
    t += [(f"AT{i}", "D") for i in range(3)]
    t += [(f"ds{c}", "D") for c in range(NCH)]
    t += [(f"KTs{i}", "A") for i in range(4)]
    t += [(f"o{i}", "D") for i in range(3)]
    t += [(f"pool{i}", "D") for i in range(4)]
    t += [("hist0", "A"), ("hist1", "A")]
    t += [(f"oT{i}", "D") for i in range(4)]
    t += [(f"out{i}", "D") for i in range(KT)]
    t += [(f"mq{i}", "D") for i in range(KT)] + [("rms1", "D")]
    t += [(f"s{i}", "A") for i in SCORES]
    t += [(f"PT{i}", "D") for i in range(5)]
    t += [(f"PV{i}", "D") for i in range(5)]
    t += [(f"mo{i}", "D") for i in range(KT)]
    t += [("router", "D")]
    t += [(f"x2_{i}", "A") for i in range(6)]
    t += [("rank", "D")]
    return t


def build(nc, a, o):
    J = Jobs(job_table())
    with ExitStack() as ctx:
        sems = {}

        def S(name):
            if name not in sems:
                sems[name] = ctx.enter_context(nc.semaphore(name))
            return sems[name]

        ps = ctx.enter_context(nc.psum_tensor("ps", [P, 8, 512], F32))
        REGIONS = (("A", 0, 16384), ("B", 16384, 16384), ("D", 32768, 8192), ("P", 40960, 12248))
        region = []
        for name, at, n in REGIONS:
            offset = -(-nc.sbuf_base // 32) * 32
            plain = ctx.enter_context(nc.sbuf_tensor("region" + name, [P, n], F32))
            region.append((at, n, plain, nc.alloc_sbuf_tensor_at("rounded" + name, [P, n], F32R, offset=offset)))

        def place(at, n, which):
            for start, size, *tensors in region:
                if start <= at < start + size:
                    assert at + n <= start + size
                    return tensors[which][:, at - start:at - start + n]

        def reg(at, n):
            return place(at, n, 0)

        def parts(at, n, k=KT):
            return place(at, n, 1).rearrange("p (k f) -> p k f", k=k)

        RA, RB0, RB1, RD, RP = 0, 16384, 24576, 32768, 40960
        upA = reg(RA, 16384).rearrange("p (k f) -> p k f", k=KT)
        upB = reg(RB0, 16384).rearrange("p (k f) -> p k f", k=KT)
        wdn = reg(RD, 8192).rearrange("p (k f) -> p k f", k=KT)
        wlast = reg(RA + 8192, 8192).rearrange("p (k f) -> p k f", k=KT)
        c = RP
        def take(n):
            nonlocal c
            r = reg(c, n); c += n
            return r
        ident, iota = take(128), take(128)
        OH_at = c
        tri, ones, below = take(128), take(128), take(128)
        bupT = take(E * 16).rearrange("p (e f) -> p e f", e=E)
        GT_at = c
        wr = take(KT * E).rearrange("p (k e) -> p k e", k=KT)
        gwr = take(KT * E).rearrange("p (k e) -> p k e", k=KT)
        vec = take(40)
        small = take(152)
        brout = take(E)
        g_mix, g_memq, g_memkv, g_moe = (vec[:, 8 * i:8 * i + 8] for i in range(4))
        g_gla, pscale = vec[:, 32:36], vec[:, 36:40]
        XT_at = c; xT = take(2560).rearrange("p (k t) -> p k t", k=KT)
        GX_at = c; take(2560)
        CAT_at = c; catT = take(2560).rearrange("p (k t) -> p k t", k=KT)
        SP_at = c
        upad = take(4 * UPAD).rearrange("p (g t) -> p g t", g=4)
        rstdb = take(NT)
        rT = take(NT)
        wgate = take(KW)
        WR_at = c; wr_col = take(KT * RANK).rearrange("p (k c) -> p k c", k=KT)
        WRH_at = c; take(KT * RANK)
        ssx, ssm = small[:, 0:3], small[:, 3:5]
        rsx, rsm = small[:, 5:8], small[:, 8:10]
        sso = small[:, 10:22].rearrange("p (i h) -> p i h", i=3)
        rso = small[:, 22:34].rearrange("p (i h) -> p i h", i=3)
        mx = small[:, 34:46]
        nmx = small[:, 46:58]
        rs = small[:, 58:70]
        rinv = small[:, 70:82]
        ss2, rs2 = small[:, 82:88], small[:, 88:91]
        top8 = small[:, 91:115].rearrange("p (i k) -> p i k", i=3)
        nt1 = small[:, 115:118]
        gsum = small[:, 118:121]
        nover = small[:, 121:122]
        over_i = small[:, 122:123].bitcast(I32)
        sst = small[:, 123:129]
        ms1, rs1, rs1p, rs1n = (small[:, 132 + 3 * i:135 + 3 * i] for i in range(4))
        xtok = reg(RB1, 3072).rearrange("p (i d) -> p i d", i=3)
        mem = reg(RB1 + 3072, 2048).rearrange("p (i d) -> p i d", i=2)
        memT = reg(RB1 + 5120, 2048).rearrange("p (k m) -> p k m", k=KT)
        memH, memL = parts(RB1 + 3072, 2048), parts(RB1 + 5120, 2048)
        wmkH, wmkL = parts(RA, 8192), parts(RB0, 8192)
        wmvH, wmvL = parts(RA + 8192, 8192), parts(RD, 8192)
        wrH, wrL = parts(WRH_at, KT * RANK), parts(WR_at, KT * RANK)
        qkH, qkL = parts(RD, 4096), parts(RA, 4096)
        vH, vL = parts(RD + 4096, 4096), parts(RA + 4096, 4096)
        gH, gL = parts(RD + 4096, 4096), parts(RA + 8192, 4096)
        uH, uL = parts(RD, 4096), parts(RA + 12288, 4096)
        mixL = parts(RB0, 2560)
        Vp = reg(RB1, 2048).rearrange("p (i d) -> p i d", i=2)
        Kp = reg(CAT_at, 2048).rearrange("p (i d) -> p i d", i=2)
        KTp = reg(RB1 + 3072, 2048).rearrange("p (k m) -> p k m", k=KT)
        Vs = reg(RB1 + 5120, 2048).rearrange("p (i d) -> p i d", i=2)
        Sbuf = [reg(RB1 + 2048 + 256 * i, 256) for i in range(4)] + [reg(RB1 + 7168 + 256 * i, 256) for i in range(3)]
        Sbuf = [s.rearrange("p (r e) -> p r e", r=2) for s in Sbuf]
        wmk = reg(RB0, 8192).rearrange("p (k f) -> p k f", k=KT)
        wmv = reg(RD, 8192).rearrange("p (k f) -> p k f", k=KT)
        Ks = reg(RB0, 2048).rearrange("p (i d) -> p i d", i=2)
        KTs = reg(RB0 + 2048, 2048).rearrange("p (k m) -> p k m", k=KT)
        sgT = reg(RB0 + 4096, 1280).rearrange("p (g t) -> p g t", g=4)
        vtok = reg(RB0 + 5376, 1536).rearrange("p (i d) -> p i d", i=3)
        qT = reg(RB0 + 6912, 640).rearrange("p (r t) -> p r t", r=2)
        kT = reg(RB0 + 7552, 640).rearrange("p (r t) -> p r t", r=2)
        w_qk = reg(RA, 4096).rearrange("p (k f) -> p k f", k=KT)
        w_v = reg(RA + 4096, 4096).rearrange("p (k f) -> p k f", k=KT)
        w_g = reg(RA + 8192, 4096).rearrange("p (k f) -> p k f", k=KT)
        w_u = reg(RA + 12288, 4096).rearrange("p (k f) -> p k f", k=KT)
        la0 = reg(CAT_at, 768).rearrange("p (i f) -> p i f", i=3)
        la1 = reg(CAT_at + 768, 768).rearrange("p (i f) -> p i f", i=3)
        at = RA
        def takeA(n):
            nonlocal at
            r = reg(at, n); at += n
            return r
        bT = takeA(640).rearrange("p (r t) -> p r t", r=2)
        eb = takeA(640).rearrange("p (r t) -> p r t", r=2)
        enb = takeA(640).rearrange("p (r t) -> p r t", r=2)
        ebl = takeA(640).rearrange("p (r t) -> p r t", r=2)
        kdT = takeA(640).rearrange("p (r t) -> p r t", r=2)
        qdz = takeA(1280).rearrange("p (h t) -> p h t", h=4)
        klz = takeA(1280).rearrange("p (c f) -> p c f", c=5)
        AT = takeA(1536).rearrange("p (i h t) -> p i h t", i=3, h=4)
        assert at <= 8192
        otok = reg(RA + 8192, 1536).rearrange("p (i d) -> p i d", i=3)
        osq = reg(RA + 9728, 1536).rearrange("p (i d) -> p i d", i=3)
        hist = reg(RA + 11264, 1024).rearrange("p (i d) -> p i d", i=2)
        s_a = reg(RA + 12288, 4 * UPAD).rearrange("p (g t) -> p g t", g=4)
        s_b = reg(RA + 12288 + 4 * UPAD, 4 * UPAD).rearrange("p (g t) -> p g t", g=4)
        invn = reg(RA + 12288 + 8 * UPAD, 4 * NT).rearrange("p (g t) -> p g t", g=4)
        poolw = reg(GX_at, 512).rearrange("p (g f) -> p g f", g=4)
        smallrows = reg(RB1 + 7168, 128)
        buprow = reg(GX_at, 2048)
        prevrow = reg(RB1 + 7168 + 256, 512)
        rT_diag = reg(CAT_at + 2048, 384).rearrange("p (i t) -> p i t", i=3)
        sgT_f = reg(RB0 + 4096, 1280)
        sgT_e = reg(RA + 9728, 1280)
        sq1 = reg(SP_at, 2560).rearrange("p (k t) -> p k t", k=KT)
        sq2 = reg(GX_at, 2560).rearrange("p (k t) -> p k t", k=KT)
        aqT = reg(RB0 + 4096, 2560).rearrange("p (k t) -> p k t", k=KT)
        probs_p = reg(RB0, 2048).rearrange("p (l h m) -> p l h m", l=2, h=4)
        probs_s = reg(RB0 + 6656, 1024).rearrange("p (h m) -> p h m", h=4)
        PTs = reg(RB0 + 7680, 512).rearrange("p (h i l) -> p h i l", h=4, i=2)
        PTp = reg(GX_at, 2048).rearrange("p (h i l) -> p h i l", h=4, i=2)
        wsq = reg(RD, 8192).rearrange("p (c k f) -> p c k f", c=4, k=KT)
        wsqH = [parts(RA + w, 2048) for w in (0, 2048, 12288, 14336)]
        wsqL = [parts(RD + 2048 * c_, 2048) for c_ in range(4)]
        catH, catL = parts(RA + 4096, 2560), parts(CAT_at, 2560)
        gxH, gxL = parts(GX_at, 2560), parts(RA + 8192, 2560)
        aoH, aoL = catL, catH
        Hm = reg(GX_at, 3072).rearrange("p (i d) -> p i d", i=3)
        acc = reg(GX_at + 3072, 3072).rearrange("p (i d) -> p i d", i=3)
        x_at = GX_at + 6144
        glu = reg(x_at, 512).rearrange("p (k s) -> p k s", k=KT)
        Y = reg(x_at + 512, 1024)
        U = reg(XT_at, 1024)
        sg = U[:, 0:512].rearrange("p (k s) -> p k s", k=KT)
        lin = reg(XT_at + 1024, 512).rearrange("p (k s) -> p k s", k=KT)
        XG = reg(XT_at + 1536, 512)
        XTe = reg(XT_at + 2048, 512).rearrange("p (q h s) -> p q h s", q=4, h=2)
        OH = reg(OH_at, 384).rearrange("p (i s) -> p i s", i=3)
        GT = reg(GT_at, NT)
        rankx = reg(GT_at + NT, 96).rearrange("p (i e) -> p i e", i=3)
        Gm = reg(GT_at + NT + 96, 96).rearrange("p (i e) -> p i e", i=3)
        gate_col = small[:, 130:131]
        logit = reg(x_at, 96).rearrange("p (i e) -> p i e", i=3)
        sel = reg(x_at + 96, 96).rearrange("p (i e) -> p i e", i=3)
        gpad = reg(x_at + 192, 288).rearrange("p (i e) -> p i e", i=3)
        work = reg(x_at + 512, 96).rearrange("p (i e) -> p i e", i=3)
        topi = reg(x_at + 608, 24).bitcast(mybir.dt.uint32).rearrange("p (i k) -> p i k", i=3)
        topf = reg(x_at + 640, 24).rearrange("p (i k) -> p i k", i=3)
        bdrow = acc[64:96, 2, :]
        nfinal = reg(RA, D)
        wide2 = reg(RA + D, D)
        GtT = Y[64:96, 0:NT]

        filled, freed = S("bank_filled"), {"A": S("bank_read_by_act"), "D": S("bank_read_by_dve")}

        def took(eng, name):
            eng.wait_ge(filled, J.filled_at(name))

        def has(eng, name):
            last, n = J.freed_at(name)
            eng.wait_ge(freed[last], n)

        columns = [slice(128 * j, 128 * j + 128) for j in range(4)]
        every = slice(0, KT)
        split = [("r", wr_col, wrH, wrL, every, slice(0, RANK))]
        split += [("qk", w_qk, qkH, qkL, every, f) for f in columns]
        split += [("v", w_v, vH, vL, slice(2 * i, 2 * i + 2), slice(0, GW)) for i in range(4)]
        split += [("u", w_u, uH, uL, every, f) for f in columns]
        split += [("g", w_g, gH, gL, every, f) for f in columns]
        split_at = {name: [n + 1 for n, x in enumerate(split) if x[0] == name] for name in ("r", "qk", "v", "u", "g")}

        def high(act, part, whole):
            return act.activation(part, whole, ACT.Copy)

        def low(dve, part, whole, upper):
            return dve.tensor_tensor(part, whole, upper.bitcast(F32), ALU.subtract)

        def product3(pe, out, lhs, rhs, start, stop):
            (lh, ll), (rh, rl) = lhs, rhs
            for n, (l_, r_) in enumerate(((lh, rl), (ll, rh), (lh, rh))):
                ins = pe.matmul(out, l_, r_, start=start and n == 0, stop=stop and n == 2)
            return ins

        def bank(name, n=512, rows=P):
            return ps[0:rows, J.bank(name), 0:n]

        PAIRS = E // 2

        def up_src(e):
            src = a["w_up"][0]
            src = src[bass.ds(e, 1)] if not isinstance(e, int) else src[e:e + 1]
            return src.rearrange("a (k p) f -> p (a k) f", p=P)

        def down_src(e):
            src = a["w_down"][0]
            src = src[bass.ds(e, 1)] if not isinstance(e, int) else src[e:e + 1]
            return src.rearrange("a (k p) f -> p (a k) f", p=P)

        def over_experts(eng, one):
            one(0, 0, 0, True, False)
            one(1, 1, 0, False, False)
            with eng.Fori(1, PAIRS - 2) as i:
                for h in range(2):
                    one(i * 2 + h, h, i, False, False)
            one(E - 4, 0, PAIRS - 2, False, False)
            one(E - 3, 1, PAIRS - 2, False, False)
            one(E - 2, 0, PAIRS - 1, False, False)
            one(E - 1, 1, PAIRS - 1, False, True)

        @contextmanager
        def overflowing(eng):
            eng.wait_ge(S("overflow"), 1)
            with eng.If(eng.value_load(over_i[0:1, 0:1], min_val=0, max_val=1) > 0):
                yield

        def block_counts(e, b):
            n = b - 1
            return E + e * (NBLK - 1) + n, n % 2, PAIRS + e * ((NBLK - 1) // 2) + n // 2

        def moe_sync(sp):
            def one(e, h, pair, first, last):
                if isinstance(e, int) and e + 2 >= E:
                    return
                for c_ in range(4):
                    if isinstance(e, int) and e == E - 3 and c_ == 1:
                        sp.wait_ge(S("down_done"), e * 2)
                    sp.wait_ge(S("up_done"), e * 4 + c_ + 1)
                    sp.dma_start((upA, upB)[h][:, 2 * c_:2 * c_ + 2, :], up_src(e + 2)[:, 2 * c_:2 * c_ + 2, :]
                                 ).then_inc(S(f"up{'AB'[h]}_in{c_}"), 16)
            over_experts(sp, one)
            sp.wait_ge(S("up_done"), (E - 1) * 4)
            for c_ in range(2):
                sp.dma_start(wlast[:, 4 * c_:4 * c_ + 4, :], down_src(E - 1)[:, 4 * c_:4 * c_ + 4, :]
                             ).then_inc(S(f"last_down_in{c_}"), 16)
            with overflowing(sp):
                sp.wait_ge(S("down_done"), E * 2)
                with sp.Fori(0, E) as e:
                    for c_ in range(4):
                        sp.wait_ge(S("up_done"), (E + e * (NBLK - 1)) * 4)
                        sp.dma_start(upA[:, 2 * c_:2 * c_ + 2, :], up_src(e)[:, 2 * c_:2 * c_ + 2, :]
                                     ).then_inc(S(f"upA_in{c_}"), 16)
                    sp.wait_ge(S("down_done"), (E + e * (NBLK - 1)) * 2)
                    for c_ in range(2):
                        sp.dma_start(wdn[:, 4 * c_:4 * c_ + 4, :], down_src(e)[:, 4 * c_:4 * c_ + 4, :]
                                     ).then_inc(S(f"down_in{c_}"), 16)
                sp.wait_ge(S("up_done"), E * NBLK * 4)
            sp.dma_start(nfinal, a["norm_final"].rearrange("(a d) -> a d", a=1).broadcast_to([P, D])).then_inc(S("nf_in"), 16)
            for i, (t0, n) in enumerate(TILES):
                sp.wait_ge(S("y"), i + 1)
                dst = o["y_p"][0, t0:t0 + n, :] if i < 2 else o["y_s"][0]
                sp.dma_start(dst, acc[0:n, i, :]).then_inc(S("y_out"), 16)
            sp.wait_ge(S("y_out"), 48)
            sp.wait_ge(S("k_out"), 16)
            sp.wait_ge(S("v_out"), 16)
            sp.wait_ge(S("states_out"), 32)
            sp.wait_ge(S("hist_out"), 32)

        def gather(pe, at_bank, h):
            for i in range(3):
                for hd in range(2):
                    ins = pe.matmul(ps[64 * hd:64 * hd + 64, at_bank, :], OH[:, i, SLOTS * h:SLOTS * h + SLOTS],
                                    Hm[:, i, 512 * hd:512 * hd + 512], start=(i == 0), stop=(i == 2))
            return ins

        def gather_turn(pe, at_bank):
            for q in range(4):
                ins = pe.transpose(ps[:, at_bank, 128 * q:128 * q + 128], XG[:, 128 * q:128 * q + 128], ident[:, :])
            return ins

        def slots_turn(pe, at_bank, e, ne):
            for i, (t0, n) in enumerate(TILES):
                pe.transpose(ps[:, at_bank, t0:t0 + n], OH[0:n, i, :], ident[0:n, 0:n])
            for i in range(3):
                g = Gm[:, i, e:e + ne] if isinstance(e, int) else Gm[:, i, bass.ds(e, ne)]
                ins = pe.matmul(ps[:, at_bank, NT:NT + ne], OH[:, i, :], g, start=(i == 0), stop=(i == 2))
            return ins

        def up_product(pe, w, k0, nk):
            for k in range(k0, k0 + nk):
                for n_ in range(2):
                    for half in range(2):
                        ins = pe.matmul(ps[64 * half:64 * half + 64, n_, :], XTe[:, k % 4, k // 4, :],
                                        w[:, k, 1024 * half + 512 * n_:1024 * half + 512 * n_ + 512],
                                        start=(k == 0), stop=(k == KT - 1))
            return ins

        def up_turn(pe, f0, nf):
            for f in range(f0, f0 + nf):
                ins = pe.transpose(ps[:, 2 + f // 4, 128 * (f % 4):128 * (f % 4) + 128], U[:, 128 * f:128 * f + 128],
                                   ident[:, :])
            return ins

        def down_product(pe, w, k0, nk):
            for k in range(k0, k0 + nk):
                for n_ in range(2):
                    ins = pe.matmul(ps[64 * n_:64 * n_ + 64, 6, :], lin[:, k, :],
                                    w[:, k, 512 * n_:512 * n_ + 512], start=(k == 0), stop=(k == KT - 1))
            return ins

        def combine(pe, i, at_bank=4):
            t0, n = TILES[i]
            for n_ in range(2):
                ins = pe.matmul(ps[0:n, at_bank + n_, :], GT[:, t0:t0 + n], Y[:, 512 * n_:512 * n_ + 512],
                                start=True, stop=True)
            return ins

        def down_bias(pe, i):
            t0, n = TILES[i]
            for n_ in range(2):
                ins = pe.matmul(ps[0:n, 4 + n_, :], GtT[:, t0:t0 + n], bdrow[:, 512 * n_:512 * n_ + 512],
                                start=True, stop=True)
            return ins

        def moe_tensor(pe):
            has(pe, "x2_5"), has(pe, "rank")
            pe.wait_ge(S("slots"), 1)
            pe.wait_ge(S("Hm"), 3)
            pe.wait_ge(S("moe_zero"), 2)
            gather(pe, 6, 0).then_inc(S("gathered"), 1)
            pe.wait_ge(S("gather_read"), 1)
            gather_turn(pe, 7).then_inc(S("gather_turned"), 1)

            def down(e, last):
                pe.wait_ge(S("act"), e + 1)
                for c_ in range(2):
                    if last:
                        pe.wait_ge(S(f"last_down_in{c_}"), 16)
                    else:
                        pe.wait_ge(S(f"down_in{c_}"), (e + 1) * 16)
                    down_product(pe, wlast if last else wdn, 4 * c_, 4).then_inc(S("down_done"), 1)

            def one(e, h, pair, first, last):
                second = isinstance(e, int) and e == 1
                rows = down_bias if second else combine if h == 0 and not first else None
                pe.wait_ge(S("tokens_in"), e + 1)
                if h == 1:
                    if second:
                        pe.wait_ge(S("Gm"), 3)
                    slots_turn(pe, 7, e - 1, 2).then_inc(S("slots_turned"), 1)
                if not first:
                    pe.wait_ge(S("up_read"), e)
                for c_ in range(4):
                    pe.wait_ge(S(f"up{'AB'[h]}_in{c_}"), (pair + 1) * 16)
                    up_product(pe, (upA, upB)[h], 2 * c_, 2).then_inc(S("up_done"), 1)
                if first:
                    pe.wait_ge(S("gates"), 3)
                    for i, (t0, n) in enumerate(TILES):
                        ins = pe.transpose(ps[0:96, 4, t0:t0 + n], gpad[0:n, i, :], ident[0:n, 0:n])
                    ins.then_inc(S("gates_turned"), 1)
                else:
                    down(e - 1, False)
                    pe.wait_ge(S("act"), e)
                pe.wait_ge(S("up_read"), e + 1)
                up_turn(pe, 0, KT).then_inc(S("up_turned"), 1)
                if second:
                    pe.wait_ge(S("GtT"), 1)
                    pe.wait_ge(S("bdown_in"), 16)
                if not first:
                    pe.wait_ge(S("y_read"), e)
                if rows:
                    if not second:
                        pe.wait_ge(S("combined"), pair * 3)
                    rows(pe, 0).then_inc(S("combine"), 1)
                count = 0 if second else pair * 3
                if not last:
                    if h == 1:
                        pe.wait_ge(S("slots"), pair + 2)
                    gather(pe, 6, 1 - h).then_inc(S("gathered"), 1)
                if rows:
                    pe.wait_ge(S("combined"), count + 1)
                    rows(pe, 1).then_inc(S("combine"), 1)
                if not last:
                    pe.wait_ge(S("gather_read"), e + 2)
                    if h == 1:
                        pe.wait_ge(S("slots_read"), pair + 1)
                    gather_turn(pe, 7).then_inc(S("gather_turned"), 1)
                if rows:
                    pe.wait_ge(S("combined"), count + 2)
                    rows(pe, 2).then_inc(S("combine"), 1)
            over_experts(pe, one)
            down(E - 1, True)
            pe.wait_ge(S("y_read"), E)
            pe.wait_ge(S("combined"), PAIRS * 3)
            for i in range(3):
                combine(pe, i, 4 - 2 * i).then_inc(S("combine"), 1)
            with overflowing(pe), pe.Fori(0, E) as e:
                for b in range(1, NBLK):
                    n, h, pair = block_counts(e, b)
                    if h == 0:
                        pe.wait_ge(S("slots"), pair + 1)
                        slots_turn(pe, 7, e, 1).then_inc(S("slots_turned"), 1)
                        pe.wait_ge(S("slots_read"), pair + 1)
                    gather(pe, 6, h).then_inc(S("gathered"), 1)
                    pe.wait_ge(S("gather_read"), n + 1)
                    gather_turn(pe, 7).then_inc(S("gather_turned"), 1)
                    pe.wait_ge(S("tokens_in"), n + 1)
                    pe.wait_ge(S("combined"), pair * 3 + 3)
                    for c_ in range(4):
                        if b == 1:
                            pe.wait_ge(S(f"upA_in{c_}"), (PAIRS + 1 + e) * 16)
                        up_product(pe, upA, 2 * c_, 2).then_inc(S("up_done"), 1)
                    pe.wait_ge(S("up_read"), n + 1)
                    up_turn(pe, 0, KT).then_inc(S("up_turned"), 1)
                    pe.wait_ge(S("act"), n + 1)
                    for c_ in range(2):
                        if b == 1:
                            pe.wait_ge(S(f"down_in{c_}"), (E + e) * 16)
                        down_product(pe, wdn, 4 * c_, 4).then_inc(S("down_done"), 1)
                    pe.wait_ge(S("y_read"), n + 1)
                    if h == 1:
                        for i in range(3):
                            combine(pe, i, 4 - 2 * i).then_inc(S("combine"), 1)

        def moe_act(act):
            def slots_read(pair, upper):
                for half in range(2):
                    col = NT + (upper if half else 0)
                    act.activation(gate_col[64 * half:64 * half + 64, :], ps[64 * half:64 * half + 64, 7, col:col + 1],
                                   ACT.Copy).then_inc(S("gate_col"), 1)
                act.wait_ge(S("gate_col"), pair * 2 + 2)
                act.activation(GT[:, :], ps[:, 7, 0:NT], ACT.Copy, scale=gate_col).then_inc(S("slots_read"), 1)

            def rows_read(h):
                for n_ in range(2):
                    ins = act.activation(Y[64 * h:64 * h + 64, 512 * n_:512 * n_ + 512], ps[64 * n_:64 * n_ + 64, 6, :],
                                         ACT.Copy)
                ins.then_inc(S("y_read"), 1)

            act.wait_ge(S("gathered"), 1)
            act.activation(XG[:, :], ps[:, 6, :], ACT.Copy).then_inc(S("gather_read"), 1)

            def one(e, h, pair, first, last):
                if h == 1:
                    act.wait_ge(S("slots_turned"), pair + 1)
                    if not isinstance(e, int) or e > 1:
                        act.wait_ge(S("combine"), pair * 3 + 3)
                    slots_read(pair, 1)
                if not first:
                    act.wait_ge(S("act"), e)
                act.wait_ge(S("up_done"), (e + 1) * 4)
                act.activation(U[:, :], ps[:, 0:2, :].rearrange("p b f -> p (b f)"), ACT.Copy).then_inc(S("up_read"), 1)
                if first:
                    act.wait_ge(S("gates_turned"), 1)
                    act.activation(GtT, ps[64:96, 4, 0:NT], ACT.Copy).then_inc(S("GtT"), 1)
                else:
                    def load_down(c_):
                        act.dma_start(wdn[:, 4 * c_:4 * c_ + 4, :], down_src(e)[:, 4 * c_:4 * c_ + 4, :]
                                      ).then_inc(S(f"down_in{c_}"), 16)
                    if not last:
                        act.wait_ge(S("down_done"), e * 2 - 1)
                        load_down(0)
                    act.wait_ge(S("down_done"), e * 2)
                    if isinstance(e, int) and e == 2:
                        act.wait_ge(S("combine"), 3)
                    rows_read(1 - h)
                    if not last:
                        load_down(1)
                if not last:
                    act.wait_ge(S("gathered"), e + 2)
                    act.activation(XG[:, :], ps[:, 6, :], ACT.Copy).then_inc(S("gather_read"), 1)
                act.wait_ge(S("glu"), e * 2 + 2)
                act.activation(sg, glu, ACT.Sigmoid, scale=1.702).then_inc(S("sigmoid"), 1)
            over_experts(act, one)
            act.wait_ge(S("down_done"), E * 2)
            rows_read(1)
            with overflowing(act), act.Fori(0, E) as e:
                for b in range(1, NBLK):
                    n, h, pair = block_counts(e, b)
                    if h == 0:
                        act.wait_ge(S("slots_turned"), pair + 1)
                        slots_read(pair, 0)
                    act.wait_ge(S("gathered"), n + 1)
                    act.activation(XG[:, :], ps[:, 6, :], ACT.Copy).then_inc(S("gather_read"), 1)
                    act.wait_ge(S("up_done"), (n + 1) * 4)
                    act.activation(U[:, :], ps[:, 0:2, :].rearrange("p b f -> p (b f)"), ACT.Copy).then_inc(S("up_read"), 1)
                    act.wait_ge(S("glu"), n * 2 + 2)
                    act.activation(sg, glu, ACT.Sigmoid, scale=1.702).then_inc(S("sigmoid"), 1)
                    act.wait_ge(S("down_done"), (n + 1) * 2)
                    rows_read(h)
                    if h == 1:
                        act.wait_ge(S("combined"), pair * 3 + 6)
            for i, (t0, n) in enumerate(TILES):
                act.wait_ge(S("combined"), PAIRS * 3 + i + 1)
                act.activation(wide2[0:n, :], acc[0:n, i, :], ACT.Square, accum_out=ss2[0:n, 3 + i:4 + i]).then_inc(S("ssq3"), 1)
                act.wait_ge(S("meansq3"), i + 1)
                act.activation(rs2[0:n, i:i + 1], rs2[0:n, i:i + 1], ACT.Sqrt).then_inc(S("root3"), 1)

        def moe_dve(dve):
            def slots(halves):
                for h, (e, block) in enumerate(halves):
                    for i in range(3):
                        r = rankx[:, i, e:e + 1] if isinstance(e, int) else rankx[:, i, bass.ds(e, 1)]
                        ins = dve.tensor_scalar(OH[:, i, SLOTS * h:SLOTS * h + SLOTS], iota[:, 0:SLOTS],
                                                float(SLOTS * block), r, ALU.add, ALU.is_equal)
                ins.then_inc(S("slots"), 1)

            def swiglu(e, n, down_done):
                u = ps[:, 2:4, :].rearrange("p b (k s) -> p (b k) s", s=P)
                be = bupT[:, e, :] if isinstance(e, int) else bupT[:, bass.ds(e, 1), :].rearrange("p e f -> p (e f)")
                dve.tensor_tensor(glu, u[:, :, 0:SLOTS], be[:, 0:8].unsqueeze(2).broadcast_to([P, KT, SLOTS]),
                                  ALU.add).then_inc(S("glu"), 1)
                if down_done is not None:
                    dve.wait_ge(S("down_done"), down_done * 2)
                dve.tensor_tensor(lin, u[:, :, SLOTS:P], be[:, 8:16].unsqueeze(2).broadcast_to([P, KT, SLOTS]),
                                  ALU.add).then_inc(S("lin"), 1)
                dve.wait_ge(S("glu"), n * 2 + 1)
                dve.tensor_scalar(glu, glu, 7.0, None, ALU.min).then_inc(S("glu"), 1)
                dve.wait_ge(S("lin"), n * 3 + 1)
                dve.tensor_scalar(lin, lin, 7.0, -7.0, ALU.min, ALU.max).then_inc(S("lin"), 1)
                dve.wait_ge(S("glu"), n * 2 + 2)
                dve.wait_ge(S("lin"), n * 3 + 2)
                dve.scalar_tensor_tensor(lin, lin, 1.0, glu, ALU.add, ALU.mult).then_inc(S("lin"), 1)

            def swiglu_end(n):
                dve.wait_ge(S("lin"), n * 3 + 3)
                dve.wait_ge(S("sigmoid"), n + 1)
                dve.tensor_tensor(lin, lin, sg, ALU.mult).then_inc(S("act"), 1)

            def tokens():
                g = g_moe.rearrange("p (h q) -> p q h", h=2).unsqueeze(3).broadcast_to([P, 4, 2, SLOTS])
                return dve.tensor_tensor(XTe, ps[:, 7, :].rearrange("p (q h s) -> p q h s", q=4, h=2), g, ALU.mult)

            dve.wait_ge(S("rankx"), 3)
            slots([(0, 0), (1, 0)])
            dve.tensor_reduce(nover, rankx.rearrange("p i e -> p (i e)"), AX.X, ALU.max).then_inc(S("rank_max"), 1)
            dve.wait_ge(S("gather_turned"), 1)
            tokens().then_inc(S("tokens_in"), 1)
            dve.wait_ge(S("gate_e"), 3)
            for i, (t0, n) in enumerate(TILES):
                dve.tensor_tensor(gpad[0:n, i, 64:96], gpad[0:n, i, 64:96], sel[0:n, i, :], ALU.mult).then_inc(S("gsel"), 1)
            dve.wait_ge(S("gsel"), 3)
            dve.tensor_reduce(gsum[:, :], gpad[:, :, 64:96], AX.X, ALU.add).then_inc(S("gsel"), 1)
            dve.wait_ge(S("gsel"), 4)
            dve.reciprocal(gsum[:, 0:2], gsum[:, 0:2]).then_inc(S("gsel"), 1)
            dve.reciprocal(gsum[0:64, 2:3], gsum[0:64, 2:3]).then_inc(S("gsel"), 1)
            dve.wait_ge(S("gsel"), 6)
            for i, (t0, n) in enumerate(TILES):
                dve.tensor_scalar(gpad[0:n, i, 64:96], gpad[0:n, i, 64:96], gsum[0:n, i:i + 1], None,
                                  ALU.mult).then_inc(S("gates"), 1)
            dve.wait_ge(S("gates"), 3)
            for i, (t0, n) in enumerate(TILES):
                dve.tensor_copy(Gm[0:n, i, :], gpad[0:n, i, 64:96]).then_inc(S("Gm"), 1)
            dve.wait_ge(S("nover"), 1)
            dve.tensor_scalar(over_i, small[:, 131:132], float(SLOTS) - 0.5, None, ALU.is_gt).then_inc(S("overflow"), 1)

            def one(e, h, pair, first, last):
                second = isinstance(e, int) and e == 1
                rows = second or (h == 0 and not first)
                if h == 1 and not last:
                    dve.wait_ge(S("slots_turned"), pair + 1)
                    dve.wait_ge(S("gathered"), e + 1)
                    slots([(e + 1, 0), (e + 2, 0)])
                def combined(i):
                    dve.wait_ge(S("combine"), (0 if second else pair * 3) + i + 1)
                    n = TILES[i][1]
                    dve.tensor_tensor(acc[0:n, i, :], ps[0:n, 4:6, :].rearrange("p b f -> p (b f)"), acc[0:n, i, :],
                                      ALU.add).then_inc(S("combined"), 1)
                if first:
                    dve.wait_ge(S("Gm"), 3)
                    dve.wait_ge(S("gates_turned"), 1)
                dve.wait_ge(S("up_turned"), e + 1)
                swiglu(e, e, None if first else e)
                if rows:
                    combined(0)
                    combined(1)
                if not last:
                    dve.wait_ge(S("gather_turned"), e + 2)
                    dve.wait_ge(S("up_done"), (e + 1) * 4)
                    tokens().then_inc(S("tokens_in"), 1)
                swiglu_end(e)
                if rows:
                    combined(2)
            over_experts(dve, one)
            for i, (t0, n) in enumerate(TILES):
                dve.wait_ge(S("combine"), PAIRS * 3 + i + 1)
                dve.tensor_tensor(acc[0:n, i, :], ps[0:n, 4 - 2 * i:6 - 2 * i, :].rearrange("p b f -> p (b f)"), acc[0:n, i, :],
                                  ALU.add).then_inc(S("combined"), 1)
            with overflowing(dve), dve.Fori(0, E) as e:
                for b in range(1, NBLK):
                    n, h, pair = block_counts(e, b)
                    if h == 0:
                        slots([(e, b), (e, b + 1)])
                    dve.wait_ge(S("gather_turned"), n + 1)
                    tokens().then_inc(S("tokens_in"), 1)
                    dve.wait_ge(S("up_turned"), n + 1)
                    swiglu(e, n, None)
                    swiglu_end(n)
                    if h == 1:
                        for i, (t0, rows) in enumerate(TILES):
                            dve.wait_ge(S("combine"), pair * 3 + 3 + i + 1)
                            dve.tensor_tensor(acc[0:rows, i, :], ps[0:rows, 4 - 2 * i:6 - 2 * i, :].rearrange("p b f -> p (b f)"),
                                              acc[0:rows, i, :], ALU.add).then_inc(S("combined"), 1)
                        dve.wait_ge(S("combined"), pair * 3 + 6)
            for i, (t0, n) in enumerate(TILES):
                dve.wait_ge(S("ssq3"), i + 1)
                dve.tensor_scalar(rs2[0:n, i:i + 1], ss2[0:n, 3 + i:4 + i], 1.0 / D, EPS, ALU.mult, ALU.add).then_inc(S("meansq3"), 1)
                dve.wait_ge(S("root3"), i + 1)
                dve.reciprocal(rs2[0:n, i:i + 1], rs2[0:n, i:i + 1]).then_inc(S("rstd3"), 1)
                dve.wait_ge(S("rstd3"), i + 1)
                dve.wait_ge(S("nf_in"), 16)
                dve.scalar_tensor_tensor(acc[0:n, i, :], acc[0:n, i, :], rs2[0:n, i:i + 1], nfinal[0:n, :],
                                         ALU.mult, ALU.mult).then_inc(S("y"), 1)

        block = ctx.enter_context(nc.Block())

        @block.sync
        def _(sp):
            def load(dst, src, name):
                sp.dma_start(dst, src).then_inc(S(name), 16)

            win = a["w_in"][0].rearrange("(k p) f -> p k f", p=P)

            def wcols(w, c0, n):
                return w[0].rearrange("(k p) f -> p k f", p=P)[:, :, c0:c0 + n]

            def wrows(w, k0, n):
                return w[0].rearrange("(k p) f -> p k f", p=P)[:, k0:k0 + n, :]

            load(mem[:, :, :], a["mem_prompt"][0].rearrange("(i p) d -> p i d", p=P), "mem_in")
            sp.wait_ge(S("vec_in"), 96)
            for i in range(4):
                load(wmk[:, 2 * i:2 * i + 2, :], wrows(a["w_mk"], 2 * i, 2), f"wmk_in{i}")
            load(xtok[:, 0:2, :], a["x_prompt"][0].rearrange("(i p) d -> p i d", p=P), "x_in")
            load(xtok[0:LS, 2, :], a["x_sample"][0], "x_in")
            for i in range(4):
                load(wmv[:, 2 * i:2 * i + 2, :], wrows(a["w_mv"], 2 * i, 2), f"wmv_in{i}")
            sp.wait_ge(filled, J.filled_at("K3"))
            load(w_qk, win[:, :, 0:2 * KW], "wqk_in")
            load(w_v, win[:, :, COL["v"]:COL["v"] + GW], "wv_in")
            sp.wait_ge(filled, J.filled_at("V3"))
            load(w_u, win[:, :, COL["u"]:COL["u"] + POOL], "wu_in")
            load(w_g, win[:, :, COL["g"]:COL["g"] + GW], "wg_in")
            has(sp, "V3")
            load(Vs[:, :, :], a["cache_mem_v"][0, 0].rearrange("(i p) h d -> p i (h d)", p=P), "vs_in")
            sp.wait_ge(filled, J.filled_at("g3"))
            load(poolw, a["pool_w"][0].rearrange("g c d -> c g d"), "poolw_in")
            load(Ks[:, :, :], a["cache_mem_k"][0, 0].rearrange("(i p) h d -> p i (h d)", p=P), "ks_in")
            for i in range(4):
                load(wsq[:, i], wcols(a["w_out"], 256 * i, 256), f"wsq_in{i}")
            def load_up0(i):
                load(upA[:, 2 * i:2 * i + 2, :], a["w_up"][0, 0].rearrange("(k p) f -> p k f", p=P)[:, 2 * i:2 * i + 2, :], f"upA_in{i}")
            has(sp, "oT3")
            sp.wait_ge(S("hist_out"), 32)
            for i in range(4):
                has(sp, f"out{2 * i + 1}")
                load(wsq[:, i], wcols(a["w_mq"], 256 * i, 256), f"wsq_in{i}")
            for i in range(4):
                has(sp, f"mq{2 * i + 1}")
                load(wsq[:, i], wcols(a["w_mo"], 256 * i, 256), f"wsq_in{i}")
            load_up0(2)
            has(sp, "PV4")
            sp.wait_ge(S("v_out"), 16)
            sp.wait_ge(S("states_out"), 32)
            for i in range(4):
                load(upB[:, 2 * i:2 * i + 2, :], a["w_up"][0, 1].rearrange("(k p) f -> p k f", p=P)[:, 2 * i:2 * i + 2, :], f"upB_in{i}")
            has(sp, "mo7")
            for i in (0, 1, 3):
                load_up0(i)
            for i in range(2):
                load(wdn[:, 4 * i:4 * i + 4, :], a["w_down"][0, 0].rearrange("(k p) f -> p k f", p=P)[:, 4 * i:4 * i + 4, :], f"down_in{i}")
            moe_sync(sp)

        @block.gpsimd
        def _(pool):
            pool.memset(ident[:, :], 0.0).then_inc(S("const0"), 1)
            pool.memset(tri[:, :], 1.0 / 16.0).then_inc(S("const0"), 1)
            pool.memset(ones[:, :], 1.0).then_inc(S("const0"), 1)
            pool.memset(below[:, :], 1.0).then_inc(S("const0"), 1)
            pool.memset(small[:, :], 1.0).then_inc(S("const0"), 1)
            pool.wait_ge(S("const0"), 1)
            pool.affine_select(out=ident[:, :], in_=ident[:, :], compare_op=ALU.not_equal, fill=1.0, base=0,
                               pattern=[[-1, P]], channel_multiplier=1).then_inc(S("const1"), 1)
            pool.wait_ge(S("const0"), 5)
            pool.dma_start(buprow[0:E, :], a["b_up"][0]).then_inc(S("bup_in"), 16)
            pool.dma_start(wr_col, a["w_in"][0].rearrange("(k p) f -> p k f", p=P)[:, :, COL["r"]:COL["r"] + RANK]).then_inc(S("gate_in"), 16)
            pool.dma_start(wgate[0:RANK, :], a["w_gate"][0]).then_inc(S("gate_in"), 16)
            pool.dma_start(wgate[RANK:RANK + 1, :], a["b_gate"]).then_inc(S("gate_in"), 16)
            pool.affine_select(out=tri[:, :], in_=tri[:, :], compare_op=ALU.is_ge, fill=0.0, base=0,
                               pattern=[[1, P]], channel_multiplier=-1).then_inc(S("const2"), 1)
            pool.wait_ge(S("const2"), 1)
            pool.memset(tri[0:CHUNK, CHUNK:P], 0.0).then_inc(S("const2"), 1)
            pool.affine_select(out=below[:, :], in_=below[:, :], compare_op=ALU.is_gt, fill=0.0, base=0,
                               pattern=[[1, P]], channel_multiplier=-1).then_inc(S("const2"), 1)
            pool.iota(iota[:, :].bitcast(I32), [[0, 2], [1, SLOTS]], 0, 0).then_inc(S("const2"), 1)
            pool.memset(rT[0:32, :], 1.0).then_inc(S("rT_ones"), 1)
            pool.memset(upad[:, :, 0:BUF], 0.0).then_inc(S("upad_zero"), 1)
            pool.dma_start(wr, a["w_router"][0].rearrange("(k p) e -> p k e", p=P)).then_inc(S("router_in"), 16)
            pool.dma_start(brout, a["b_router"].broadcast_to([P, E])).then_inc(S("router_in"), 16)
            has(pool, "vec")
            pool.dma_start(prevrow[0:BUF, :], a["state_pool"][0, 0]).then_inc(S("prev_in"), 16)
            has(pool, "K3")
            pool.dma_start(o["mem_k"][0, 0].rearrange("(i p) h d -> p i (h d)", p=P), Kp[:, :, :]).then_inc(S("k_out"), 16)
            has(pool, "V3")
            pool.dma_start(o["mem_v"][0, 0].rearrange("(i p) h d -> p i (h d)", p=P), Vp[:, :, :]).then_inc(S("v_out"), 16)
            pool.dma_start(Sbuf[4], a["state_gla"][0, 0].rearrange("(r h) d e -> (h d) r e", r=2)).then_inc(S("s0_in"), 16)
            has(pool, "v2")
            for z in (qdz, klz, AT):
                pool.memset(z, 0.0).then_inc(S("gla_zero"), 1)
            has(pool, "u3")
            for g in range(4):
                w = 2 << g
                pool.memset(invn[:, g, :], 1.0 / w).then_inc(S("invn"), 1)
            pool.wait_ge(S("invn"), 4)
            n = 4
            for g in range(4):
                for t in range((2 << g) - 1):
                    pool.memset(invn[:, g, t:t + 1], 1.0 / (t + 1)).then_inc(S("invn"), 1)
                    n += 1
            has(pool, "prevT")
            src, steps = upad, 0
            for j in range(4):
                dst = (s_a, s_b)[j % 2]
                if j:
                    pool.wait_ge(S("window"), steps)
                off = 1 << j
                pool.tensor_tensor(dst[:, j:4, off:UPAD], src[:, j:4, off:UPAD], src[:, j:4, 0:UPAD - off],
                                   ALU.add).then_inc(S("window"), 1)
                steps += 1
                if j == 0:
                    pool.tensor_copy(dst[:, :, 0:off], src[:, :, 0:off]).then_inc(S("window"), 1)
                    steps += 1
                elif j < 3:
                    pool.tensor_copy(dst[:, j:4, 0:off], src[:, j:4, 0:off]).then_inc(S("window"), 1)
                    steps += 1
                src = dst
            pool.wait_ge(S("invn"), n)
            pool.wait_ge(S("window"), steps)
            k = 0
            for g in range(4):
                sg_ = (s_a, s_b)[g % 2]
                for t0, n0, u0 in ((0, LP, BUF), (LP, LS, UP_P + BUF)):
                    pool.tensor_tensor(sg_[:, g, u0:u0 + n0], sg_[:, g, u0:u0 + n0], invn[:, g, t0:t0 + n0],
                                       ALU.mult).then_inc(S("mean"), 1)
                    k += 1
                    pool.wait_ge(S("mean"), k)
                    pool.tensor_tensor(invn[:, g, t0:t0 + n0], sg_[:, g, u0:u0 + n0], upad[:, g, u0:u0 + n0],
                                       ALU.subtract).then_inc(S("pool_diff"), 1)
            has(pool, "ds4")
            pool.wait_ge(S("state"), 15)
            pool.dma_start(o["gla_p"][0, 0].rearrange("(r h) d e -> (h d) r e", r=2), Sbuf[3]).then_inc(S("states_out"), 16)
            pool.dma_start(o["gla_s"][0, 0].rearrange("(r h) d e -> (h d) r e", r=2), Sbuf[5]).then_inc(S("states_out"), 16)
            has(pool, "hist1")
            for i, name in enumerate(("pool_p", "pool_s")):
                pool.dma_start(o[name][0, 0], hist[0:BUF, i, :]).then_inc(S("hist_out"), 16)
            has(pool, "router")
            pool.wait_ge(S("states_out"), 32)
            pool.wait_ge(S("k_out"), 16)
            pool.memset(Hm[64:P, 2, :], 0.0).then_inc(S("moe_zero"), 1)
            pool.wait_ge(S("moe_zero"), 1)
            pool.memset(gpad[:, :, :], 0.0).then_inc(S("moe_zero"), 1)
            pool.dma_start(bdrow, a["b_down"][0]).then_inc(S("bdown_in"), 16)
            pool.wait_ge(S("rank_max"), 1)
            pool.partition_all_reduce(small[:, 131:132], nover, P, bass.bass_isa.ReduceOp.max).then_inc(S("nover"), 1)

        @block.scalar
        def _(act):
            def free(ins, name):
                assert J.freed_at(name) == ("A", free.n + 1), name
                free.n += 1
                ins.then_inc(freed["A"], 1)
            free.n = 0
            r = 0
            for name, n in (("norm_mix", 8), ("norm_mem_q", 8), ("norm_mem_kv", 8), ("norm_moe", 8),
                            ("gla_gain", 4), ("pool_scale", 4)):
                act.dma_start(smallrows[r:r + n, :], a[name][0].rearrange("(k p) -> k p", p=P)).then_inc(S("vec_in"), 16)
                r += n
            act.wait_ge(S("const0"), 5)
            act.wait_ge(S("mem_in"), 16)
            for i in range(2):
                if i:
                    act.wait_ge(S("ssq_mem"), i)
                act.activation(catT.rearrange("p k t -> p (k t)")[:, 0:D], mem[:, i, :], ACT.Square,
                               accum_out=ssm[:, i:i + 1]).then_inc(S("ssq_mem"), 1)
            has(act, "vec")
            for i in range(4):
                took(act, f"memT{i}")
                b = bank(f"memT{i}")
                act.activation(memT[:, 2 * i, :], b[:, 0:256], ACT.Copy, scale=g_memkv[:, 2 * i:2 * i + 1])
                free(act.activation(memT[:, 2 * i + 1, :], b[:, 256:512], ACT.Copy,
                                    scale=g_memkv[:, 2 * i + 1:2 * i + 2]), f"memT{i}")
            took(act, "memT3")
            for i in (1, 2, 3, 0):
                has(act, f"memT{i}")
                high(act, memH[:, 2 * i:2 * i + 2, :], memT[:, 2 * i:2 * i + 2, :]).then_inc(S("memH"), 1)
            def high_memory(w, wH, what, chunks):
                for i in chunks:
                    act.wait_ge(S(f"w{what}_in{i}"), 16)
                    high(act, wH[:, 2 * i:2 * i + 2, :], w[:, 2 * i:2 * i + 2, :]).then_inc(S(f"w{what}H"), 1)
            high_memory(wmk, wmkH, "mk", range(1, 4))
            act.wait_ge(S("x_in"), 32)
            for i, (t0, n) in enumerate(TILES):
                if i:
                    act.wait_ge(S("ssq_x"), i)
                act.activation(catT.rearrange("p k t -> p (k t)")[0:n, 1024:1024 + D], xtok[0:n, i, :], ACT.Square,
                               accum_out=ssx[0:n, i:i + 1]).then_inc(S("ssq_x"), 1)
            act.wait_ge(S("meansq0"), 1)
            act.activation(sst[:, 0:5], sst[:, 0:5], ACT.Sqrt).then_inc(S("root0"), 1)
            high_memory(wmv, wmvH, "mv", range(3))
            act.wait_ge(S("rstd0"), 1)
            def gained(k):
                has(act, f"xT{k}")
                if k == 0:
                    has(act, "bup")
                act.activation(gxH[:, k, :], xT[:, k, :], ACT.Copy, scale=g_mix[:, k:k + 1]).then_inc(S("gx"), 1)
            for i in range(4):
                took(act, f"K{i}")
                if i == 0:
                    act.wait_ge(S("ssq_x"), 3)
                free(act.activation(Kp[:, i // 2, 512 * (i % 2):512 * (i % 2) + 512], bank(f"K{i}"), ACT.Copy,
                                    scale=rsm[:, i // 2:i // 2 + 1]), f"K{i}")
            high_memory(wmv, wmvH, "mv", (3,))
            for k in range(KT):
                gained(k)
            for i in range(4):
                took(act, f"V{i}")
                free(act.activation(Vp[:, i // 2, 512 * (i % 2):512 * (i % 2) + 512], bank(f"V{i}"), ACT.Copy,
                                    scale=rsm[:, i // 2:i // 2 + 1]), f"V{i}")
            def high_in(name):
                for j, n in enumerate(split_at[name]):
                    _, w, wH, _, rows, cols = split[n - 1]
                    if name == "u":
                        took(act, ("q0", "q1", "k0", "k1")[j])
                    high(act, wH[:, rows, cols], w[:, rows, cols]).then_inc(S("w_inH"), 1)
            act.wait_ge(S("gate_in"), 48)
            high_in("r")
            took(act, "V3")
            act.wait_ge(S("wqk_in"), 16)
            high_in("qk")
            for i in range(4):
                took(act, f"KTp{i}")
                free(act.activation(KTp[:, 2 * i:2 * i + 2, :].rearrange("p k m -> p (k m)"), bank(f"KTp{i}"),
                                    ACT.Copy), f"KTp{i}")
            act.wait_ge(S("wv_in"), 16)
            high_in("v")
            for j, (i0, ni, n) in enumerate(((0, 2, P), (2, 1, 64))):
                took(act, f"gate{j}")
                act.wait_ge(S("gate_min"), j + 1)
                free(act.activation(la1[0:n, i0:i0 + ni, :].rearrange("p i f -> p (i f)"), bank(f"gate{j}", 256 * ni, n),
                                    ACT.Abs), f"gate{j}")
            for j, (i0, ni, n) in enumerate(((0, 2, P), (2, 1, 64))):
                v_ = la1[0:n, i0:i0 + ni, :].rearrange("p i f -> p (i f)")
                has(act, f"gate{j}")
                act.activation(v_, v_, ACT.Exp, scale=-1.0).then_inc(S("gate_exp"), 1)
                act.wait_ge(S("gate_exp"), j + 1)
                act.activation(v_, v_, ACT.Ln, bias=1.0).then_inc(S("gate_ln"), 1)
            act.wait_ge(S("wu_in"), 16)
            high_in("u")
            for i, (t0, n) in enumerate(TILES):
                took(act, f"v{i}")
                free(act.activation(vtok[0:n, i, :], bank(f"v{i}", 512, n), ACT.Copy, scale=rsx[0:n, i:i + 1]), f"v{i}")
            act.wait_ge(S("wg_in"), 16)
            high_in("g")
            has(act, "cum1")
            fl = lambda z: z.rearrange("p r t -> p (r t)")
            act.activation(fl(eb), fl(bT), ACT.Exp).then_inc(S("decays"), 1)
            act.activation(fl(enb), fl(bT), ACT.Exp, scale=-1.0).then_inc(S("decays"), 1)
            act.wait_ge(S("bl_diff"), 1)
            act.activation(fl(ebl), fl(ebl), ACT.Exp).then_inc(S("decays"), 1)
            took(act, "prevT")
            free(act.activation(upad[:, :, UP_P:UP_P + BUF], bank("prevT", 4 * BUF).rearrange("p (g t) -> p g t", g=4),
                                ACT.Copy), "prevT")
            act.wait_ge(S("gla_zero"), 2)
            for c_ in range(5):
                i, r0 = c_ // 2, 64 * (c_ % 2)
                j = 0 if i < 2 else 1
                if c_ in (0, 4):
                    took(act, f"klT{j}")
                b = ps[r0:r0 + 64, J.bank(f"klT{j}"), 256 * (i % 2):256 * (i % 2) + 256]
                ins = act.activation(klz[r0:r0 + 64, c_, :], b, ACT.Copy)
                if c_ in (3, 4):
                    free(ins, f"klT{j}")
            has(act, "g3")
            act.activation(sgT_e, sgT_f, ACT.Sigmoid).then_inc(S("g_sigmoid"), 1)
            for i in range(4):
                took(act, f"KTs{i}")
                free(act.activation(KTs[:, 2 * i:2 * i + 2, :].rearrange("p k m -> p (k m)"), bank(f"KTs{i}"),
                                    ACT.Copy), f"KTs{i}")
            for i, (t0, n) in enumerate(TILES):
                has(act, f"o{i}")
                act.activation(osq[0:n, i, :], otok[0:n, i, :], ACT.Square).then_inc(S("o_sq"), 1)
            act.wait_ge(S("meansq_o"), 1)
            act.activation(small[:, 22:34], small[:, 22:34], ACT.Sqrt).then_inc(S("root_o"), 1)
            took(act, "o2")
            def high_square(g, rows=KT):
                act.wait_ge(S(f"wsq_in{g % 4}"), (g // 4 + 1) * 16)
                if g >= 4:
                    took(act, f"{('out', 'mq', 'mo')[g // 4 - 1]}{2 * (g % 4) + 1}")
                high(act, wsqH[g % 4][:, 0:rows], wsq[:, g % 4, 0:rows]).then_inc(S("wsqH"), 1)
            high_square(0, 4)
            high_square(1, 4)
            def high_cat(k, name):
                has(act, name)
                high(act, catH[:, k, :], catT[:, k, :]).then_inc(S("catH"), 1)
            for i in range(2):
                took(act, f"hist{i}")
                free(act.activation(hist[0:BUF, i, :], bank(f"hist{i}", 512, BUF), ACT.Copy), f"hist{i}")
            for g in range(4):
                high_cat(4 + g, f"pool{g}")
            high_square(2)
            high_square(3)
            for h in range(4):
                high_cat(h, f"oT{h}")
            for k in range(KT):
                has(act, f"out{k}")
                act.activation(gxH[:, k, :], xT[:, k, :], ACT.Copy, scale=g_memq[:, k:k + 1]).then_inc(S("gx1H"), 1)
                act.activation(sq1[:, k, :], xT[:, k, :], ACT.Square).then_inc(S("sq1"), 1)
                if k in (3, 5, 7):
                    high_square(4 + (k - 3) // 2)
            for g in range(7, 10):
                high_square(g)
            has(act, "rms1")
            act.activation(ms1[:, :], ms1[:, :], ACT.Sqrt).then_inc(S("root1"), 1)
            for m, j in enumerate(SCORES):
                took(act, f"s{j}")
                act.wait_ge(S("nmax"), m + 1)
                n = P if j < 4 else 64
                for h2 in range(2):
                    h = 2 * (j % 2) + h2
                    dst = probs_p[:, j // 2, h, :] if j < 4 else probs_s[0:64, h, :]
                    cidx = (j // 2) * 4 + h
                    ins = act.activation(dst, bank(f"s{j}", 512, n)[:, 256 * h2:256 * h2 + 256], ACT.Exp,
                                         bias=nmx[0:n, cidx:cidx + 1], scale=rs1p[0:n, j // 2:j // 2 + 1],
                                         accum_out=rs[0:n, cidx:cidx + 1])
                free(ins, f"s{j}")
            high_square(10)
            high_square(11)
            for h in range(4):
                took(act, f"PV{h}")
                act.activation(aoH[:, 2 * h:2 * h + 2, 0:LP], bank(f"PV{h}").rearrange("p (d l) -> p d l", d=2),
                               ACT.Copy).then_inc(S("aoH"), 1)
            took(act, "PV4")
            act.activation(aoH[:, :, LP:NT], bank("PV4").rearrange("p (d l) -> p d l", d=KT), ACT.Copy).then_inc(S("aoH"), 1)
            for k in range(KT):
                has(act, f"mo{k}")
                act.activation(sq2[:, k, :], xT[:, k, :], ACT.Square).then_inc(S("sq2"), 1)
            act.wait_ge(S("meansq2"), 1)
            act.activation(rs2[:, :], rs2[:, :], ACT.Sqrt).then_inc(S("root2"), 1)
            for j in range(6):
                i, n = j // 2, TILES[j // 2][1]
                took(act, f"x2_{j}")
                free(act.activation(acc[0:n, i, 512 * (j % 2):512 * (j % 2) + 512], bank(f"x2_{j}", 512, n), ACT.Copy),
                     f"x2_{j}")
            act.wait_ge(S("rstd2"), 1)
            for i, (t0, n) in enumerate(TILES):
                has(act, f"x2_{2 * i + 1}")
                act.activation(Hm[0:n, i, :], acc[0:n, i, :], ACT.Copy, scale=rs2[0:n, i:i + 1]).then_inc(S("Hm"), 1)
            act.wait_ge(S("top"), 1)
            act.wait_ge(S("moe_zero"), 2)
            for i, (t0, n) in enumerate(TILES):
                act.activation(gpad[0:n, i, 64:96], logit[0:n, i, :], ACT.Exp, bias=nt1[0:n, i:i + 1],
                               scale=1.0).then_inc(S("gate_e"), 1)
            moe_act(act)

        @block.vector
        def _(dve):
            def free(ins, name):
                assert J.freed_at(name) == ("D", free.n + 1), (name, free.n)
                free.n += 1
                ins.then_inc(freed["D"], 1)
            free.n = 0
            dve.wait_ge(S("const2"), 4)
            dve.tensor_copy(iota[:, :], iota[:, :].bitcast(I32)).then_inc(S("iota"), 1)
            took(dve, "vec")
            free(dve.tensor_copy(vec[:, :], bank("vec", 40)), "vec")
            def low_mem(i, n):
                dve.wait_ge(S("memH"), n)
                low(dve, memL[:, 2 * i:2 * i + 2, :], memT[:, 2 * i:2 * i + 2, :], memH[:, 2 * i:2 * i + 2, :]).then_inc(S("memL"), 1)
            def low_memory(w, wH, wL, what, i, n):
                dve.wait_ge(S(f"w{what}H"), n)
                low(dve, wL[:, 2 * i:2 * i + 2, :], w[:, 2 * i:2 * i + 2, :], wH[:, 2 * i:2 * i + 2, :]).then_inc(S(f"w{what}L"), 1)
            for i in (1, 2, 3):
                low_mem(i, i)
                low_memory(wmk, wmkH, wmkL, "mk", i, i)
            dve.wait_ge(S("mem_whole_used"), 1)
            low_mem(0, 4)
            dve.wait_ge(S("ssq_mem"), 2)
            dve.wait_ge(S("ssq_x"), 3)
            dve.tensor_scalar(sst[:, 0:5], small[:, 0:5], 1.0 / D, EPS, ALU.mult, ALU.add).then_inc(S("meansq0"), 1)
            dve.wait_ge(S("root0"), 1)
            dve.reciprocal(small[:, 5:10], sst[:, 0:5]).then_inc(S("rstd0"), 1)
            for i in range(2):
                low_memory(wmv, wmvH, wmvL, "mv", i, i + 1)
            took(dve, "bup")
            free(dve.tensor_copy(bupT.rearrange("p e f -> p f e"), bank("bup").rearrange("p (f e) -> p f e", e=E)), "bup")
            for k in range(KT):
                took(dve, f"xT{k}")
                free(dve.tensor_copy(xT[:, k, :], bank(f"xT{k}", NT)), f"xT{k}")
                if k == 0:
                    dve.wait_ge(S("rstd0"), 1)
                    for i in range(3):
                        dve.tensor_scalar(rT_diag[:, i, :], ident[:, :], rsx[:, i:i + 1], None,
                                          ALU.mult).then_inc(S("diag"), 1)
            for i in range(2, 4):
                low_memory(wmv, wmvH, wmvL, "mv", i, i + 1)
            def low_mix(k):
                dve.wait_ge(S("gx"), k + 1)
                dve.scalar_tensor_tensor(mixL[:, k, :], xT[:, k, :], g_mix[:, k:k + 1], gxH[:, k, :].bitcast(F32),
                                         ALU.mult, ALU.subtract).then_inc(S("gxL"), 1)
            def low_in(name, j):
                n = split_at[name][j]
                dve.wait_ge(S("w_inH"), n)
                _, w, wH, wL, rows, cols = split[n - 1]
                low(dve, wL[:, rows, cols], w[:, rows, cols], wH[:, rows, cols]).then_inc(S("w_inL"), 1)
            for k in range(KT):
                low_mix(k)
            took(dve, "rms0")
            free(dve.tensor_copy(rstdb[:, :], bank("rms0", NT)), "rms0")
            has(dve, "rms0")
            low_in("r", 0)
            low_in("qk", 0)
            took(dve, "r")
            dve.wait_ge(S("rT_ones"), 1)
            free(dve.tensor_tensor(rT[0:RANK, :], bank("r", NT, RANK), rstdb[0:RANK, :], ALU.mult), "r")
            low_in("qk", 1)
            for j in range(2):
                low_in("qk", 2 + j)
                took(dve, f"q{j}")
                free(dve.tensor_tensor(qT[:, j, :], bank(f"q{j}", NT), rstdb[:, :], ALU.mult), f"q{j}")
            for i in range(4):
                low_in("v", i)
            dve.wait_ge(S("k_out"), 16)
            for j, (i0, ni, n) in enumerate(((0, 2, P), (2, 1, 64))):
                took(dve, f"gate{j}")
                dve.tensor_scalar(la0[0:n, i0:i0 + ni, :].rearrange("p i f -> p (i f)"), bank(f"gate{j}", 256 * ni, n),
                                  0.0, None, ALU.min).then_inc(S("gate_min"), 1)
            for j in range(2):
                took(dve, f"k{j}")
                free(dve.tensor_tensor(kT[:, j, :], bank(f"k{j}", NT), rstdb[:, :], ALU.mult), f"k{j}")
            dve.wait_ge(S("gate_ln"), 2)
            for j, (i0, ni, n) in enumerate(((0, 2, P), (2, 1, 64))):
                dve.tensor_tensor(la0[0:n, i0:i0 + ni, :], la0[0:n, i0:i0 + ni, :], la1[0:n, i0:i0 + ni, :],
                                  ALU.subtract).then_inc(S("log_a"), 1)
            for j in range(4):
                low_in("u", j)
            for g in range(4):
                if g:
                    low_in("g", g - 1)
                took(dve, f"u{g}")
                b = bank(f"u{g}", NT)
                dve.tensor_tensor(upad[:, g, BUF:UP_P], b[:, 0:LP], rstdb[:, 0:LP], ALU.mult)
                free(dve.tensor_tensor(upad[:, g, UP_P + BUF:UPAD], b[:, LP:NT], rstdb[:, LP:NT], ALU.mult), f"u{g}")
            low_in("g", 3)
            for j in range(2):
                took(dve, f"cum{j}")
                free(dve.tensor_copy(bT[:, j, :], bank(f"cum{j}", NT)), f"cum{j}")
            has(dve, "cum1")
            for r_ in range(2):
                bc = bT[:, r_, :].rearrange("p (c t) -> p c t", c=5)
                last = dve.tensor_tensor(ebl[:, r_, :].rearrange("p (c t) -> p c t", c=5),
                                         bc[:, :, CHUNK - 1:CHUNK].broadcast_to([P, 5, CHUNK]), bc, ALU.subtract)
            last.then_inc(S("bl_diff"), 1)
            dve.wait_ge(S("gla_zero"), 3)
            dve.wait_ge(S("decays"), 1)
            for h in range(4):
                r0 = 64 * (h % 2)
                dve.scalar_tensor_tensor(qdz[r0:r0 + 64, h, :], qT[r0:r0 + 64, h // 2, :], DK ** -0.5,
                                         eb[r0:r0 + 64, h // 2, :], ALU.mult, ALU.mult).then_inc(S("decayed"), 1)
            dve.wait_ge(S("decays"), 2)
            fl = lambda z: z.rearrange("p r t -> p (r t)")
            dve.tensor_tensor(fl(kdT), fl(kT), fl(enb), ALU.mult).then_inc(S("decayed"), 1)
            dve.wait_ge(S("decays"), 3)
            dve.tensor_tensor(fl(ebl), fl(kT), fl(ebl), ALU.mult).then_inc(S("decayed"), 1)
            for g in range(4):
                took(dve, f"g{g}")
                free(dve.tensor_tensor(sgT[:, g, :], bank(f"g{g}", NT), rstdb[:, :], ALU.mult), f"g{g}")
            for i, (t0, n) in enumerate(TILES):
                took(dve, f"AT{i}")
                m = tri[0:n, 0:n].bitcast(I32).unsqueeze(1).broadcast_to([n, 4, n])
                free(dve.copy_predicated(AT[0:n, i, :, 0:n], m, bank(f"AT{i}", 4 * n, n).rearrange("p (h t) -> p h t", h=4)),
                     f"AT{i}")
            n = 0
            for c_ in range(NCH):
                took(dve, f"ds{c_}")
                b = bank(f"ds{c_}").rearrange("p (r f) -> p r f", r=2)
                src = {0: None, 1: Sbuf[0], 2: Sbuf[1], 3: Sbuf[2], 4: Sbuf[4]}[c_]
                dst = Sbuf[c_] if c_ < 4 else Sbuf[5]
                if c_ in (1, 2, 3):
                    dve.wait_ge(S("state"), n)
                if c_ == 4:
                    dve.wait_ge(S("s0_in"), 16)
                    has(dve, "prevT")
                for hh in range(2):
                    r0 = 64 * hh
                    for r_ in range(2):
                        bb = b[r0:r0 + 64, r_, 128 * hh:128 * hh + 128]
                        if src is None:
                            ins = dve.tensor_copy(dst[r0:r0 + 64, r_, :], bb)
                        else:
                            ins = dve.scalar_tensor_tensor(dst[r0:r0 + 64, r_, :], src[r0:r0 + 64, r_, :],
                                                           eb[r0:r0 + 64, r_, CHUNK * c_ + 63:CHUNK * c_ + 64], bb,
                                                           ALU.mult, ALU.add)
                        if (hh, r_) == (1, 1):
                            free(ins, f"ds{c_}")
                        else:
                            ins.then_inc(S("state"), 1)
                            n += 1
                has(dve, f"ds{c_}")
            dve.wait_ge(S("g_sigmoid"), 1)
            dve.tensor_tensor(sgT_f, sgT_f, sgT_e, ALU.mult).then_inc(S("silu"), 1)
            for i, (t0, n) in enumerate(TILES):
                took(dve, f"o{i}")
                free(dve.tensor_copy(otok[0:n, i, :], bank(f"o{i}", 512, n)), f"o{i}")
            for i, (t0, n) in enumerate(TILES):
                dve.wait_ge(S("o_sq"), i + 1)
                dve.tensor_reduce(sso[0:n, i, :], osq[0:n, i, :].rearrange("p (h e) -> p h e", h=4), AX.X,
                                  ALU.add).then_inc(S("o_sum"), 1)
            dve.wait_ge(S("o_sum"), 3)
            dve.tensor_scalar(small[:, 22:34], small[:, 10:22], 1.0 / DV, EPS, ALU.mult, ALU.add).then_inc(S("meansq_o"), 1)
            for g in range(4):
                took(dve, f"pool{g}")
                free(dve.tensor_scalar(catT[:, 4 + g, :], bank(f"pool{g}", NT), pscale[:, g:g + 1], None, ALU.mult),
                     f"pool{g}")
            def low_square(g, rows=KT):
                dve.wait_ge(S("wsqH"), g + 1)
                low(dve, wsqL[g % 4][:, 0:rows], wsq[:, g % 4, 0:rows], wsqH[g % 4][:, 0:rows]).then_inc(S("wsqL"), 1)
            def low_cat(k, n):
                dve.wait_ge(S("catH"), n)
                low(dve, catL[:, k, :], catT[:, k, :], catH[:, k, :]).then_inc(S("catL"), 1)
            dve.wait_ge(S("root_o"), 1)
            dve.reciprocal(small[:, 22:34], small[:, 22:34]).then_inc(S("rstd_o"), 1)
            dve.wait_ge(S("rstd_o"), 1)
            for i, (t0, n) in enumerate(TILES):
                v_ = otok[0:n, i, :].rearrange("p (h e) -> p h e", h=4)
                dve.tensor_tensor(v_, v_, rso[0:n, i, :].unsqueeze(2).broadcast_to([n, 4, DV]),
                                  ALU.mult).then_inc(S("o_norm"), 1)
            low_square(0, 4)
            low_square(1, 4)
            dve.wait_ge(S("silu"), 1)
            for h in range(5):
                if h < 4:
                    took(dve, f"oT{h}")
                    free(dve.scalar_tensor_tensor(catT[:, h, :], bank(f"oT{h}", NT), g_gla[:, h:h + 1], sgT[:, h, :],
                                                  ALU.mult, ALU.mult), f"oT{h}")
                if h:
                    low_cat(h - 1, 4 + h)
            low_square(2)
            dve.wait_ge(S("pool_rows_used"), 1)
            for g in range(4):
                low_cat(4 + g, g + 1)
            low_square(3)
            def low_queries(k):
                dve.wait_ge(S("gx1H"), k + 1)
                dve.scalar_tensor_tensor(gxL[:, k, :], xT[:, k, :], g_memq[:, k:k + 1], gxH[:, k, :].bitcast(F32),
                                         ALU.mult, ALU.subtract).then_inc(S("gx1L"), 1)
            def add_square(k, sq, square, total):
                dve.wait_ge(S(square), k + 1)
                if k > 1:
                    dve.wait_ge(S(total), k - 1)
                dve.tensor_tensor(sq[:, 0, :], sq[:, 0, :], sq[:, k, :], ALU.add).then_inc(S(total), 1)
            for k in range(KT):
                took(dve, f"out{k}")
                free(dve.tensor_tensor(xT[:, k, :], bank(f"out{k}", NT), xT[:, k, :], ALU.add), f"out{k}")
                if k:
                    low_queries(k - 1)
                if k > 1:
                    add_square(k - 1, sq1, "sq1", "sqsum1")
                if k in (4, 6):
                    low_square(2 + k // 2)
            low_queries(7)
            add_square(7, sq1, "sq1", "sqsum1")
            low_square(6)
            for k in range(KT):
                took(dve, f"mq{k}")
                free(dve.tensor_copy(aqT[:, k, :], bank(f"mq{k}", NT)), f"mq{k}")
                if k in (1, 4, 7):
                    low_square(7 + k // 3)
            took(dve, "rms1")
            dve.tensor_scalar(ms1[:, 0:2], bank("rms1", 2), 1.0 / D, EPS, ALU.mult, ALU.add)
            free(dve.tensor_scalar(ms1[0:LS, 2:3], ps[0:LS, J.bank("rms1"), 2:3], 1.0 / D, EPS, ALU.mult, ALU.add), "rms1")
            dve.wait_ge(S("root1"), 1)
            dve.reciprocal(rs1[:, :], ms1[:, :]).then_inc(S("rstd1"), 1)
            dve.wait_ge(S("rstd1"), 1)
            dve.tensor_scalar(rs1p[:, :], rs1[:, :], 1.0 / 16.0, None, ALU.mult).then_inc(S("rstd1"), 1)
            dve.tensor_scalar(rs1n[:, :], rs1[:, :], -1.0 / 16.0, None, ALU.mult).then_inc(S("rstd1"), 1)
            dve.wait_ge(S("rstd1"), 3)
            def normalise(m):
                j = SCORES[m]
                has(dve, f"s{j}")
                n = P if j < 4 else 64
                c0 = (j // 2) * 4 + 2 * (j % 2)
                dve.reciprocal(rinv[0:n, c0:c0 + 2], rs[0:n, c0:c0 + 2]).then_inc(S("rinv"), 1)
                dve.wait_ge(S("rinv"), m + 1)
                for h2 in range(2):
                    h = 2 * (j % 2) + h2
                    v_ = probs_p[:, j // 2, h, :] if j < 4 else probs_s[0:64, h, :]
                    dve.tensor_scalar(v_, v_, rinv[0:n, c0 + h2:c0 + h2 + 1], None, ALU.mult).then_inc(S("probs"), 1)
            for m, j in enumerate(SCORES):
                took(dve, f"s{j}")
                n = P if j < 4 else 64
                c0 = (j // 2) * 4 + 2 * (j % 2)
                dve.tensor_reduce(mx[0:n, c0:c0 + 2], bank(f"s{j}", 512, n).rearrange("p (h m) -> p h m", h=2), AX.X,
                                  ALU.max).then_inc(S("smax"), 1)
                dve.wait_ge(S("smax"), m + 1)
                dve.tensor_scalar(nmx[0:n, c0:c0 + 2], mx[0:n, c0:c0 + 2], rs1n[0:n, j // 2:j // 2 + 1], None,
                                  ALU.mult).then_inc(S("nmax"), 1)
                if m >= 2:
                    normalise(m - 2)
            normalise(4)
            normalise(5)
            for h in range(4):
                took(dve, f"PT{h}")
                free(dve.tensor_copy(PTp[:, h, :, :].rearrange("p i l -> p (i l)"), bank(f"PT{h}")), f"PT{h}")
            took(dve, "PT4")
            free(dve.tensor_copy(PTs.rearrange("p h i l -> p (h i l)"), bank("PT4")), "PT4")
            low_square(10)
            low_square(11)
            for h in range(4):
                dve.wait_ge(S("aoH"), h + 1)
                free(dve.tensor_tensor(aoL[:, 2 * h:2 * h + 2, 0:LP],
                                       bank(f"PV{h}").rearrange("p (d l) -> p d l", d=2), aoH[:, 2 * h:2 * h + 2, 0:LP].bitcast(F32),
                                       ALU.subtract), f"PV{h}")
            dve.wait_ge(S("aoH"), 5)
            free(dve.tensor_tensor(aoL[:, :, LP:NT], bank("PV4").rearrange("p (d l) -> p d l", d=KT),
                                   aoH[:, :, LP:NT].bitcast(F32), ALU.subtract), "PV4")
            dve.wait_ge(S("router_in"), 32)
            dve.tensor_tensor(gwr, wr, g_moe.unsqueeze(2).broadcast_to([P, KT, E]), ALU.mult).then_inc(S("gwr"), 1)
            for k in range(KT):
                took(dve, f"mo{k}")
                free(dve.tensor_tensor(xT[:, k, :], bank(f"mo{k}", NT), xT[:, k, :], ALU.add), f"mo{k}")
                if k > 1:
                    add_square(k - 1, sq2, "sq2", "sqsum2")
            add_square(7, sq2, "sq2", "sqsum2")
            took(dve, "router")
            dve.tensor_scalar(rs2[:, 0:2], ps[:, J.bank("router"), 96:98], 1.0 / D, EPS, ALU.mult, ALU.add)
            dve.tensor_scalar(rs2[0:LS, 2:3], ps[0:LS, J.bank("router"), 98:99], 1.0 / D, EPS, ALU.mult,
                              ALU.add).then_inc(S("meansq2"), 1)
            dve.wait_ge(S("root2"), 1)
            dve.reciprocal(rs2[:, :], rs2[:, :]).then_inc(S("rstd2"), 1)
            dve.wait_ge(S("rstd2"), 1)
            for i, (t0, n) in enumerate(TILES):
                ins = dve.scalar_tensor_tensor(logit[0:n, i, :], ps[0:n, J.bank("router"), 32 * i:32 * i + 32],
                                               rs2[0:n, i:i + 1], brout[0:n, :], ALU.mult, ALU.add)
            free(ins, "router")
            has(dve, "router")
            for i, (t0, n) in enumerate(TILES):
                dve.max(top8[0:n, i, :], logit[0:n, i, :]).then_inc(S("max8"), 1)
            dve.memset(topf[64:P, 2, :], 0.0)
            dve.memset(rankx[64:P, 2, :], -1.0)
            dve.memset(Gm[64:P, 2, :], 0.0).then_inc(S("max8"), 1)
            dve.wait_ge(S("max8"), 4)
            dve.tensor_scalar(nt1[:, :], top8[:, :, 0], -1.0, None, ALU.mult).then_inc(S("top"), 1)
            for i, (t0, n) in enumerate(TILES):
                dve.max_index(topi[0:n, i, :], top8[0:n, i, :], logit[0:n, i, :]).then_inc(S("top_at"), 1)
            dve.wait_ge(S("top_at"), 3)
            for i, (t0, n) in enumerate(TILES):
                dve.tensor_copy(topf[0:n, i, :], topi[0:n, i, :]).then_inc(S("top_at"), 1)
            dve.wait_ge(S("top_at"), 6)
            for k in range(4):
                dst = sel if k == 0 else work
                dve.tensor_tensor(dst, iota[:, 0:E].unsqueeze(1).broadcast_to([P, 3, E]),
                                  topf[:, :, k:k + 1].broadcast_to([P, 3, E]), ALU.is_equal).then_inc(S("sel"), 1)
                if k:
                    dve.wait_ge(S("sel"), 2 * k)
                    dve.tensor_tensor(sel, sel, work, ALU.add).then_inc(S("sel"), 1)
                    dve.wait_ge(S("sel"), 2 * k + 1)
            took(dve, "rank")
            for i, (t0, n) in enumerate(TILES):
                ins = dve.scalar_tensor_tensor(rankx[0:n, i, :], ps[0:n, J.bank("rank"), 32 * i:32 * i + 32], 1.0,
                                               sel[0:n, i, :], ALU.add, ALU.mult)
            free(ins, "rank")
            has(dve, "rank")
            for i, (t0, n) in enumerate(TILES):
                dve.tensor_scalar(rankx[0:n, i, :], rankx[0:n, i, :], -1.0, None, ALU.add).then_inc(S("rankx"), 1)
            moe_dve(dve)

        @block.tensor
        def _(pe):
            def begin(name):
                before = J.occupant_before(name)
                if before:
                    pe.wait_ge(freed[before[0]], before[1])

            def end(ins):
                ins.then_inc(filled, 1)

            def turn(name, pieces):
                begin(name)
                for c0, src, rows, cols in pieces:
                    ins = pe.transpose(ps[0:cols, J.bank(name), c0:c0 + rows], src, ident[0:rows, 0:rows])
                end(ins)

            pe.wait_ge(S("const1"), 1)
            pe.wait_ge(S("vec_in"), 96)
            turn("vec", [(0, smallrows[0:40, :], 40, P)])
            pe.wait_ge(S("mem_in"), 16)
            for j in range(4):
                turn(f"memT{j}", [(256 * kk + 128 * i, mem[:, i, 128 * (2 * j + kk):128 * (2 * j + kk) + 128], P, P)
                                  for kk in range(2) for i in range(2)])

            def memory_product(what, wH, wL, sem):
                for j in range(4):
                    begin(f"{what}{j}")
                for k in range(KT):
                    whole = what == "K" and k < 2
                    if whole and k == 0:
                        has(pe, "memT0")
                        pe.wait_ge(S("wmk_in0"), 16)
                    elif k % 2 == 0:
                        first = 0 if what == "K" else 1
                        pe.wait_ge(S(sem), k // 2 + first)
                        pe.wait_ge(S("memL"), k // 2 if what == "K" else 4)
                    for j in range(4):
                        m, f = slice(128 * (j // 2), 128 * (j // 2) + 128), slice(512 * (j % 2), 512 * (j % 2) + 512)
                        if whole:
                            ins = pe.matmul(bank(f"{what}{j}"), memT[:, k, m], wmk[:, k, f], start=(k == 0), stop=False)
                            if (k, j) == (1, 3):
                                ins.then_inc(S("mem_whole_used"), 1)
                            continue
                        ins = product3(pe, bank(f"{what}{j}"), (memH[:, k, m], memL[:, k, m]), (wH[:, k, f], wL[:, k, f]),
                                       k == 0, k == KT - 1)
                        if k == KT - 1:
                            end(ins)
            memory_product("K", wmkH, wmkL, "wmkL")
            pe.wait_ge(S("bup_in"), 16)
            turn("bup", [(E * f, buprow[0:E, 128 * f:128 * f + 128], E, P) for f in range(16)])
            pe.wait_ge(S("x_in"), 32)
            for k in range(KT):
                turn(f"xT{k}", [(t0, xtok[0:n, i, 128 * k:128 * k + 128], n, P) for i, (t0, n) in enumerate(TILES)])
            pe.wait_ge(S("diag"), 3)
            begin("rms0")
            for i, (t0, n) in enumerate(TILES):
                ins = pe.matmul(bank("rms0", NT)[:, t0:t0 + n], ones[0:n, :], rT_diag[0:n, i, 0:n], start=True, stop=True)
            end(ins)
            memory_product("V", wmvH, wmvL, "wmvL")
            has(pe, "K3")
            for j in range(4):
                turn(f"KTp{j}", [(256 * kk + 128 * i, Kp[:, i, 128 * (2 * j + kk):128 * (2 * j + kk) + 128], P, P)
                                 for kk in range(2) for i in range(2)])
            def project3(name, part, cols, rows=P):
                wH, wL = {"r": (wrH, wrL), "qk": (qkH, qkL), "u": (uH, uL), "g": (gH, gL)}[part]
                begin(name)
                for k in range(KT):
                    ins = product3(pe, bank(name, NT, rows), (wH[:, k, cols], wL[:, k, cols]), (gxH[:, k, :], mixL[:, k, :]),
                                   k == 0, k == KT - 1)
                end(ins)
            pe.wait_ge(S("gxL"), 8)
            pe.wait_ge(S("w_inL"), split_at["r"][0])
            project3("r", "r", slice(0, RANK), RANK)
            for j in range(2):
                pe.wait_ge(S("w_inL"), split_at["qk"][j])
                project3(f"q{j}", "qk", columns[j])
            has(pe, "r")
            for j, tiles in enumerate(((0, 1), (2,))):
                begin(f"gate{j}")
                for m, i in enumerate(tiles):
                    t0, n = TILES[i]
                    ins = pe.matmul(ps[0:n, J.bank(f"gate{j}"), 256 * m:256 * m + 256], rT[0:RANK + 1, t0:t0 + n],
                                    wgate[0:RANK + 1, :], start=True, stop=True)
                end(ins)
            for j in range(2):
                pe.wait_ge(S("w_inL"), split_at["qk"][2 + j])
                project3(f"k{j}", "qk", columns[2 + j])
            for i, (t0, n) in enumerate(TILES):
                begin(f"v{i}")
                for k in range(KT):
                    if i == 0 and k % 2 == 0:
                        pe.wait_ge(S("w_inL"), split_at["v"][k // 2])
                    ins = product3(pe, bank(f"v{i}", 512, n), (gxH[:, k, t0:t0 + n], mixL[:, k, t0:t0 + n]),
                                   (vH[:, k, :], vL[:, k, :]), k == 0, k == KT - 1)
                end(ins)
            for g in range(4):
                pe.wait_ge(S("w_inL"), split_at["u"][g])
                project3(f"u{g}", "u", columns[g])
            pe.wait_ge(S("log_a"), 2)
            pe.wait_ge(S("const2"), 4)
            for j in range(2):
                begin(f"cum{j}")
                for i, (t0, n) in enumerate(TILES):
                    ins = pe.matmul(bank(f"cum{j}", NT)[:, t0:t0 + n], la0[0:n, i, 128 * j:128 * j + 128], tri[0:n, 0:n],
                                    start=True, stop=True)
                end(ins)
            pe.wait_ge(S("prev_in"), 16)
            turn("prevT", [(BUF * g, prevrow[0:BUF, 128 * g:128 * g + 128], BUF, P) for g in range(4)])
            for g in range(4):
                pe.wait_ge(S("w_inL"), split_at["g"][g])
                project3(f"g{g}", "g", columns[g])
            pe.wait_ge(S("decayed"), 6)
            for j, tiles in enumerate(((0, 1), (2,))):
                begin(f"klT{j}")
                for m, i in enumerate(tiles):
                    t0, n = TILES[i]
                    for r_ in range(2):
                        ins = pe.transpose(ps[0:n, J.bank(f"klT{j}"), 256 * m + 128 * r_:256 * m + 128 * r_ + 128],
                                           ebl[:, r_, t0:t0 + n], ident[:, :])
                end(ins)
            pe.wait_ge(S("decayed"), 4)
            pe.wait_ge(S("decayed"), 5)
            for i, (t0, n) in enumerate(TILES):
                begin(f"AT{i}")
                for h in range(4):
                    ins = pe.matmul(ps[0:n, J.bank(f"AT{i}"), n * h:n * h + n], kdT[:, h // 2, t0:t0 + n],
                                    qdz[:, h, t0:t0 + n], start=True, stop=True)
                end(ins)
            has(pe, "klT1")
            has(pe, "v2")
            for c_ in range(NCH):
                i, n = c_ // 2, TILES[c_ // 2][1]
                begin(f"ds{c_}")
                for r_ in range(2):
                    ins = pe.matmul(ps[:, J.bank(f"ds{c_}"), 256 * r_:256 * r_ + 256], klz[0:n, c_, 128 * r_:128 * r_ + 128],
                                    vtok[0:n, i, 256 * r_:256 * r_ + 256], start=True, stop=True)
                end(ins)
            pe.wait_ge(S("ks_in"), 16)
            for j in range(4):
                turn(f"KTs{j}", [(256 * kk + 128 * i, Ks[:, i, 128 * (2 * j + kk):128 * (2 * j + kk) + 128], P, P)
                                 for kk in range(2) for i in range(2)])
            has(pe, "AT2")
            has(pe, "ds4")
            pe.wait_ge(S("state"), 15)
            for i, (t0, n) in enumerate(TILES):
                begin(f"o{i}")
                for h in range(4):
                    c0 = 128 * h
                    ins = pe.matmul(ps[0:n, J.bank(f"o{i}"), c0:c0 + 128], AT[0:n, i, h, 0:n], vtok[0:n, i, c0:c0 + 128],
                                    start=True, stop=False, skip_group_check=True)
                    for c_ in ((0, 1), (2, 3), (4,))[i]:
                        if c_ == 0:
                            continue
                        st = Sbuf[c_ - 1] if c_ < 4 else Sbuf[4]
                        r0 = 64 * (c_ % 2)
                        ins = pe.matmul(ps[r0:r0 + 64, J.bank(f"o{i}"), c0:c0 + 128], qdz[:, h, 64 * c_:64 * c_ + 64],
                                        st[:, h // 2, :], start=False, stop=True, skip_group_check=True)
                end(ins)
            pe.wait_ge(S("pool_diff"), 8)
            pe.wait_ge(S("poolw_in"), 16)
            for g in range(4):
                begin(f"pool{g}")
                end(pe.matmul(bank(f"pool{g}", NT), poolw[:, g, :], invn[:, g, :], start=True, stop=True))
            for j, t_end in enumerate((UP_P, UPAD)):
                begin(f"hist{j}")
                for g in range(4):
                    ins = pe.transpose(ps[0:BUF, J.bank(f"hist{j}"), 128 * g:128 * g + 128],
                                       upad[:, g, t_end - BUF:t_end], ident[:, :])
                end(ins)
            def square(name, k, g, x, js, start=None, stop=KT - 1):
                for j in js:
                    cols = slice(128 * (k % 2), 128 * (k % 2) + 128)
                    ins = product3(pe, bank(f"{name}{k}", NT), (wsqH[g % 4][:, j, cols], wsqL[g % 4][:, j, cols]),
                                   (x[0][:, j, :], x[1][:, j, :]), j == start, j == stop)
                return ins
            has(pe, "pool3")
            for k in range(4):
                if k % 2 == 0:
                    pe.wait_ge(S(f"wsq_in{k // 2}"), 16)
                begin(f"out{k}")
                for j in range(4, 8):
                    ins = pe.matmul(bank(f"out{k}", NT), wsq[:, k // 2, j, 128 * (k % 2):128 * (k % 2) + 128],
                                    catT[:, j, :], start=(j == 4), stop=False)
            ins.then_inc(S("pool_rows_used"), 1)
            pe.wait_ge(S("o_norm"), 3)
            for h in range(4):
                turn(f"oT{h}", [(t0, otok[0:n, i, 128 * h:128 * h + 128], n, P) for i, (t0, n) in enumerate(TILES)])
            has(pe, "oT3")
            for k in range(KT):
                pe.wait_ge(S("wsqL"), 1 + k // 2)
                if k == 4:
                    begin(f"out{k}")
                    pe.wait_ge(S("catL"), 8)
                elif k > 4:
                    begin(f"out{k}")
                if k >= 4:
                    square("out", k, k // 2, (catH, catL), range(4, 8), 4, None)
                for j in range(4):
                    if k == 0:
                        pe.wait_ge(S("catL"), j + 1)
                    ins = square("out", k, k // 2, (catH, catL), range(j, j + 1), None, 3)
                end(ins)
            for k in range(KT):
                pe.wait_ge(S("wsqL"), 5 + k // 2)
                begin(f"mq{k}")
                for j in range(KT):
                    if k == 0:
                        pe.wait_ge(S("gx1L"), j + 1)
                    ins = square("mq", k, 4 + k // 2, (gxH, gxL), range(j, j + 1), 0)
                end(ins)
            pe.wait_ge(S("sqsum1"), KT - 1)
            begin("rms1")
            for i, (t0, n) in enumerate(TILES):
                ins = pe.matmul(ps[0:n, J.bank("rms1"), i:i + 1], sq1[:, 0, t0:t0 + n], ones[:, 0:1],
                                start=True, stop=True)
            end(ins)
            has(pe, "mq7")
            for j in SCORES:
                begin(f"s{j}")
                t0, n = TILES[j // 2]
                KTx = KTp if j < 4 else KTs
                for h2 in range(2):
                    h = 2 * (j % 2) + h2
                    for d_ in range(2):
                        ins = pe.matmul(ps[0:n, J.bank(f"s{j}"), 256 * h2:256 * h2 + 256], aqT[:, 2 * h + d_, t0:t0 + n],
                                        KTx[:, 2 * h + d_, :], start=(d_ == 0), stop=(d_ == 1))
                end(ins)
            for h in range(4):
                pe.wait_ge(S("probs"), 4 + 4 * (h // 2))
                turn(f"PT{h}", [(256 * i + 128 * l, probs_p[:, l, h, 128 * i:128 * i + 128], P, P)
                                for i in range(2) for l in range(2)])
            pe.wait_ge(S("probs"), 12)
            turn("PT4", [(128 * h + 64 * i, probs_s[0:64, h, 128 * i:128 * i + 128], 64, P)
                         for h in range(4) for i in range(2)])
            for h in range(4):
                begin(f"PV{h}")
                has(pe, f"PT{h}")
                for d_ in range(2):
                    for i in range(2):
                        c0 = 256 * h + 128 * d_
                        ins = pe.matmul(bank(f"PV{h}")[:, 256 * d_:256 * d_ + 256], Vp[:, i, c0:c0 + 128], PTp[:, h, i, :],
                                        start=(i == 0), stop=(i == 1))
                end(ins)
            begin("PV4")
            has(pe, "PT4")
            pe.wait_ge(S("vs_in"), 16)
            for d_ in range(KT):
                for i in range(2):
                    ins = pe.matmul(bank("PV4")[:, 64 * d_:64 * d_ + 64], Vs[:, i, 128 * d_:128 * d_ + 128],
                                    PTs[:, d_ // 2, i, :], start=(i == 0), stop=(i == 1))
            end(ins)
            has(pe, "PV4")
            for k in range(KT):
                pe.wait_ge(S("wsqL"), 9 + k // 2)
                begin(f"mo{k}")
                end(square("mo", k, 8 + k // 2, (aoH, aoL), range(KT), 0))
            has(pe, "mo7")
            pe.wait_ge(S("gwr"), 1)
            begin("router")
            for i, (t0, n) in enumerate(TILES):
                for k in range(KT):
                    pe.matmul(ps[0:n, J.bank("router"), E * i:E * i + E], xT[:, k, t0:t0 + n], gwr[:, k, :],
                              start=(k == 0), stop=(k == KT - 1))
            pe.wait_ge(S("sqsum2"), KT - 1)
            for i, (t0, n) in enumerate(TILES):
                ins = pe.matmul(ps[0:n, J.bank("router"), 96 + i:97 + i], sq2[:, 0, t0:t0 + n], ones[:, 0:1],
                                start=True, stop=True)
            end(ins)
            for j in range(6):
                i, n = j // 2, TILES[j // 2][1]
                t0 = TILES[i][0]
                begin(f"x2_{j}")
                for kk in range(4):
                    ins = pe.transpose(ps[0:n, J.bank(f"x2_{j}"), 128 * kk:128 * kk + 128],
                                       xT[:, 4 * (j % 2) + kk, t0:t0 + n], ident[:, :])
                end(ins)
            pe.wait_ge(S("sel"), 7)
            begin("rank")
            for i, (t0, n) in enumerate(TILES):
                for j in range(i + 1):
                    m = TILES[j][1]
                    lhs = below[0:m, 0:n] if j == i else ones[0:m, 0:n]
                    ins = pe.matmul(ps[0:n, J.bank("rank"), E * i:E * i + E], lhs, sel[0:m, j, :], start=(j == 0),
                                    stop=(j == i))
            end(ins)
            moe_tensor(pe)


IN = ["x_prompt", "x_sample", "mem_prompt", "state_gla", "state_pool", "cache_mem_k", "cache_mem_v", "norm_mix",
      "w_in", "w_gate", "b_gate", "gla_gain", "pool_w", "pool_scale", "w_out", "norm_mem_q", "norm_mem_kv", "w_mq",
      "w_mk", "w_mv", "w_mo", "norm_moe", "w_router", "b_router", "w_up", "b_up", "w_down", "b_down", "norm_final"]
OUT = [("y_p", (1, LP, D)), ("y_s", (1, LS, D)), ("gla_p", (1, 1, HEADS, DK, DV)), ("pool_p", (1, 1, BUF, POOL)),
       ("mem_k", (1, 1, NMEM, AH, AHD)), ("mem_v", (1, 1, NMEM, AH, AHD)), ("gla_s", (1, 1, HEADS, DK, DV)),
       ("pool_s", (1, 1, BUF, POOL))]


def kernel(**inputs):
    import numpy as np
    import concourse.bacc as bacc
    from concourse.bass_utils import run_bass_kernel_spmd

    nc = bacc.Bacc("TRN2", target_bir_lowering=False, num_devices=1)
    arrays, a, o = {}, {}, {}
    for name in IN:
        x = np.ascontiguousarray(inputs[name])
        arrays[f"in_{name}"] = x
        a[name] = nc.dram_tensor(f"in_{name}", x.shape, mybir.dt.from_np(x.dtype), kind="ExternalInput").ap()
    for name, shape in OUT:
        o[name] = nc.dram_tensor(f"out_{name}", shape, F32, kind="ExternalOutput").ap()
    build(nc, a, o)
    r = run_bass_kernel_spmd(nc, [arrays], core_ids=[0])
    return tuple(r.results[0][f"out_{name}"] for name, _ in OUT)
```
